# Optimizing a Trainium2 kernel written in Bass

```python
import jax, jax.numpy as jnp
from jax import lax
import numpy as np

D_MODEL = 1024
BATCH = 1
SEQ = 256
DEPTH = 1

GRID_W = 64
MEM_LEN = 256
HG_HEADS = 8
HG_DIM = 128
HG_WIDTH = HG_HEADS * HG_DIM
HG_CHUNK = 64
NA_HEADS = 8
NA_DIM = 64
NA_WIDTH = NA_HEADS * NA_DIM
NA_KH = 8
NA_KW = 16
CA_HEADS = 4
CA_DIM = 128
CA_WIDTH = CA_HEADS * CA_DIM
N_BRANCH = 3
D_FF = 2816
CONV_W = 3
EPS = 1e-6
F_FLOOR = 1e-12
MASK_NEG = -1e30
IN_SIZES = (HG_WIDTH,) * 5 + (NA_WIDTH,) * 3 + (CA_WIDTH,) + (D_MODEL,) * N_BRANCH
IN_COLS = sum(IN_SIZES)


def rmsnorm(x, g):
    xf = x.astype(jnp.float32)
    y = xf * lax.rsqrt(jnp.mean(xf * xf, axis=-1, keepdims=True) + EPS)
    return (y * g.astype(jnp.float32)).astype(x.dtype)

def to_heads(a, n):
    b, t, w = a.shape
    return a.reshape(b, t, n, w // n).transpose(0, 2, 1, 3)

def split_cols(a):
    return jnp.split(a, np.cumsum(IN_SIZES)[:-1].tolist(), axis=-1)

def gla_chunk_scan(q, k, v, log_f):
    b, h, t, dk = q.shape
    dv = v.shape[-1]
    n = t // HG_CHUNK

    def chunks(a):
        return jnp.moveaxis(a.reshape(b, h, n, HG_CHUNK, a.shape[-1]), 2, 0)

    tri = jnp.tril(jnp.ones((HG_CHUNK, HG_CHUNK), dtype=bool))[:, :, None]

    def step(S, inp):
        qc, kc, vc, gc = inp
        cum = jnp.cumsum(gc, axis=2)
        diff = cum[:, :, :, None, :] - cum[:, :, None, :, :]
        decay = jnp.where(tri, jnp.exp(jnp.where(tri, diff, 0.0)), 0.0)
        scores = jnp.einsum('bhtk,bhsk,bhtsk->bhts', qc, kc, decay)
        o = jnp.einsum('bhts,bhsv->bhtv', scores, vc) + jnp.einsum('bhtk,bhkv->bhtv', qc * jnp.exp(cum), S)
        last = cum[:, :, -1:, :]
        S = jnp.exp(last[:, :, 0, :, None]) * S + jnp.einsum('bhsk,bhsv->bhkv', kc * jnp.exp(last - cum), vc)
        return S, o

    S0 = jnp.zeros((b, h, dk, dv), q.dtype)
    _, o = lax.scan(step, S0, (chunks(q), chunks(k), chunks(v), chunks(log_f)))
    return jnp.moveaxis(o, 0, 2).reshape(b, h, t, dv)

def hgrn2_branch(zq, zi, zf_fwd, zf_bwd, zg, lb, gnorm, w_o):
    f32 = jnp.float32
    dt = zq.dtype
    b, t = zq.shape[:2]
    q = to_heads(jax.nn.silu(zq.astype(f32)) * HG_DIM ** -0.5, HG_HEADS)
    v = to_heads(zi.astype(f32), HG_HEADS)

    def one_direction(zf, lb_d, reverse):
        zf = zf.astype(f32)
        f = lb_d + (1.0 - lb_d) * jax.nn.sigmoid(zf)
        log_f = jnp.log(jnp.maximum(f, F_FLOOR))
        k = (1.0 - lb_d) * jax.nn.sigmoid(-zf)
        ins = (q, to_heads(k, HG_HEADS), v, to_heads(log_f, HG_HEADS))
        if reverse:
            ins = tuple(jnp.flip(a, axis=2) for a in ins)
            return jnp.flip(gla_chunk_scan(*ins), axis=2)
        return gla_chunk_scan(*ins)

    o = one_direction(zf_fwd, lb[0], False) + one_direction(zf_bwd, lb[1], True)
    o = rmsnorm(o.transpose(0, 2, 1, 3), gnorm)
    gate = jax.nn.silu(zg.astype(f32)).reshape(o.shape)
    o = (o * gate).reshape(b, t, HG_WIDTH).astype(dt)
    return o @ w_o

def neighbourhood_attention(zq, zk, zv, rpb, w_o):
    b, t, _ = zq.shape
    rows = t // GRID_W
    kh = min(NA_KH, rows)
    r = np.arange(rows)
    row_idx = np.clip(r - kh // 2, 0, rows - kh)[:, None] + np.arange(kh)[None, :]
    c = np.arange(GRID_W)
    col_start = np.clip(c - NA_KW // 2, 0, GRID_W - NA_KW)
    col_mask = (c[None, :] >= col_start[:, None]) & (c[None, :] < col_start[:, None] + NA_KW)
    dr = row_idx - r[:, None] + (NA_KH - 1)
    dc = np.clip(c[None, :] - c[:, None], -(NA_KW - 1), NA_KW - 1) + (NA_KW - 1)
    bias = rpb[:, dr[:, None, :, None], dc[None, :, None, :]]

    def grid(a):
        return a.reshape(b, rows, GRID_W, NA_HEADS, NA_DIM)

    q = grid(zq) * NA_DIM ** -0.5
    k = grid(zk)[:, row_idx]
    v = grid(zv)[:, row_idx]
    s = jnp.einsum('brqhd,brkwhd->bhrqkw', q, k).astype(jnp.float32) + bias.astype(jnp.float32)
    s = jnp.where(col_mask[:, None, :], s, MASK_NEG)
    p = jax.nn.softmax(s.reshape(b, NA_HEADS, rows, GRID_W, kh * GRID_W), axis=-1)
    p = p.reshape(s.shape).astype(zv.dtype)
    o = jnp.einsum('bhrqkw,brkwhd->brqhd', p, v).reshape(b, t, NA_WIDTH)
    return o @ w_o

def memory_cross_attention(zq, mem_n, w_kv, w_o):
    b, t, _ = zq.shape
    m = mem_n.shape[1]
    q = zq.reshape(b, t, CA_HEADS, CA_DIM) * CA_DIM ** -0.5
    kv = (mem_n @ w_kv).reshape(b, m, 2, CA_HEADS, CA_DIM)
    s = jnp.einsum('bthd,bmhd->bhtm', q, kv[:, :, 0]).astype(jnp.float32)
    p = jax.nn.softmax(s, axis=-1).astype(zq.dtype)
    o = jnp.einsum('bhtm,bmhd->bthd', p, kv[:, :, 1]).reshape(b, t, CA_WIDTH)
    return o @ w_o

def conv_ffn(h, w_up, conv_w, conv_b, w_down):
    t = h.shape[1]
    u = h @ w_up
    up = jnp.pad(u, ((0, 0), (CONV_W // 2, CONV_W // 2), (0, 0)))
    u = sum(up[:, j:j + t] * conv_w[j] for j in range(CONV_W)) + conv_b
    a, g = jnp.split(u, 2, axis=-1)
    return (jax.nn.gelu(a) * g) @ w_down

def first_inputs(seed: int = 0) -> dict:
    key = jax.random.key(seed)
    ks = jax.random.split(key, 19)

    def nrm(k, shape, scale):
        return jax.random.normal(k, shape, jnp.float32) * scale

    return {
        'x': nrm(ks[0], (BATCH, SEQ, D_MODEL), 1.0),
        'mem': nrm(ks[1], (BATCH, MEM_LEN, D_MODEL), 1.0),
        'norm_mix': 1.0 + nrm(ks[2], (DEPTH, D_MODEL), 0.02),
        'w_in': nrm(ks[3], (DEPTH, D_MODEL, IN_COLS), D_MODEL ** -0.5),
        'hg_lb_logits': nrm(ks[4], (DEPTH, 2, HG_WIDTH), 1.0),
        'hg_gnorm': 1.0 + nrm(ks[5], (DEPTH, HG_DIM), 0.02),
        'w_hg_o': nrm(ks[6], (DEPTH, HG_WIDTH, D_MODEL), HG_WIDTH ** -0.5),
        'na_rpb': nrm(ks[7], (DEPTH, NA_HEADS, 2 * NA_KH - 1, 2 * NA_KW - 1), 0.1),
        'w_na_o': nrm(ks[8], (DEPTH, NA_WIDTH, D_MODEL), NA_WIDTH ** -0.5),
        'mem_norm': 1.0 + nrm(ks[9], (D_MODEL,), 0.02),
        'w_mem_kv': nrm(ks[10], (DEPTH, D_MODEL, 2 * CA_WIDTH), D_MODEL ** -0.5),
        'w_ca_o': nrm(ks[11], (DEPTH, CA_WIDTH, D_MODEL), CA_WIDTH ** -0.5),
        'w_out': nrm(ks[12], (DEPTH, D_MODEL, D_MODEL), D_MODEL ** -0.5),
        'norm_ffn': 1.0 + nrm(ks[13], (DEPTH, D_MODEL), 0.02),
        'w_up': nrm(ks[14], (DEPTH, D_MODEL, 2 * D_FF), D_MODEL ** -0.5),
        'conv_w': nrm(ks[15], (DEPTH, CONV_W, 2 * D_FF), CONV_W ** -0.5),
        'conv_b': nrm(ks[16], (DEPTH, 2 * D_FF), 0.01),
        'w_down': nrm(ks[17], (DEPTH, D_FF, D_MODEL), D_FF ** -0.5),
        'norm_final': 1.0 + nrm(ks[18], (D_MODEL,), 0.02),
    }

def first_block(x, mem, norm_mix, w_in, hg_lb_logits, hg_gnorm, w_hg_o, na_rpb, w_na_o, mem_norm,
              w_mem_kv, w_ca_o, w_out, norm_ffn, w_up, conv_w, conv_b, w_down, norm_final):
    p_lb = jax.nn.softmax(hg_lb_logits.astype(jnp.float32), axis=0)
    lower_bounds = jnp.clip(jnp.cumsum(p_lb, axis=0) - p_lb[0], 0.0, 1.0)
    mem_n = rmsnorm(mem, mem_norm)
    for l in range(DEPTH):
        h = rmsnorm(x, norm_mix[l])
        (hq, hi, hff, hfb, hg, nq, nk, nv, cq, g_hg, g_na, g_ca) = split_cols(h @ w_in[l])
        y_hg = hgrn2_branch(hq, hi, hff, hfb, hg, lower_bounds[l], hg_gnorm[l], w_hg_o[l])
        y_na = neighbourhood_attention(nq, nk, nv, na_rpb[l], w_na_o[l])
        y_ca = memory_cross_attention(cq, mem_n, w_mem_kv[l], w_ca_o[l])
        merged = jax.nn.sigmoid(g_hg) * y_hg + jax.nn.sigmoid(g_na) * y_na + jax.nn.sigmoid(g_ca) * y_ca
        x = x + merged @ w_out[l]
        x = x + conv_ffn(rmsnorm(x, norm_ffn[l]), w_up[l], conv_w[l], conv_b[l], w_down[l])
    return rmsnorm(x, norm_final)


DEPTH_2 = 2

N_MIXERS = 2
N_RWKV_LAYERS = (DEPTH_2 + 1) // 2
N_GMLP_LAYERS = DEPTH_2 // 2
N_MEM = 256

RWKV_HEAD = 64
RWKV_HEADS = D_MODEL // RWKV_HEAD
LORA_DECAY = 64
LORA_AAA = 64
LORA_GATE = 160
GN_EPS = 64e-5

GMLP_CHUNK = 128
GMLP_WIDTH = 2 * D_MODEL
GMLP_GROUP_DIM = 128
GMLP_GROUPS = GMLP_WIDTH // GMLP_GROUP_DIM

XATTN_HEADS = 4
XATTN_HEAD_DIM = D_MODEL // XATTN_HEADS

RMS_EPS = 1e-6


def rms_norm(x, g):
    x32 = x.astype(jnp.float32)
    y = x32 * lax.rsqrt(jnp.mean(x32 * x32, axis=-1, keepdims=True) + RMS_EPS)
    return (y * g.astype(jnp.float32)).astype(x.dtype)

def swiglu_ffn(h, w_in, w_out):
    gate, up = jnp.split(h @ w_in, 2, axis=-1)
    return (jax.nn.silu(gate) * up) @ w_out

def token_shift(x):
    return jnp.pad(x[:, :-1], ((0, 0), (1, 0), (0, 0)))

def rwkv7_time_mix(h, mu, w_rkv, w0, w1, w2, a0, a1, a2, g1, g2, k_k, k_a, r_k, ln_w, ln_b, w_o):
    B, S, C = h.shape
    H, N = RWKV_HEADS, RWKV_HEAD
    dx = token_shift(h) - h
    xr = h + dx * mu[0]
    xw = h + dx * mu[1]
    xk = h + dx * mu[2]
    xv = h + dx * mu[3]
    xa = h + dx * mu[4]
    xg = h + dx * mu[5]
    x3 = jnp.stack([xr, xk, xv], axis=0)
    rkv = jnp.einsum('nbsc,cnd->nbsd', x3, w_rkv.reshape(C, 3, C))
    r, k, v = rkv[0], rkv[1], rkv[2]
    w = -jax.nn.softplus(-(w0 + jnp.tanh(xw @ w1) @ w2)) - 0.5
    decay = jnp.exp(-jnp.exp(w.astype(jnp.float32)))
    a = jax.nn.sigmoid(a0 + (xa @ a1) @ a2)
    g = jax.nn.sigmoid(xg @ g1) @ g2
    kk = (k * k_k).reshape(B, S, H, N).astype(jnp.float32)
    kk = kk / jnp.maximum(jnp.linalg.norm(kk, axis=-1, keepdims=True), 1e-12)
    k = k * (1.0 + (a - 1.0) * k_a)

    def heads(t):
        return t.reshape(B, S, H, N).astype(jnp.float32)

    r_h, k_h, v_h, a_h = heads(r), heads(k), heads(v), heads(a)
    b_h = kk * a_h
    xs = tuple(jnp.moveaxis(t, 1, 0) for t in (r_h, heads(decay), k_h, v_h, kk, b_h))

    def step(state, inp):
        r_t, w_t, k_t, v_t, kk_t, b_t = inp
        sa = jnp.einsum('bhij,bhj->bhi', state, -kk_t)
        state = (state * w_t[:, :, None, :] + sa[..., None] * b_t[:, :, None, :]
                 + v_t[..., :, None] * k_t[:, :, None, :])
        y = jnp.einsum('bhij,bhj->bhi', state, r_t)
        return state, y

    s0 = jnp.zeros((B, H, N, N), jnp.float32)
    _, ys = lax.scan(step, s0, xs)
    y = jnp.moveaxis(ys, 0, 1)
    mean = jnp.mean(y, axis=-1, keepdims=True)
    var = jnp.mean(jnp.square(y - mean), axis=-1, keepdims=True)
    y = ((y - mean) * lax.rsqrt(var + GN_EPS)).reshape(B, S, C)
    y = y * ln_w.astype(jnp.float32) + ln_b.astype(jnp.float32)
    bonus = jnp.sum(r_h * k_h * r_k.astype(jnp.float32), axis=-1, keepdims=True) * v_h
    y = (y + bonus.reshape(B, S, C)).astype(h.dtype)
    return (y * g) @ w_o

def gmlp_chunk_mix(h, w_uv, v_norm, w_s, b_s, w_o):
    B, S, _ = h.shape
    z = jax.nn.gelu(h @ w_uv)
    u, v = jnp.split(z, 2, axis=-1)
    v = rms_norm(v, v_norm)
    v = v.reshape(B, S // GMLP_CHUNK, GMLP_CHUNK, GMLP_GROUPS, GMLP_GROUP_DIM)
    causal = jnp.tril(jnp.ones((GMLP_CHUNK, GMLP_CHUNK), dtype=bool))
    ws = jnp.where(causal[None], w_s, jnp.zeros_like(w_s))
    sv = jnp.einsum('gts,bcsgd->bctgd', ws, v) + jnp.transpose(b_s)[:, :, None]
    sv = sv.reshape(B, S, GMLP_WIDTH)
    return (u * sv) @ w_o

def memory_cross_attention_2(h, mem_k, mem_v, wq, wo):
    B, S, C = h.shape
    q = (h @ wq).reshape(B, S, XATTN_HEADS, XATTN_HEAD_DIM)
    s = jnp.einsum('bshd,bmhd->bhsm', q, mem_k).astype(jnp.float32) * (XATTN_HEAD_DIM ** -0.5)
    p = jax.nn.softmax(s, axis=-1).astype(h.dtype)
    o = jnp.einsum('bhsm,bmhd->bshd', p, mem_v).reshape(B, S, C)
    return o @ wo

def second_inputs(seed: int = 0) -> dict:
    key = jax.random.key(seed)
    ks = iter(jax.random.split(key, 48))
    C, F = D_MODEL, D_FF
    L, NA, NB = DEPTH_2, N_RWKV_LAYERS, N_GMLP_LAYERS

    def nrm(shape, scale):
        return jax.random.normal(next(ks), shape, jnp.float32) * scale

    def gain(shape):
        return 1.0 + 0.05 * jax.random.normal(next(ks), shape, jnp.float32)

    return {
        "x": jax.random.normal(next(ks), (BATCH, SEQ, C), jnp.float32),
        "mem": jax.random.normal(next(ks), (BATCH, N_MEM, C), jnp.float32),
        "mem_norm": gain((C,)),
        "mem_w_kv": nrm((C, 2 * C), C ** -0.5),
        "ffn1_norm": gain((L, C)),
        "ffn1_w_in": nrm((L, C, 2 * F), C ** -0.5),
        "ffn1_w_out": nrm((L, F, C), F ** -0.5),
        "mix_norm": gain((L, C)),
        "xattn_norm": gain((L, C)),
        "xattn_wq": nrm((L, C, C), C ** -0.5),
        "xattn_wo": nrm((L, C, C), C ** -0.5),
        "ffn2_norm": gain((L, C)),
        "ffn2_w_in": nrm((L, C, 2 * F), C ** -0.5),
        "ffn2_w_out": nrm((L, F, C), F ** -0.5),
        "rwkv_mu": jax.random.uniform(next(ks), (NA, 6, C), jnp.float32),
        "rwkv_w_rkv": nrm((NA, C, 3 * C), C ** -0.5),
        "rwkv_w0": jax.random.uniform(next(ks), (NA, C), jnp.float32, -6.0, -0.5),
        "rwkv_w1": nrm((NA, C, LORA_DECAY), C ** -0.5),
        "rwkv_w2": nrm((NA, LORA_DECAY, C), 0.5 * LORA_DECAY ** -0.5),
        "rwkv_a0": nrm((NA, C), 0.1),
        "rwkv_a1": nrm((NA, C, LORA_AAA), C ** -0.5),
        "rwkv_a2": nrm((NA, LORA_AAA, C), 0.5 * LORA_AAA ** -0.5),
        "rwkv_g1": nrm((NA, C, LORA_GATE), C ** -0.5),
        "rwkv_g2": nrm((NA, LORA_GATE, C), LORA_GATE ** -0.5),
        "rwkv_k_k": gain((NA, C)),
        "rwkv_k_a": gain((NA, C)),
        "rwkv_r_k": nrm((NA, RWKV_HEADS, RWKV_HEAD), 0.1),
        "rwkv_ln_w": gain((NA, C)),
        "rwkv_ln_b": nrm((NA, C), 0.01),
        "rwkv_w_o": nrm((NA, C, C), C ** -0.5),
        "gmlp_w_uv": nrm((NB, C, 2 * GMLP_WIDTH), C ** -0.5),
        "gmlp_v_norm": gain((NB, GMLP_WIDTH)),
        "gmlp_w_s": nrm((NB, GMLP_GROUPS, GMLP_CHUNK, GMLP_CHUNK), 0.5 * GMLP_CHUNK ** -0.5),
        "gmlp_b_s": gain((NB, GMLP_GROUPS, GMLP_CHUNK)),
        "gmlp_w_o": nrm((NB, GMLP_WIDTH, C), GMLP_WIDTH ** -0.5),
        "final_norm": gain((C,)),
    }

def second_block(x, mem, mem_norm, mem_w_kv,
              ffn1_norm, ffn1_w_in, ffn1_w_out, mix_norm, xattn_norm, xattn_wq, xattn_wo,
              ffn2_norm, ffn2_w_in, ffn2_w_out,
              rwkv_mu, rwkv_w_rkv, rwkv_w0, rwkv_w1, rwkv_w2, rwkv_a0, rwkv_a1, rwkv_a2,
              rwkv_g1, rwkv_g2, rwkv_k_k, rwkv_k_a, rwkv_r_k, rwkv_ln_w, rwkv_ln_b, rwkv_w_o,
              gmlp_w_uv, gmlp_v_norm, gmlp_w_s, gmlp_b_s, gmlp_w_o,
              final_norm):
    B = mem.shape[0]
    mem_k, mem_v = jnp.split(rms_norm(mem, mem_norm) @ mem_w_kv, 2, axis=-1)
    mem_k = mem_k.reshape(B, N_MEM, XATTN_HEADS, XATTN_HEAD_DIM)
    mem_v = mem_v.reshape(B, N_MEM, XATTN_HEADS, XATTN_HEAD_DIM)

    for i in range(DEPTH_2):
        x = x + 0.5 * swiglu_ffn(rms_norm(x, ffn1_norm[i]), ffn1_w_in[i], ffn1_w_out[i])
        h = rms_norm(x, mix_norm[i])
        j = i // N_MIXERS
        if i % N_MIXERS == 0:
            y = rwkv7_time_mix(h, rwkv_mu[j], rwkv_w_rkv[j], rwkv_w0[j], rwkv_w1[j], rwkv_w2[j],
                               rwkv_a0[j], rwkv_a1[j], rwkv_a2[j], rwkv_g1[j], rwkv_g2[j],
                               rwkv_k_k[j], rwkv_k_a[j], rwkv_r_k[j], rwkv_ln_w[j], rwkv_ln_b[j],
                               rwkv_w_o[j])
        else:
            y = gmlp_chunk_mix(h, gmlp_w_uv[j], gmlp_v_norm[j], gmlp_w_s[j], gmlp_b_s[j], gmlp_w_o[j])
        x = x + y
        x = x + memory_cross_attention_2(rms_norm(x, xattn_norm[i]), mem_k, mem_v,
                                       xattn_wq[i], xattn_wo[i])
        x = x + 0.5 * swiglu_ffn(rms_norm(x, ffn2_norm[i]), ffn2_w_in[i], ffn2_w_out[i])
    return rms_norm(x, final_norm)


def setup_inputs(seed=0):
    out = dict(first_inputs(seed))
    for name, value in second_inputs(seed + 1).items():
        if name != "x":
            out[name + "_2"] = value
    return out


def reference(
    x, mem, norm_mix, w_in, hg_lb_logits, hg_gnorm, w_hg_o, na_rpb, w_na_o, mem_norm, w_mem_kv,
    w_ca_o, w_out, norm_ffn, w_up, conv_w, conv_b, w_down, norm_final, mem_2, mem_norm_2,
    mem_w_kv_2, ffn1_norm_2, ffn1_w_in_2, ffn1_w_out_2, mix_norm_2, xattn_norm_2, xattn_wq_2,
    xattn_wo_2, ffn2_norm_2, ffn2_w_in_2, ffn2_w_out_2, rwkv_mu_2, rwkv_w_rkv_2, rwkv_w0_2,
    rwkv_w1_2, rwkv_w2_2, rwkv_a0_2, rwkv_a1_2, rwkv_a2_2, rwkv_g1_2, rwkv_g2_2, rwkv_k_k_2,
    rwkv_k_a_2, rwkv_r_k_2, rwkv_ln_w_2, rwkv_ln_b_2, rwkv_w_o_2, gmlp_w_uv_2, gmlp_v_norm_2,
    gmlp_w_s_2, gmlp_b_s_2, gmlp_w_o_2, final_norm_2,
):
    x = first_block(
        x, mem, norm_mix, w_in, hg_lb_logits, hg_gnorm, w_hg_o, na_rpb, w_na_o, mem_norm,
        w_mem_kv, w_ca_o, w_out, norm_ffn, w_up, conv_w, conv_b, w_down, norm_final,
    )
    return second_block(
        x, mem_2, mem_norm_2, mem_w_kv_2, ffn1_norm_2, ffn1_w_in_2, ffn1_w_out_2, mix_norm_2,
        xattn_norm_2, xattn_wq_2, xattn_wo_2, ffn2_norm_2, ffn2_w_in_2, ffn2_w_out_2, rwkv_mu_2,
        rwkv_w_rkv_2, rwkv_w0_2, rwkv_w1_2, rwkv_w2_2, rwkv_a0_2, rwkv_a1_2, rwkv_a2_2,
        rwkv_g1_2, rwkv_g2_2, rwkv_k_k_2, rwkv_k_a_2, rwkv_r_k_2, rwkv_ln_w_2, rwkv_ln_b_2,
        rwkv_w_o_2, gmlp_w_uv_2, gmlp_v_norm_2, gmlp_w_s_2, gmlp_b_s_2, gmlp_w_o_2,
        final_norm_2,
    )


_drawn_inputs = setup_inputs


def setup_inputs(seed=0):
    import zlib

    import numpy as np

    out = dict(_drawn_inputs(seed))
    spreads = {}
    factors = {'norm_mix': 3.487,
     'hg_gnorm': 4.847,
     'na_rpb': 3.557,
     'mem_norm': 8.0,
     'conv_b': 5.129,
     'mem_norm_2': 6.436,
     'xattn_norm_2': 8.0,
     'rwkv_w1_2': 4.467,
     'rwkv_w2_2': 4.595,
     'rwkv_k_k_2': 3.447,
     'rwkv_ln_b_2': 8.0,
     'gmlp_v_norm_2': 6.969,
     'ffn2_norm_2': 3.661,
     'gmlp_b_s_2': 2.883}
    for name, (base, spread) in spreads.items():
        noise = np.random.default_rng([zlib.crc32(name.encode()), seed]).standard_normal(out[name].shape)
        drawn = base * np.exp(spread * noise) if base else spread * noise
        out[name] = __import__('jax').numpy.asarray(drawn.astype(out[name].dtype))
    for name, factor in factors.items():
        out[name] = (out[name] * factor).astype(out[name].dtype)
    return out
```

```python
from contextlib import ExitStack

import numpy as np

import concourse.bass as bass
from concourse import mybir

F32 = mybir.dt.float32
I32 = mybir.dt.int32
ALU = mybir.AluOpType
ACT = mybir.ActivationFunctionType
AX = mybir.AxisListType.X

P = 128
D = 1024
KT = D // P
T = 256
TB = T // P
FF = 2816
FIT = FF // 256
FP = KT * T
HG_H, HG_D = 8, 128
NA_H, NA_D, NA_COLS, NA_WIN = 8, 64, 64, 16
CA_H, CA_D = 4, 128
XA_H, XA_D = 4, 256
RW_H, RW_D, CH = 16, 64, 64
NCH = T // CH
GM_W, GM_G = 2048, 16
EPS = 1e-6
GN_EPS = 64e-5
F_FLOOR = 1e-12
NEG = -1e30
LEVELS = (32, 16, 8, 4, 2, 1)
U_SLOTS = 4
N_PAGES = 16

PARAMS = [
    ("norm_mix", 8), ("norm_ffn", 8), ("norm_final", 8), ("mem_norm", 8), ("hg_lb_logits", 16),
    ("hg_gnorm", 1), ("conv_w", 132), ("conv_b", 44), ("mem_norm_2", 8), ("ffn1_norm_2", 16),
    ("mix_norm_2", 16), ("xattn_norm_2", 16), ("ffn2_norm_2", 16), ("final_norm_2", 8),
    ("rwkv_mu_2", 48), ("rwkv_w0_2", 8), ("rwkv_a0_2", 8), ("rwkv_k_k_2", 8), ("rwkv_k_a_2", 8),
    ("rwkv_r_k_2", 8), ("rwkv_ln_w_2", 8), ("rwkv_ln_b_2", 8),
]
PCOL = {}
_at = 0
for _name, _n in PARAMS:
    PCOL[_name] = _at
    _at += _n
N_PARAM = _at

CONSTS = ["ident", "flip", "ones", "head_ones"] + [f"pair{m}" for m in LEVELS] + [f"upper{m}" for m in LEVELS] + [
    "lower1", "strict", "incl", "causal"]
CCOL = {name: 128 * i for i, name in enumerate(CONSTS)}
C_RESET = 128 * len(CONSTS)
C_WINDOW = C_RESET + T
N_CONST = C_WINDOW + NA_COLS

SEGMENTS = [
    ("mem_k", 2), ("mem_v", 2), ("w_in", 40), ("na_o", 4), ("ca_o", 4), ("hg_o", 4), ("w_out", 4),
    ("ffn0", 22), ("ffn1", 22), ("rw_r", 4), ("rw_k", 4), ("rw_v", 4), ("lora", 4), ("rw_o", 4),
    ("mem2_k", 4), ("mem2_v", 4),
    ("xq0", 4), ("xo0", 4), ("ffn2", 22), ("ffn3", 22), ("gm_u", 8), ("gm_v", 8), ("gm_s", 1), ("gm_o", 8),
    ("xq1", 4), ("xo1", 4), ("ffn4", 22),
]
SEG = {}
_at = 0
for _name, _n in SEGMENTS:
    SEG[_name] = _at
    _at += _n
N_U = _at
N_FFN = 5
N_D = N_FFN * FIT

NORM = {n: i for i, n in enumerate(
    ["mem", "mix0", "ffn0", "fin0", "ffn1", "mix1", "mem2", "x0", "ffn2", "ffn3", "mix2", "x1", "ffn4", "fin2"])}
XUP = {n: i for i, n in enumerate(
    ["w_out", "ffn0", "ffn1", "rw_o", "xo0", "ffn2", "ffn3", "gm_o", "xo1", "ffn4"])}
SEM_NAMES = """
consts_in x_in mem_in mem2_in bias_in rows_in out_done u_done u_evac d_done zero_row norm_sq norm_sum norm_var
norm_std norm_out x_up gate_ready hidden_ready conv_mid gelu_ready dve_chain pool_chain att_scores att_max
att_exp att_prob att_turned att_turned_sb att_out att_out_sb lb_zero lb_exp bias_ready conv_done hg_sig
hg_silu hg_floor hg_log rw_kk rw_zero lora_mm gm_vvar hg_expo hg_exp hg_gh hg_sc hg_kept hg_av hg_o hg_sq
hg_var hg_varsb hg_std hg_out merged lora_mid lora_out rw_mix rw_act rw_kk2 rw_kksum rw_kkvar rw_bonus_in
rw_bonus_sum rw_cum rw_exp rw_dec rw_t rw_t_sb rw_m rw_m_sb rw_lm rw_y rw_y_sb rw_z rw_z_sb rw_rhs rw_rhs_sb
rw_u rw_u_sb rw_ds rw_s rw_yt rw_yt_sb rw_mean rw_cent rw_sq rw_var rw_varsb rw_std rw_out gm_vnorm gm_vstd
gm_vout gm_mask gm_mix gm_mixed
""".split()


class Bag:
    pass


class Link:

    def __init__(self, eng, sem):
        self.eng, self.sem, self.n, self.iv = eng, sem, 0, 0

    def __call__(self, ins):
        self.n += 1
        ins.then_inc(self.sem, 1)
        self.eng.wait_ge(self.sem, self.n + self.iv)

    def loop(self, i, per):
        self.iv, self.start, self.per = i * per, self.n, per

    def end(self, trips):
        assert self.n - self.start == self.per, (self.n - self.start, self.per)
        self.n, self.iv = self.start + trips * self.per, 0


def _in_slot(block):
    return block % U_SLOTS


def build(nc, a):
    ctx = ExitStack()
    with ctx:
        def sb(name, shape):
            return ctx.enter_context(nc.sbuf_tensor(name, shape, F32))

        t = Bag()
        t.x = sb("x", [P, FP])
        t.h = sb("h", [P, FP])
        t.sq = sb("sq", [P, FP])
        t.work = sb("work", [P, FP])
        t.u = [sb(f"u{i}", [P, 2048]) for i in range(U_SLOTS)]
        t.d = [sb(f"d{i}", [P, 2048]) for i in range(2)]
        t.pages = sb("pages", [P, N_PAGES * FP])
        t.page = [t.pages[:, i * FP:(i + 1) * FP] for i in range(N_PAGES)]
        t.const = sb("const", [P, N_CONST])
        t.param = sb("param", [P, N_PARAM])
        t.rstd = sb("rstd", [P, T])
        t.stat = sb("stat", [P, 48])
        t.lb = sb("lb", [P, 48])
        t.pc = sb("pc", [P, KT * NCH])
        t.zrow = ctx.enter_context(nc.sbuf_tensor("zrow", [P, P], mybir.dt.bfloat16))
        t.ps = ctx.enter_context(nc.psum_tensor("ps", [P, 8, 512], F32))
        s = {n: ctx.enter_context(nc.semaphore(n)) for n in SEM_NAMES}
        s["u_in"] = [ctx.enter_context(nc.semaphore(f"u_in{i}")) for i in range(U_SLOTS)]
        s["d_in"] = [ctx.enter_context(nc.semaphore(f"d_in{i}")) for i in range(2)]
        block = ctx.enter_context(nc.Block())

        @block.sync
        def _(sp):
            load_program(sp, a, t, s)

        @block.tensor
        def _(pe):
            tensor_program(pe, t, s)

        @block.scalar
        def _(act):
            scalar_program(act, a, t, s)

        @block.vector
        def _(dve):
            vector_program(dve, t, s)

        @block.gpsimd
        def _(pool):
            pool_program(pool, t, s)


def cst(t, name, rows=P):
    return t.const[0:rows, CCOL[name]:CCOL[name] + 128]


def par(t, name, i=0, n=1):
    c = PCOL[name] + i
    return t.param[:, c:c + n]


def tiles(ap, n=KT):
    return ap.rearrange("p (n t) -> p n t", n=n)


def load_program(sp, a, t, s):
    def load_u(n, slot, first=False):
        if not first:
            sp.wait_ge(s["u_done"], n - (U_SLOTS - 1))
        src = a.u_stream[n] if isinstance(n, int) else a.u_stream[bass.ds(n, 1)].rearrange("a p n -> p (a n)")
        sp.dma_start(t.u[slot][:], src).then_inc(s["u_in"][slot], 16)

    def load_d(m, slot, first=False):
        if not first:
            sp.wait_ge(s["d_done"], m - 1)
        src = a.d_stream[m] if isinstance(m, int) else a.d_stream[bass.ds(m, 1)].rearrange("a p n -> p (a n)")
        sp.dma_start(t.d[slot][:], src).then_inc(s["d_in"][slot], 16)

    def load_run(n0, n1):
        rounds = (n1 - n0) // U_SLOTS
        if rounds >= 2:
            with sp.Fori(0, rounds) as i:
                for k in range(U_SLOTS):
                    load_u(i * U_SLOTS + (n0 + k), (n0 + k) % U_SLOTS)
            n0 += rounds * U_SLOTS
        for n in range(n0, n1):
            load_u(n, n % U_SLOTS)

    def load_ffn(f, seg):
        n, m = SEG[seg], f * FIT + 1
        load_u(n, n % U_SLOTS)
        load_u(n + 1, (n + 1) % U_SLOTS)

        def two_steps(i, first=False):
            for k in range(2):
                load_u(i * 4 + (n + 2 + 2 * k), (n + 2 + 2 * k) % U_SLOTS)
                load_u(i * 4 + (n + 3 + 2 * k), (n + 3 + 2 * k) % U_SLOTS)
                load_d(i * 2 + (m + k), (m + k) % 2, first=first and k == 0)

        if f == 0:
            two_steps(0, first=True)
        with sp.Fori(int(f == 0), (FIT - 1) // 2) as i:
            two_steps(i)
        if f + 1 < N_FFN:
            load_d(m + FIT - 1, (m + FIT - 1) % 2)

    sp.dma_start(t.const[:], a.consts).then_inc(s["consts_in"], 16)
    sp.dma_start(t.param[:], a.params).then_inc(s["consts_in"], 16)
    sp.dma_start(t.page[0], a.mem_t).then_inc(s["mem_in"], 16)
    for n in range(U_SLOTS):
        load_u(n, n, first=True)
    sp.dma_start(t.x[:], a.x_t).then_inc(s["x_in"], 16)
    for row in range(T // NA_COLS):
        part = slice(NA_COLS * (1 - row % 2), NA_COLS * (2 - row % 2))
        dst = t.page[14 + row // 2][part, :].rearrange("p (h r c) -> p h r c", h=NA_H, r=4)
        for h in range(NA_H):
            sp.dma_start(dst[:, h], a.bias_window(h, row)).then_inc(s["bias_in"], 16)
    load_run(U_SLOTS, SEG["ffn0"])
    load_d(0, 0, first=True)
    load_ffn(0, "ffn0")
    load_ffn(1, "ffn1")
    load_run(SEG["rw_r"], SEG["ffn2"])
    load_ffn(2, "ffn2")
    load_ffn(3, "ffn3")
    load_run(SEG["gm_u"], SEG["ffn4"])
    load_ffn(4, "ffn4")


def tensor_program(pe, t, s):
    ps = t.ps

    def block_in(n, slot):
        pe.wait_ge(s["u_in"][slot], (n // U_SLOTS + 1) * 16 if isinstance(n, int) else n[1])
        if isinstance(n, int):
            if n >= U_SLOTS:
                pe.wait_ge(s["u_evac"], n - (U_SLOTS - 1))
        else:
            pe.wait_ge(s["u_evac"], n[0] - (U_SLOTS - 1))

    def at(i, n, per):
        return i * per + n, i * (per // U_SLOTS * 16) + (n // U_SLOTS + 1) * 16

    def up_block(n, slot, act, kts=KT):
        block_in(n, slot)
        for j in range(2):
            for k in range(kts):
                mm = pe.matmul(ps[:, slot, j * T:(j + 1) * T], t.u[slot][:, k * 256 + j * P:k * 256 + (j + 1) * P],
                               act[:, k * T:(k + 1) * T], start=k == 0, stop=k == kts - 1)
        mm.then_inc(s["u_done"], 1)

    def token_block(n, slot, act):
        block_in(n, slot)
        for b in range(TB):
            for k in range(KT):
                mm = pe.matmul(ps[:, slot, b * 256:(b + 1) * 256], act[:, k * T + b * P:k * T + (b + 1) * P],
                               t.u[slot][:, k * 256:(k + 1) * 256], start=k == 0, stop=k == KT - 1)
        mm.then_inc(s["u_done"], 1)

    def project(seg, act, first=0, n=4, groups=1, token=False, kts=KT):
        n0 = SEG[seg] + first
        if groups > 1:
            with pe.Fori(0, groups) as i:
                for k in range(n):
                    up_block(at(i, n0 + k, n), (n0 + k) % U_SLOTS, act)
            return
        for k in range(n):
            if token:
                token_block(n0 + k, (n0 + k) % U_SLOTS, act)
            else:
                up_block(n0 + k, (n0 + k) % U_SLOTS, act, kts)

    def norm_sum(name):
        i = NORM[name]
        for k in range(KT):
            if k % 4 == 0:
                pe.wait_ge(s["norm_sq"], 2 * i + k // 4 + 1)
            mm = pe.matmul(ps[:, 4, 0:T], cst(t, "ones"), t.sq[:, k * T:(k + 1) * T], start=k == 0, stop=k == KT - 1)
        mm.then_inc(s["norm_sum"], 1)

    def norm_done(name):
        pe.wait_ge(s["norm_out"], KT * (NORM[name] + 1))

    def ffn(f, seg, name):
        norm_sum(name)
        norm_done(name)
        n, m = SEG[seg], f * FIT

        def down(step, d_val, slot, hb):
            pe.wait_ge(s["d_in"][slot], d_val)
            if f == 0:
                pe.wait_ge(s["hidden_ready"], step + 1)
            else:
                pe.wait_ge(s["u_evac"], step * 2 + (n + 2))
            for k in range(2):
                for j in range(KT):
                    mm = pe.matmul(ps[:, 4 + j // 2, (j % 2) * T:(j % 2 + 1) * T],
                                   t.d[slot][:, k * D + j * P:k * D + (j + 1) * P],
                                   t.work[:, hb * 512 + k * T:hb * 512 + (k + 1) * T],
                                   start=False, stop=False, skip_group_check=True)
            mm.then_inc(s["d_done"], 1)

        up_block(n, n % U_SLOTS, t.h)
        up_block(n + 1, (n + 1) % U_SLOTS, t.h)
        if f == 0:
            pe.wait_ge(s["zero_row"], 1)
        for bank in range(4, 8):
            pe.matmul(ps[:, bank, :], t.zrow[:, :], t.zrow[:, 0:1].broadcast_to([P, 512]), start=True, stop=True, skip_group_check=True)
        with pe.Fori(0, (FIT - 1) // 2) as i:
            for k in range(2):
                up_block(at(i, n + 2 + 2 * k, 4), (n + 2 + 2 * k) % U_SLOTS, t.h)
                up_block(at(i, n + 3 + 2 * k, 4), (n + 3 + 2 * k) % U_SLOTS, t.h)
                down(i * 2 + k, i * 16 + ((m + k) // 2 + 1) * 16, (m + k) % 2, k)
        last = m + FIT - 1
        down(FIT - 1, (last // 2 + 1) * 16, last % 2, 0)

    def attention(g0, heads, q, k, v, kcs, dcs, dst_rows, bias=None):
        def scores(g):
            h = g - g0
            if g >= 2:
                pe.wait_ge(s["att_exp"], g - 1)
            for qb in range(TB):
                if bias:
                    pe.matmul(ps[:, 4 + g % 2, qb * 256:(qb + 1) * 256], cst(t, "flip"), bias(h, qb),
                              start=True, stop=False, skip_group_check=True)
                for c in range(kcs):
                    mm = pe.matmul(ps[:, 4 + g % 2, qb * 256:(qb + 1) * 256], q(h, c)[:, qb * P:(qb + 1) * P],
                                   k(h, c), start=c == 0 and not bias, stop=c == kcs - 1, skip_group_check=bool(bias))
            mm.then_inc(s["att_scores"], 1)

        def turn(g):
            pe.wait_ge(s["att_prob"], g + 1)
            if g >= 1:
                pe.wait_ge(s["att_turned_sb"], g)
            for qb in range(TB):
                for mb in range(TB):
                    mm = pe.transpose(ps[:, 6, mb * 256 + qb * P:mb * 256 + (qb + 1) * P],
                                      att_buf(t, g)[:, qb * 256 + mb * P:qb * 256 + (mb + 1) * P], cst(t, "ident"))
            mm.then_inc(s["att_turned"], 1)

        def mix(g):
            h = g - g0
            pe.wait_ge(s["att_turned_sb"], g + 1)
            if g >= 1:
                pe.wait_ge(s["att_out_sb"], g)
            for c in range(dcs):
                for mb in range(TB):
                    mm = pe.matmul(ps[dst_rows(h), 7, c * T:(c + 1) * T], v(h, c, mb),
                                   att_turned(t, g)[:, mb * T:(mb + 1) * T], start=mb == 0, stop=mb == TB - 1)
            mm.then_inc(s["att_out"], 1)

        scores(g0)
        for g in range(g0, g0 + heads):
            if g + 1 < g0 + heads:
                scores(g + 1)
            turn(g)
            mix(g)

    pe.wait_ge(s["consts_in"], 32)
    norm_sum("mem")
    norm_done("mem")
    project("mem_k", t.page[1], n=2)
    project("mem_v", t.page[1], n=2, token=True)

    norm_sum("mix0")
    norm_done("mix0")
    project("w_in", t.h)
    project("w_in", t.h, first=4, token=True)
    project("w_in", t.h, first=8, groups=4)
    project("w_in", t.h, first=24, n=2, token=True)
    project("w_in", t.h, first=26, n=2)
    project("w_in", t.h, first=28, groups=3)

    half = FP // 2
    pe.wait_ge(s["u_evac"], SEG["w_in"] + 28)
    pe.wait_ge(s["bias_ready"], 2)
    pr = lambda h: slice(NA_D * (h % 2), NA_D * (h % 2 + 1))
    attention(0, NA_H,
              lambda h, c: t.page[5][pr(h), h // 2 * T:(h // 2 + 1) * T],
              lambda h, c: t.page[5][pr(h), half + h // 2 * T:half + (h // 2 + 1) * T],
              lambda h, c, mb: t.page[6][:, mb * 512 + h * NA_D:mb * 512 + (h + 1) * NA_D],
              1, 1, pr, lambda h, qb: t.page[14 + qb][:, h * 256:(h + 1) * 256])
    whole = lambda h: slice(0, P)
    attention(NA_H, CA_H,
              lambda h, c: t.page[6][:, half + h * T:half + (h + 1) * T],
              lambda h, c: t.page[10][:, h * T:(h + 1) * T],
              lambda h, c, mb: t.page[10][:, half + mb * 512 + h * CA_D:half + mb * 512 + (h + 1) * CA_D],
              1, 1, whole)
    pe.wait_ge(s["att_out_sb"], NA_H + CA_H)
    project("na_o", t.h[:, 0:half], kts=4)
    project("ca_o", t.h[:, half:FP], kts=4)

    for i, (level, hh) in enumerate(HG_STEPS):
        pe.wait_ge(s["hg_gh"], i + 1)
        if i >= 2:
            pe.wait_ge(s["hg_kept"], i - 1)
        keys, queries = hg_buf(t, i)
        if level == "same":
            queries = t.page[0][:, hh * 1024:(hh + 1) * 1024]
        for j in range(8):
            h, b = j // 2, j % 2
            qb = 1 - b if level == 128 else b
            mm = pe.matmul(ps[:, 4 + 2 * (i % 2) + j // 4, (j % 4) * P:(j % 4 + 1) * P],
                           keys[:, h * T + b * P:h * T + (b + 1) * P], queries[:, h * T + qb * P:h * T + (qb + 1) * P],
                           start=True, stop=True)
        mm.then_inc(s["hg_sc"], 1)
    pe.wait_ge(s["hg_kept"], len(HG_STEPS))
    for h in range(HG_H):
        for qb in range(TB):
            for b in range(TB):
                kept = (t.page[14] if b == qb else t.page[15])[:, (h * 2 + b) * P:(h * 2 + b + 1) * P]
                mm = pe.matmul(ps[:, 4 + h // 2, (h % 2) * T + qb * P:(h % 2) * T + (qb + 1) * P],
                               t.page[1][:, b * D + h * HG_D:b * D + (h + 1) * HG_D], kept, start=b == 0, stop=b == 1)
        if h % 2:
            mm.then_inc(s["hg_av"], 1)
    for q in range(4):
        pe.wait_ge(s["hg_sq"], q + 1)
        pe.matmul(ps[:, q, :], cst(t, "ones"), t.page[6][:, q * 512:(q + 1) * 512],
                  start=True, stop=True).then_inc(s["hg_var"], 1)
    pe.wait_ge(s["hg_out"], 4)
    project("hg_o", t.page[5])
    pe.wait_ge(s["merged"], 1)
    project("w_out", t.page[10])

    ffn(0, "ffn0", "ffn0")
    norm_sum("fin0")
    ffn(1, "ffn1", "ffn1")

    norm_sum("mix1")
    for i, seg in enumerate(("rw_r", "rw_k", "rw_v")):
        pe.wait_ge(s["rw_mix"], i + 1)
        project(seg, t.page[1 + i])
    n = SEG["lora"]
    for i in range(2):
        pe.wait_ge(s["u_in"][(n + i) % 4], ((n + i) // 4 + 1) * 16)
    la, lb_ = t.u[n % 4], t.u[(n + 1) % 4]
    pe.wait_ge(s["rw_mix"], 6)
    for bank, act, w, width, step in ((4, t.page[4], la, 64, 256), (5, t.page[5], la[:, 64:], 64, 256),
                                      (6, t.page[6], la[:, 128:], 128, 256), (7, t.page[6], lb_, 128, 128)):
        for k in range(KT):
            mm = pe.matmul(ps[0:width, bank, 0:T], w[:, k * step:k * step + width], act[:, k * T:(k + 1) * T],
                           start=k == 0, stop=k == KT - 1)
    mm.then_inc(s["u_done"], 2)
    for i in range(2, 4):
        pe.wait_ge(s["u_in"][(n + i) % 4], ((n + i) // 4 + 1) * 16)
    pe.wait_ge(s["lora_mid"], 1)
    wa, g2 = t.u[(n + 2) % 4], t.u[(n + 3) % 4]
    for which in range(3):
        if which:
            pe.wait_ge(s["lora_out"], which)
        for j in range(KT):
            out = ps[:, 4 + j // 2, (j % 2) * T:(j % 2 + 1) * T]
            if which < 2:
                mm = pe.matmul(out, wa[0:64, which * D + j * P:which * D + (j + 1) * P],
                               t.work[0:64, which * T:(which + 1) * T], start=True, stop=True)
            else:
                for c in range(2):
                    mm = pe.matmul(out, g2[:, c * D + j * P:c * D + (j + 1) * P],
                                   t.work[:, (2 + c) * T:(3 + c) * T], start=c == 0, stop=c == 1)
        if which < 2:
            mm.then_inc(s["lora_mm"], 1)
    mm.then_inc(s["u_done"], 2)

    for q in range(4):
        pe.wait_ge(s["rw_kk2"], q + 1)
        if q == 0:
            pe.wait_ge(s["u_evac"], n)
        pe.matmul(ps[:, q, :], cst(t, "head_ones"), t.sq[:, q * 512:(q + 1) * 512],
                  start=True, stop=True).then_inc(s["rw_kksum"], 1)
    for q in range(4):
        if q == 0:
            pe.wait_ge(s["rw_bonus_in"], 1)
        pe.matmul(ps[:, q, :], cst(t, "head_ones"), t.work[:, q * 512:(q + 1) * 512],
                  start=True, stop=True).then_inc(s["rw_bonus_sum"], 1)

    for q in range(12):
        src = (t.page[9], t.page[5], t.page[6])[q // 4]
        b, c0 = q % 4 // 2, q % 2 * 4
        if q == 0:
            pe.wait_ge(s["lora_out"], 3)
            pe.wait_ge(s["rw_dec"], 1)
        if q >= 4:
            pe.wait_ge(s["rw_t_sb"], q - 3)
        for c in range(4):
            mm = pe.transpose(ps[:, 4 + q % 4, c * P:(c + 1) * P],
                              src[:, (c0 + c) * T + b * P:(c0 + c) * T + (b + 1) * P], cst(t, "ident"))
        mm.then_inc(s["rw_t"], 1)

    A, B, K, R = t.page[3], t.page[5], t.page[6], t.page[7]

    def chunk_matrices(c):
        for p, pair in enumerate((((B, A), (A, B)), ((K, A), (B, R)), ((K, R),))):
            q = 3 * c + p
            if q == 0:
                pe.wait_ge(s["rw_act"], 1)
            if q >= 2:
                pe.wait_ge(s["rw_m_sb"], q - 1)
            for e in range(2):
                hp = slice(RW_D * e, RW_D * (e + 1))
                for j, (left, right) in enumerate(pair):
                    for b in range(TB):
                        tok = slice(c * T + b * P, c * T + (b + 1) * P)
                        mm = pe.matmul(ps[:, 2 * (q % 2) + e, (2 * j + b) * P:(2 * j + b + 1) * P],
                                       left[hp, tok], right[hp, tok], start=True, stop=True)
            mm.then_inc(s["rw_m"], 1)

    def invert_y(c, lv):
        q, buf = inv_at(c, lv), inv_buf(t, c)
        if lv == 0:
            pe.wait_ge(s["rw_m_sb"], 3 * c + 3)
        else:
            pe.wait_ge(s["rw_z_sb"], q - 1)
        pe.wait_ge(s["rw_lm"], q + 1)
        if q == 0:
            pe.wait_ge(s["rw_t_sb"], 12)
        for j in range(4):
            mm = pe.matmul(ps[:, 4 + 2 * (c % 2), j * P:(j + 1) * P], buf.lm[:, j * P:(j + 1) * P],
                           buf.x[:, j * P:(j + 1) * P], start=True, stop=True)
        mm.then_inc(s["rw_y"], 1)

    def invert_z(c, lv):
        q, buf, xt = inv_at(c, lv), inv_buf(t, c), inv_xt(t, c)
        pe.wait_ge(s["rw_y_sb"], q + 1)
        if lv < len(LEVELS) - 2:
            for j in range(4):
                pe.matmul(ps[:, 4 + 2 * (c % 2), j * P:(j + 1) * P], xt[:, j * P:(j + 1) * P],
                          buf.y[:, j * P:(j + 1) * P], start=True, stop=True)
        for j in range(4):
            mm = pe.matmul(ps[:, 5 + 2 * (c % 2), j * P:(j + 1) * P], buf.y[:, j * P:(j + 1) * P],
                           xt[:, j * P:(j + 1) * P], start=True, stop=True)
        mm.then_inc(s["rw_z"], 1)

    for c in range(0, KT, 2):
        chunk_matrices(c)
        chunk_matrices(c + 1)
        for lv in range(len(LEVELS) - 1):
            invert_y(c, lv)
            invert_y(c + 1, lv)
            invert_z(c, lv)
            invert_z(c + 1, lv)

    rhs, usb, st = t.page[5][:, 0:1024], t.page[5][:, 1024:], t.page[6][:, 0:1024]
    vt, bt, kt_ = t.page[1], t.page[2], t.page[4]

    def mat(base, c, e, b):
        page = base[c // 4]
        at_ = ((c % 4) * 4 + e * 2 + b) * P
        return page[:, at_:at_ + P]

    pe.wait_ge(s["rw_z_sb"], 8 * (len(LEVELS) - 1))
    pe.wait_ge(s["rw_m_sb"], 24)
    pe.wait_ge(s["rw_zero"], 1)
    for n_ in range(NCH):
        b, po = n_ // 2, slice(CH * (n_ % 2), CH * (n_ % 2 + 1))
        if n_ > 0:
            pe.wait_ge(s["rw_s"], n_)
        for c in range(KT):
            out = ps[po, c // 4, (c % 4) * P:(c % 4 + 1) * P]
            tok = slice(c * T + n_ * CH, c * T + (n_ + 1) * CH)
            pe.matmul(out, A[:, tok], st[:, c * P:(c + 1) * P], start=True, stop=False, skip_group_check=True)
            for e in range(2):
                mm = pe.matmul(out[:, e * CH:(e + 1) * CH], mat(RW_MT(t), c, e, b)[:, po],
                               vt[:, b * D + c * P + e * RW_D:b * D + c * P + (e + 1) * RW_D],
                               start=False, stop=e == 1, skip_group_check=True)
        mm.then_inc(s["rw_rhs"], 1)
        for c in range(KT):
            pe.matmul(ps[:, 4 + c // 2, (c % 2) * T + n_ * CH:(c % 2) * T + (n_ + 1) * CH],
                      st[:, c * P:(c + 1) * P], R[:, c * T + n_ * CH:c * T + (n_ + 1) * CH],
                      start=n_ == 0 and c % 2 == 0, stop=False, skip_group_check=True)
        pe.wait_ge(s["rw_rhs_sb"], 2 * (n_ + 1))
        for c in range(KT):
            for e in range(2):
                cols = slice(c * P + e * RW_D, c * P + (e + 1) * RW_D)
                mm = pe.matmul(ps[po, 2 + c // 4, (c % 4) * P + e * CH:(c % 4) * P + (e + 1) * CH],
                               mat(RW_TT(t), c, e, b)[:, po], rhs[:, cols], start=True, stop=True,
                               skip_group_check=True)
        mm.then_inc(s["rw_u"], 1)
        pe.wait_ge(s["rw_u_sb"], 2 * (n_ + 1))
        if n_ < NCH - 1:
            for c in range(KT):
                out = ps[:, c // 4, (c % 4) * P:(c % 4 + 1) * P]
                cols = slice(c * P, (c + 1) * P)
                full = slice(b * D + c * P, b * D + (c + 1) * P)
                pe.matmul(out, bt[po, full], usb[po, cols], start=True, stop=False, skip_group_check=True)
                mm = pe.matmul(out, kt_[po, full], vt[po, full], start=False, stop=True, skip_group_check=True)
            mm.then_inc(s["rw_ds"], 1)
        if n_ % 2:
            for c in range(KT):
                for e in range(2):
                    out = ps[e * RW_D:(e + 1) * RW_D, 4 + c // 2, (c % 2) * T + b * P:(c % 2) * T + (b + 1) * P]
                    cols = slice(c * P + e * RW_D, c * P + (e + 1) * RW_D)
                    pe.matmul(out, vt[:, b * D + cols.start:b * D + cols.stop], mat(RW_RKT(t), c, e, b),
                              start=False, stop=False, skip_group_check=True)
                    mm = pe.matmul(out, usb[:, cols], mat(RW_RBT(t), c, e, b), start=False,
                                   stop=False, skip_group_check=True)
    mm.then_inc(s["rw_yt"], 1)
    for q in range(4):
        pe.wait_ge(s["rw_yt_sb"], q + 1)
        pe.matmul(ps[:, q, :], cst(t, "head_ones"), t.page[8][:, q * 512:(q + 1) * 512],
                  start=True, stop=True).then_inc(s["rw_mean"], 1)
    for q in range(4):
        pe.wait_ge(s["rw_sq"], q + 1)
        pe.matmul(ps[:, q, :], cst(t, "head_ones"), t.sq[:, q * 512:(q + 1) * 512],
                  start=True, stop=True).then_inc(s["rw_var"], 1)
    pe.wait_ge(s["rw_out"], 1)
    project("rw_o", t.page[7])

    norm_sum("mem2")
    norm_done("mem2")
    project("mem2_k", t.page[3])
    project("mem2_v", t.page[3], token=True)

    def memory_attention(i, name):
        norm_sum(name)
        norm_done(name)
        project(f"xq{i}", t.h)
        pe.wait_ge(s["u_evac"], SEG[f"xq{i}"] + 4)
        attention(NA_H + CA_H + XA_H * i, XA_H,
                  lambda h, c: t.page[0][:, (2 * h + c) * T:(2 * h + c + 1) * T],
                  lambda h, c: t.page[14][:, (2 * h + c) * T:(2 * h + c + 1) * T],
                  lambda h, c, mb: t.page[15][:, mb * D + h * XA_D + c * P:mb * D + h * XA_D + (c + 1) * P],
                  2, 2, whole)
        pe.wait_ge(s["att_out_sb"], NA_H + CA_H + XA_H * (i + 1))
        project(f"xo{i}", t.page[1])

    memory_attention(0, "x0")
    ffn(2, "ffn2", "ffn2")
    ffn(3, "ffn3", "ffn3")

    norm_sum("mix2")
    norm_done("mix2")
    project("gm_u", t.h, groups=2)
    for k in range(8):
        token_block(SEG["gm_v"] + k, (SEG["gm_v"] + k) % U_SLOTS, t.h)
    pe.wait_ge(s["gm_mask"], 1)
    for q in range(8):
        if q < 2:
            pe.wait_ge(s["gm_vout"], 1)
        else:
            pe.wait_ge(s["gm_mixed"], q - 1)
        for j in range(4):
            g, b = 2 * q + j // 2, j % 2
            mm = pe.matmul(ps[:, 4 + q % 2, j * P:(j + 1) * P],
                           t.page[2 + b][:, g * P:(g + 1) * P], t.page[4][:, g * P:(g + 1) * P],
                           start=True, stop=True)
        mm.then_inc(s["gm_mix"], 1)
        if q == 0:
            pe.wait_ge(s["gm_mix"], 1)
            pe.sem_inc(s["u_done"], 1)
    pe.wait_ge(s["gm_mixed"], 8)
    for pr_ in range(4):
        n = SEG["gm_o"] + 2 * pr_
        s0, s1 = n % U_SLOTS, (n + 1) % U_SLOTS
        pe.wait_ge(s["u_in"][s0], (n // 4 + 1) * 16)
        pe.wait_ge(s["u_in"][s1], ((n + 1) // 4 + 1) * 16)
        pe.wait_ge(s["u_evac"], n - 3)
        for j in range(2):
            for k in range(2 * KT):
                w = t.u[s0 if k < KT else s1]
                act = t.page[7 + k // KT]
                mm = pe.matmul(ps[:, s0, j * T:(j + 1) * T], w[:, (k % KT) * 256 + j * P:(k % KT) * 256 + (j + 1) * P],
                               act[:, (k % KT) * T:(k % KT + 1) * T], start=k == 0, stop=k == 2 * KT - 1)
        mm.then_inc(s["u_done"], 2)
    memory_attention(1, "x1")
    ffn(4, "ffn4", "ffn4")
    norm_sum("fin2")


HG_STEPS = [(level, hh) for level in (64, *LEVELS, 128, "same") for hh in range(2)]


def hg_buf(t, i):
    buf = t.page[13] if i % 2 == 0 else t.sq[:, :]
    return buf[:, 1024:2048], buf[:, 0:1024]


def att_buf(t, g):
    return t.page[13][:, (g % 2) * 512:(g % 2 + 1) * 512]


def att_turned(t, g):
    return t.page[13][:, 1024 + (g % 2) * 512:1024 + (g % 2 + 1) * 512]


def inv_at(c, lv):
    return c // 2 * 2 * (len(LEVELS) - 1) + 2 * lv + c % 2


def inv_buf(t, c):
    buf = t.sq[:, :] if c % 2 == 0 else t.work[:, :]
    parts = Bag()
    parts.lt, parts.lm, parts.x, parts.y = (buf[:, i:i + 512] for i in range(0, 2048, 512))
    return parts


def stack(pages, c):
    return pages[c // 4][:, (c % 4) * 512:(c % 4 + 1) * 512]


def RW_MT(t):
    return t.page[8], t.page[9]


def RW_RBT(t):
    return t.page[10], t.page[11]


def RW_RKT(t):
    return t.page[12], t.page[14]


def RW_TT(t):
    return t.page[15], t.h[:, :]


def inv_xt(t, c):
    return stack(RW_TT(t), c)


def norm_table(t, s):
    x, h, seg = t.x[:, :], t.h[:, :], SEG
    up = lambda n, f: (s["x_up"], 4 * f + 2, 2)
    rows = {
        "mem": (t.page[0], (s["mem_in"], 16, 0), ("mem_norm", 0), t.page[1]),
        "mix0": (x, (s["x_in"], 16, 0), ("norm_mix", 0), h),
        "ffn0": (x, (s["u_evac"], seg["w_out"] + 2, 2), ("norm_ffn", 0), h),
        "fin0": (x, (s["x_up"], 2, 2), ("norm_final", 0), x),
        "ffn1": (x, (s["norm_out"], KT * NORM["fin0"] + 4, 4), ("ffn1_norm_2", 0), h),
        "mix1": (x, (s["x_up"], 4 + 2, 2), ("mix_norm_2", 0), h),
        "mem2": (t.page[3], (s["mem2_in"], 16, 0), ("mem_norm_2", 0), t.page[3]),
        "x0": (x, (s["u_evac"], seg["rw_o"] + 2, 2), ("xattn_norm_2", 0), h),
        "ffn2": (x, (s["u_evac"], seg["xo0"] + 2, 2), ("ffn2_norm_2", 0), h),
        "ffn3": (x, (s["x_up"], 8 + 2, 2), ("ffn1_norm_2", 8), h),
        "mix2": (x, (s["x_up"], 12 + 2, 2), ("mix_norm_2", 8), h),
        "x1": (x, (s["u_evac"], seg["gm_o"] + 4, 4), ("xattn_norm_2", 8), h),
        "ffn4": (x, (s["u_evac"], seg["xo1"] + 2, 2), ("ffn2_norm_2", 8), h),
        "fin2": (x, (s["x_up"], 16 + 2, 2), ("final_norm_2", 0), h),
    }
    return rows


def scalar_program(act, a, t, s):
    ps = t.ps
    norms = norm_table(t, s)
    f = act.activation

    def norm(name):
        i = NORM[name]
        src, (sem, first, step), _, _ = norms[name]
        if i:
            act.wait_ge(s["norm_sum"], i)
        for hf in range(2):
            act.wait_ge(sem, first + step * hf)
            f(t.sq[:, hf * 1024:(hf + 1) * 1024], src[:, hf * 1024:(hf + 1) * 1024], ACT.Square).then_inc(s["norm_sq"], 1)
        act.wait_ge(s["norm_var"], i + 1)
        f(t.rstd[:], t.rstd[:], ACT.Sqrt).then_inc(s["norm_std"], 1)

    def take(n, slot, dst, func=ACT.Copy):
        act.wait_ge(s["u_done"], n + 1)
        src = ps[:, slot, :]
        if len(dst.shape) == 3:
            src = src.rearrange("p (b c) -> p b c", b=dst.shape[1])
        f(dst, src, func).then_inc(s["u_evac"], 1)

    def take_run(seg, page, first=0, n=4, func=ACT.Copy):
        for k in range(n):
            b = SEG[seg] + first + k
            take(b, b % U_SLOTS, page[:, k * 512:(k + 1) * 512], func)

    def take_groups(seg, page0, first, groups, func=ACT.Copy):
        n0 = SEG[seg] + first
        with act.Fori(0, groups) as i:
            for k in range(4):
                take(i * 4 + (n0 + k), (n0 + k) % U_SLOTS,
                     t.pages[:, bass.ds(i * FP + (page0 * FP + k * 512), 512)], func)

    def take_tokens(seg, region, width, first=0, n=4, func=ACT.Copy):
        for k in range(n):
            b = SEG[seg] + first + k
            dst = region.rearrange("p (b c) -> p b c", b=TB)[:, :, k * 256:(k + 1) * 256]
            take(b, b % U_SLOTS, dst, func)

    def attention(g0, heads, scale, cols, dst):
        def exp(g):
            buf, st = att_buf(t, g), (g % 2) * 8
            act.wait_ge(s["att_max"], g + 1)
            if g >= 2:
                act.wait_ge(s["att_turned"], g - 1)
            for qb in range(TB):
                src = ps[:, 4 + g % 2, qb * 256:(qb + 1) * 256]
                ins = f(buf[:, qb * 256:(qb + 1) * 256], src, ACT.Exp, bias=t.stat[:, st + 2 + qb:st + 3 + qb],
                        scale=scale, accum_out=t.stat[:, st + 4 + qb:st + 5 + qb])
            ins.then_inc(s["att_exp"], 1)

        exp(g0)
        for g in range(g0, g0 + heads):
            if g + 1 < g0 + heads:
                exp(g + 1)
            act.wait_ge(s["att_turned"], g + 1)
            if g >= 2:
                act.wait_ge(s["att_out"], g - 1)
            f(att_turned(t, g), ps[:, 6, :], ACT.Copy).then_inc(s["att_turned_sb"], 1)
            act.wait_ge(s["att_out"], g + 1)
            out = dst(g - g0)
            rows = slice(out[0], out[1])
            f(out[2], ps[rows, 7, 0:cols], ACT.Copy).then_inc(s["att_out_sb"], 1)

    act.wait_ge(s["consts_in"], 32)
    norm("mem")
    act.wait_ge(s["lb_zero"], 1)
    f(t.lb[:, 16:32], t.lb[:, 0:16], ACT.Exp).then_inc(s["lb_exp"], 1)
    norm("mix0")
    take_run("mem_k", t.page[10], n=2)
    take_tokens("mem_v", t.page[10][:, 1024:2048], 512, n=2)
    take_run("w_in", t.page[0])
    take_tokens("w_in", t.page[1], D, first=4)
    take_groups("w_in", 2, 8, 4)
    take_tokens("w_in", t.page[6][:, 0:1024], 512, first=24, n=2)
    take_run("w_in", t.page[6][:, 1024:2048], first=26, n=2)

    act.wait_ge(s["u_evac"], SEG["w_in"] + 20)
    for src, dst in ((2, 11), (3, 12)):
        f(t.page[dst], t.page[src], ACT.Sigmoid).then_inc(s["hg_sig"], 1)
        f(t.page[src], t.page[src], ACT.Sigmoid, scale=-1.0).then_inc(s["hg_sig"], 1)
    take_groups("w_in", 7, 28, 3, ACT.Sigmoid)
    f(t.page[0], t.page[0], ACT.Silu).then_inc(s["hg_silu"], 1)
    f(t.page[4], t.page[4], ACT.Silu).then_inc(s["hg_silu"], 1)
    for i in range(2):
        act.wait_ge(s["hg_floor"], i + 1)
        f(t.page[11 + i], t.page[11 + i], ACT.Ln).then_inc(s["hg_log"], 1)

    def na_dst(h):
        lo = NA_D * (h % 2)
        return lo, lo + NA_D, t.h[lo:lo + NA_D, h // 2 * T:(h // 2 + 1) * T]

    attention(0, NA_H, NA_D ** -0.5, T, na_dst)
    attention(NA_H, CA_H, CA_D ** -0.5, T, lambda h: (0, P, t.h[:, 1024 + h * T:1024 + (h + 1) * T]))

    for i, (level, hh) in enumerate(HG_STEPS):
        if level == "same":
            continue
        act.wait_ge(s["hg_expo"], i + 1)
        buf = t.page[13] if i % 2 == 0 else t.sq[:, :]
        f(buf, buf, ACT.Exp).then_inc(s["hg_exp"], 1)
    for q in range(4):
        c = slice(q * 512, (q + 1) * 512)
        act.wait_ge(s["hg_av"], q + 1)
        f(t.page[5][:, c], ps[:, 4 + q, :], ACT.Copy, scale=HG_D ** -0.5).then_inc(s["hg_o"], 1)
        act.wait_ge(s["hg_o"], q + 1)
        f(t.page[6][:, c], t.page[5][:, c], ACT.Square).then_inc(s["hg_sq"], 1)
    for q in range(4):
        act.wait_ge(s["hg_varsb"], q + 1)
        f(t.page[2][:, q * 512:(q + 1) * 512], t.page[2][:, q * 512:(q + 1) * 512], ACT.Sqrt).then_inc(s["hg_std"], 1)

    norm("ffn0")
    n0 = SEG["ffn0"]
    cw, cb = PCOL["conv_w"] + 44, PCOL["conv_b"]

    def conv_mid(i, tile, k, first=False):
        slot = (n0 + 2 * k) % U_SLOTS
        act.wait_ge(s["u_done"], i * 2 + (n0 + 2))
        if not first:
            act.wait_ge(s["hidden_ready"], i - 1)
        for j in range(4):
            col = tile + (j % 2 + FF // P * (j // 2))
            sel = (lambda base: t.param[:, base + col:base + col + 1]) if isinstance(col, int) else (
                lambda base: t.param[:, bass.ds(col + base, 1)])
            ins = f(t.page[k][:, j * T:(j + 1) * T], ps[:, (slot + j // 2) % 4, (j % 2) * T:(j % 2 + 1) * T],
                    ACT.Identity, scale=sel(cw), bias=sel(cb))
        ins.then_inc(s["conv_mid"], 1)

    def conv_gelu(val, k):
        act.wait_ge(s["conv_done"], val)
        f(t.page[k][:, 0:512], t.page[k][:, 0:512], ACT.Gelu_apprx_tanh).then_inc(s["gelu_ready"], 1)

    conv_mid(0, 0, 0, first=True)

    def conv_steps(i, first=False):
        for k in range(2):
            conv_mid(i * 2 + (1 + k), i * 4 + (2 + 2 * k), (1 + k) % 2, first and k == 0)
            conv_gelu(i * 2 + (1 + k), k)

    conv_steps(0, first=True)
    with act.Fori(1, (FIT - 1) // 2) as i:
        conv_steps(i)
    conv_gelu(FIT, 0)
    norm("fin0")

    def swiglu(seg):
        n0 = SEG[seg]

        def gate(n, slot, k):
            act.wait_ge(s["u_done"], n + 1)
            act.wait_ge(s["u_evac"], n - 2)
            f(t.work[:, 1024 + k * 512:1536 + k * 512], ps[:, slot, :], ACT.Silu).then_inc(s["gate_ready"], 1)

        gate(n0, n0 % U_SLOTS, 0)
        with act.Fori(0, (FIT - 1) // 2) as i:
            for k in range(2):
                gate(i * 4 + (n0 + 2 + 2 * k), (n0 + 2 + 2 * k) % U_SLOTS, (1 + k) % 2)

    norm("ffn1")
    swiglu("ffn1")

    norm("mix1")
    take_run("rw_r", t.page[7])
    take_run("rw_k", t.page[8])
    take_run("rw_v", t.page[9])
    n = SEG["lora"]
    act.wait_ge(s["u_done"], n + 2)
    f(t.work[0:64, 0:T], ps[0:64, 4, 0:T], ACT.Tanh)
    f(t.work[0:64, T:2 * T], ps[0:64, 5, 0:T], ACT.Copy)
    for j in range(2):
        ins = f(t.work[:, (2 + j) * T:(3 + j) * T], ps[:, 6 + j, 0:T], ACT.Sigmoid)
    ins.then_inc(s["lora_mid"], 1)
    for which, name in ((0, "rwkv_w0_2"), (1, "rwkv_a0_2")):
        act.wait_ge(s["lora_mm"], which + 1)
        for j in range(KT):
            ins = f(t.page[11 + which][:, j * T:(j + 1) * T], ps[:, 4 + j // 2, (j % 2) * T:(j % 2 + 1) * T],
                    ACT.Sigmoid, bias=par(t, name, j))
        ins.then_inc(s["lora_out"], 1)
    act.wait_ge(s["u_done"], n + 4)
    f(t.page[13][:, 0:1024].rearrange("p (a b) -> p a b", a=2), ps[:, 4:6, :], ACT.Copy).then_inc(s["u_evac"], 4)
    f(t.page[13][:, 1024:].rearrange("p (a b) -> p a b", a=2), ps[:, 6:8, :], ACT.Copy).then_inc(s["lora_out"], 1)
    for q in range(4):
        c = slice(q * 512, (q + 1) * 512)
        act.wait_ge(s["rw_kk"], q + 1)
        f(t.sq[:, c], t.page[1][:, c], ACT.Square).then_inc(s["rw_kk2"], 1)
    for q in range(4):
        c = slice(q * 512, (q + 1) * 512)
        act.wait_ge(s["rw_kksum"], q + 1)
        f(t.page[2][:, c], ps[:, q, :], ACT.Sqrt).then_inc(s["rw_kkvar"], 1)
    RATE = float(np.exp(-0.5))
    act.wait_ge(s["rw_cum"], 1)
    f(t.page[3], t.page[3], ACT.Exp, scale=-RATE).then_inc(s["rw_exp"], 1)
    f(t.page[4], t.page[2], ACT.Exp, scale=RATE).then_inc(s["rw_exp"], 1)
    f(t.page[10], t.page[2], ACT.Exp, scale=-RATE).then_inc(s["rw_exp"], 1)
    for q in range(12):
        dst = (t.page[1], t.page[2], t.page[4])[q // 4]
        b, half = q % 4 // 2, q % 2
        act.wait_ge(s["rw_t"], q + 1)
        f(dst[:, b * D + half * 512:b * D + (half + 1) * 512], ps[:, 4 + q % 4, :], ACT.Copy).then_inc(s["rw_t_sb"], 1)
    for c0 in range(0, KT, 2):
        for lv in range(len(LEVELS) - 1):
            for c in (c0, c0 + 1):
                act.wait_ge(s["rw_y"], inv_at(c, lv) + 1)
                f(inv_buf(t, c).y, ps[:, 4 + 2 * (c % 2), :], ACT.Copy).then_inc(s["rw_y_sb"], 1)
    for n_ in range(NCH):
        po = slice(CH * (n_ % 2), CH * (n_ % 2 + 1))
        act.wait_ge(s["rw_rhs"], n_ + 1)
        f(t.page[5][po, 512:1024], ps[po, 1, :], ACT.Copy, scale=-1.0).then_inc(s["rw_rhs_sb"], 1)
        act.wait_ge(s["rw_u"], n_ + 1)
        f(t.page[5][po, 1536:2048], ps[po, 3, :], ACT.Copy).then_inc(s["rw_u_sb"], 1)
    act.wait_ge(s["rw_yt"], 1)
    act.dma_start(t.page[3], a.mem2_t).then_inc(s["mem2_in"], 16)
    act.dma_start(t.page[5], a.bias_rows).then_inc(s["rows_in"], 16)
    act.dma_start(t.page[6], a.gain_rows).then_inc(s["rows_in"], 16)
    for q in range(4):
        f(t.page[8][:, q * 512:(q + 1) * 512], ps[:, 4 + q, :], ACT.Copy).then_inc(s["rw_yt_sb"], 1)
    for q in range(4):
        c = slice(q * 512, (q + 1) * 512)
        act.wait_ge(s["rw_cent"], q + 1)
        f(t.sq[:, c], t.page[8][:, c], ACT.Square).then_inc(s["rw_sq"], 1)
    for q in range(4):
        c = slice(q * 512, (q + 1) * 512)
        act.wait_ge(s["rw_varsb"], q + 1)
        f(t.page[2][:, c], t.page[2][:, c], ACT.Sqrt).then_inc(s["rw_std"], 1)

    norm("mem2")
    take_run("mem2_k", t.page[14])
    take_tokens("mem2_v", t.page[15], D)

    def memory_attention(i):
        norm(f"x{i}")
        take_run(f"xq{i}", t.page[0])
        attention(NA_H + CA_H + XA_H * i, XA_H, XA_D ** -0.5, 2 * T,
                  lambda h: (0, P, t.page[1][:, h * 512:(h + 1) * 512]))

    memory_attention(0)
    norm("ffn2")
    swiglu("ffn2")
    norm("ffn3")
    swiglu("ffn3")

    norm("mix2")
    take_groups("gm_u", 0, 0, 2, ACT.Gelu_apprx_tanh)
    take_tokens("gm_v", t.pages[:, 2 * FP:4 * FP], GM_W, n=8, func=ACT.Gelu_apprx_tanh)
    act.wait_ge(s["u_evac"], SEG["gm_v"] + 8)
    for b in range(TB):
        ins = f((t.sq, t.work)[b][:, :], t.page[2 + b], ACT.Square, accum_out=t.stat[:, 16 + b:17 + b])
    ins.then_inc(s["gm_vnorm"], 1)
    act.wait_ge(s["gm_vvar"], 1)
    f(t.stat[:, 18:20], t.stat[:, 18:20], ACT.Sqrt).then_inc(s["gm_vstd"], 1)
    memory_attention(1)
    norm("ffn4")
    swiglu("ffn4")
    norm("fin2")
    act.wait_ge(s["norm_out"], KT * len(NORM))
    act.dma_start(a.out, t.h[:, :]).then_inc(s["out_done"], 16)
    act.wait_ge(s["out_done"], 16)


def vector_program(dve, t, s):
    ps = t.ps
    norms = norm_table(t, s)
    link = Link(dve, s["dve_chain"])
    ts, tt, stt = dve.tensor_scalar, dve.tensor_tensor, dve.scalar_tensor_tensor

    def norm(name):
        i = NORM[name]
        src, _, gain, dst = norms[name]
        dve.wait_ge(s["norm_sum"], i + 1)
        link(ts(t.rstd[:], ps[:, 4, 0:T], 1.0 / D, EPS, ALU.mult, ALU.add))
        dve.reciprocal(t.rstd[:], t.rstd[:]).then_inc(s["norm_var"], 1)
        dve.wait_ge(s["norm_std"], i + 1)
        for k in range(KT):
            c = slice(k * T, (k + 1) * T)
            stt(dst[:, c], src[:, c], par(t, gain[0], gain[1] + k), t.rstd[:],
                ALU.mult, ALU.mult).then_inc(s["norm_out"], 1)

    def residual(seg):
        for k in range(4):
            n = SEG[seg] + k
            dve.wait_ge(s["u_done"], n + 1)
            c = slice(k * 512, (k + 1) * 512)
            tt(t.x[:, c], ps[:, n % U_SLOTS, :], t.x[:, c], ALU.add).then_inc(s["u_evac"], 1)

    def ffn_residual(f_, scale):
        dve.wait_ge(s["d_done"], (f_ + 1) * FIT)
        for q in range(4):
            c = slice(q * 512, (q + 1) * 512)
            stt(t.x[:, c], ps[:, 4 + q, :], scale, t.x[:, c], ALU.mult, ALU.add).then_inc(s["x_up"], 1)

    def attention(g0, heads, scale):
        def pre(g):
            st = (g % 2) * 8
            src = ps[:, 4 + g % 2, :].rearrange("p (b m) -> p b m", b=TB)
            dve.wait_ge(s["att_scores"], g + 1)
            link(dve.tensor_reduce(t.stat[:, st:st + 2], src, AX, ALU.max))
            ts(t.stat[:, st + 2:st + 4], t.stat[:, st:st + 2], -scale, None,
               ALU.mult).then_inc(s["att_max"], 1)

        pre(g0)
        for g in range(g0, g0 + heads):
            if g + 1 < g0 + heads:
                pre(g + 1)
            st, buf = (g % 2) * 8, att_buf(t, g)
            dve.wait_ge(s["att_exp"], g + 1)
            link(dve.reciprocal(t.stat[:, st + 6:st + 8], t.stat[:, st + 4:st + 6]))
            for qb in range(TB):
                c = slice(qb * 256, (qb + 1) * 256)
                ins = ts(buf[:, c], buf[:, c], t.stat[:, st + 6 + qb:st + 7 + qb], None, ALU.mult)
            ins.then_inc(s["att_prob"], 1)

    dve.wait_ge(s["consts_in"], 32)
    logits = par(t, "hg_lb_logits", 0, 16)
    tt(t.lb[:, 0:16], logits, logits, ALU.subtract).then_inc(s["lb_zero"], 1)
    norm("mem")
    dve.wait_ge(s["lb_exp"], 1)
    link(dve.reciprocal(t.lb[:, 32:48], t.lb[:, 16:32]))
    link(tt(t.lb[:, 16:32], t.lb[:, 16:32], t.lb[:, 32:48], ALU.mult))
    link(tt(t.lb[:, 0:16], t.lb[:, 16:32], t.lb[:, 16:32], ALU.subtract))
    link(ts(t.lb[:, 0:16], t.lb[:, 0:16], 0.0, 1.0, ALU.max, ALU.min))
    link(ts(t.lb[:, 16:32], t.lb[:, 0:16], -1.0, 1.0, ALU.mult, ALU.add))
    norm("mix0")

    for d in range(2):
        dve.wait_ge(s["hg_sig"], 2 * d + 1)
        fp = t.page[11 + d]
        for h in range(HG_H):
            c = slice(h * T, (h + 1) * T)
            ins = ts(fp[:, c], fp[:, c], t.lb[:, 16 + 8 * d + h:17 + 8 * d + h], t.lb[:, 8 * d + h:8 * d + h + 1],
                     ALU.mult, ALU.add)
        link(ins)
        ts(fp, fp, F_FLOOR, None, ALU.max).then_inc(s["hg_floor"], 1)
        dve.wait_ge(s["hg_sig"], 2 * d + 2)
        kp = t.page[2 + d]
        for h in range(HG_H):
            c = slice(h * T, (h + 1) * T)
            ins = ts(kp[:, c], kp[:, c], t.lb[:, 16 + 8 * d + h:17 + 8 * d + h], None, ALU.mult)
        link(ins)
    reset = t.const[:, C_RESET:C_RESET + T]
    for d in range(2):
        dve.wait_ge(s["hg_log"], d + 1)
        for h in range(HG_H):
            c = t.page[11 + d][:, h * T:(h + 1) * T]
            if d:
                c = c[:, ::-1]
            ins = dve.tensor_tensor_scan(c, reset, c, 0.0, ALU.mult, ALU.add)
        link(ins)

    attention(0, NA_H, NA_D ** -0.5)
    attention(NA_H, CA_H, CA_D ** -0.5)
    for seg, gate in (("na_o", 8), ("ca_o", 9)):
        for k in range(4):
            n = SEG[seg] + k
            c = slice(k * 512, (k + 1) * 512)
            dve.wait_ge(s["u_done"], n + 1)
            if seg == "na_o":
                tt(t.page[10][:, c], ps[:, n % U_SLOTS, :], t.page[gate][:, c], ALU.mult).then_inc(s["u_evac"], 1)
                dve.wait_ge(s["u_evac"], n + 1)
            else:
                tt(t.work[:, c], ps[:, n % U_SLOTS, :], t.page[gate][:, c], ALU.mult).then_inc(s["u_evac"], 1)
                dve.wait_ge(s["u_evac"], n + 1)
                link(tt(t.page[10][:, c], t.page[10][:, c], t.work[:, c], ALU.add))

    def expo(i):
        level, hh = HG_STEPS[i]
        if level == "same":
            return
        half = slice(hh * 1024, (hh + 1) * 1024)
        eg, eh = hg_buf(t, i)
        cf, cb = t.page[11][:, half], t.page[12][:, half]
        if i >= 2:
            dve.wait_ge(s["hg_sc"], i - 1)
        if level == 128:
            v = lambda ap: ap.rearrange("p (h c m) -> p h c m", h=4, c=NCH)
            cf, cb, eg, eh = v(cf), v(cb), v(eg), v(eh)
            tf = lambda c: cf[:, :, c, CH - 1:CH].broadcast_to([P, 4, CH])
            tb = lambda c: cb[:, :, c, 0:1].broadcast_to([P, 4, CH])
            tt(eg[:, :, 0], tf(0), cf[:, :, 0], ALU.subtract)
            tt(eg[:, :, 1], tf(1), cf[:, :, 1], ALU.subtract)
            tt(eg[:, :, 2], tb(2), cb[:, :, 2], ALU.subtract)
            link(tt(eg[:, :, 3], tb(3), cb[:, :, 3], ALU.subtract))
            tt(eg[:, :, 0], eg[:, :, 0], tf(1), ALU.add)
            tt(eg[:, :, 3], eg[:, :, 3], tb(2), ALU.add)
            tt(eh[:, :, 0], cb[:, :, 0], tb(1), ALU.add)
            dve.tensor_copy(eh[:, :, 1], cb[:, :, 1])
            dve.tensor_copy(eh[:, :, 2], cf[:, :, 2])
            tt(eh[:, :, 3], cf[:, :, 3], tf(2), ALU.add).then_inc(s["hg_expo"], 1)
            return
        v = lambda ap: ap.rearrange("p (g two m) -> p g two m", two=2, m=level)
        n = 1024 // (2 * level)
        cf, cb, eg, eh = v(cf), v(cb), v(eg), v(eh)
        lastf = cf[:, :, 0, level - 1:level].broadcast_to([P, n, level])
        firstb = cb[:, :, 1, 0:1].broadcast_to([P, n, level])
        tt(eg[:, :, 0], lastf, cf[:, :, 0], ALU.subtract)
        tt(eg[:, :, 1], firstb, cb[:, :, 1], ALU.subtract)
        if level == CH:
            dve.tensor_copy(eh[:, :, 0], cb[:, :, 0])
            dve.tensor_copy(eh[:, :, 1], cf[:, :, 1]).then_inc(s["hg_expo"], 1)
        else:
            tt(eh[:, :, 0], cb[:, :, 0], firstb, ALU.subtract)
            tt(eh[:, :, 1], cf[:, :, 1], lastf, ALU.subtract).then_inc(s["hg_expo"], 1)

    def decayed(i):
        level, hh = HG_STEPS[i]
        half = slice(hh * 1024, (hh + 1) * 1024)
        eg, eh = hg_buf(t, i)
        if level == "same":
            dve.wait_ge(s["hg_sc"], i - 1)
            tt(eg, t.page[2][:, half], t.page[3][:, half], ALU.add).then_inc(s["hg_gh"], 1)
            return
        dve.wait_ge(s["hg_exp"], i + 1)
        v = lambda ap: ap.rearrange("p (g two m) -> p g two m", two=2, m=level)
        tt(eh, eh, t.page[0][:, half], ALU.mult)
        eg = v(eg)
        tt(eg[:, :, 0], eg[:, :, 0], v(t.page[2][:, half])[:, :, 0], ALU.mult)
        tt(eg[:, :, 1], eg[:, :, 1], v(t.page[3][:, half])[:, :, 1], ALU.mult).then_inc(s["hg_gh"], 1)

    def keep(i):
        level, hh = HG_STEPS[i]
        half = slice(hh * 1024, (hh + 1) * 1024)
        bank = 4 + 2 * (i % 2)
        dve.wait_ge(s["hg_sc"], i + 1)
        if level in (64, 128):
            dst = t.page[14 if level == 64 else 15][:, half]
            dve.tensor_copy(dst.rearrange("p (a c) -> p a c", a=2), ps[:, bank:bank + 2, :]).then_inc(s["hg_kept"], 1)
        else:
            mask = cst(t, "ident" if level == "same" else f"pair{level}").bitcast(I32)
            dve.copy_predicated(t.page[14][:, half].rearrange("p (n c) -> p n c", n=8),
                                mask.unsqueeze(1).broadcast_to([P, 8, P]),
                                ps[:, bank:bank + 2, :].rearrange("p a (n c) -> p (a n) c", c=P)).then_inc(s["hg_kept"], 1)

    dve.wait_ge(s["hg_silu"], 2)
    expo(0)
    for i in range(len(HG_STEPS)):
        if i + 1 < len(HG_STEPS):
            expo(i + 1)
        decayed(i)
        if i:
            keep(i - 1)
            dve.wait_ge(s["hg_kept"], i)
    keep(len(HG_STEPS) - 1)
    for q in range(4):
        c = slice(q * 512, (q + 1) * 512)
        dve.wait_ge(s["hg_var"], q + 1)
        link(ts(t.page[2][:, c], ps[:, q, :], 1.0 / HG_D, EPS, ALU.mult, ALU.add))
        dve.reciprocal(t.page[2][:, c], t.page[2][:, c]).then_inc(s["hg_varsb"], 1)
    for q in range(4):
        c = slice(q * 512, (q + 1) * 512)
        dve.wait_ge(s["hg_std"], q + 1)
        link(tt(t.page[5][:, c], t.page[5][:, c], t.page[2][:, c], ALU.mult))
        stt(t.page[5][:, c], t.page[5][:, c], par(t, "hg_gnorm"), t.page[4][:, c],
            ALU.mult, ALU.mult).then_inc(s["hg_out"], 1)
    for k in range(4):
        n = SEG["hg_o"] + k
        c = slice(k * 512, (k + 1) * 512)
        dve.wait_ge(s["u_done"], n + 1)
        tt(t.work[:, c], ps[:, n % U_SLOTS, :], t.page[7][:, c], ALU.mult).then_inc(s["u_evac"], 1)
        dve.wait_ge(s["u_evac"], n + 1)
        ins = tt(t.page[10][:, c], t.page[10][:, c], t.work[:, c], ALU.add)
    ins.then_inc(s["merged"], 1)
    residual("w_out")

    norm("ffn0")
    n0 = SEG["ffn0"]

    def outer_taps(val, tile, k):
        slot = (n0 + 2 * k) % U_SLOTS
        dve.wait_ge(s["conv_mid"], val)
        for tap in (0, 2):
            for j in range(4):
                col = tile + (j % 2 + FF // P * (j // 2)) + (PCOL["conv_w"] + 44 * tap)
                w = t.param[:, col:col + 1] if isinstance(col, int) else t.param[:, bass.ds(col, 1)]
                u = ps[:, (slot + j // 2) % 4, (j % 2) * T:(j % 2 + 1) * T]
                c = t.page[k][:, j * T:(j + 1) * T]
                o, i_ = (c[:, 1:T], u[:, 0:T - 1]) if tap == 0 else (c[:, 0:T - 1], u[:, 1:T])
                ins = stt(o, i_, w, o, ALU.mult, ALU.add)
            if tap == 0:
                link(ins)
        link(ins)
        dve.sem_inc(s["conv_done"], 1)
        dve.sem_inc(s["u_evac"], 2)

    def conv_hidden(val, dval, k, first=False):
        dve.wait_ge(s["gelu_ready"], val)
        if not first:
            dve.wait_ge(s["d_done"], dval)
        tt(t.work[:, k * 512:(k + 1) * 512], t.page[k][:, 0:512], t.page[k][:, 512:1024],
           ALU.mult).then_inc(s["hidden_ready"], 1)

    outer_taps(1, 0, 0)

    def conv_steps(i, first=False):
        for k in range(2):
            outer_taps(i * 2 + (2 + k), i * 4 + (2 + 2 * k), (1 + k) % 2)
            conv_hidden(i * 2 + (1 + k), i * 2 + (k - 1), k, first)

    conv_steps(0, first=True)
    with dve.Fori(0, (FIT - 1) // 2 - 1) as i:
        link.loop(i, 4)
        conv_steps(i + 1)
    link.end((FIT - 1) // 2 - 1)
    conv_hidden(FIT, FIT - 2, 0)
    ffn_residual(0, 1.0)
    norm("fin0")

    def swiglu(f_, seg):
        n0, m = SEG[seg], f_ * FIT

        def hidden(n, slot, gval, dval, k):
            dve.wait_ge(s["gate_ready"], gval)
            dve.wait_ge(s["u_done"], n + 2)
            dve.wait_ge(s["d_done"], dval)
            tt(t.work[:, k * 512:(k + 1) * 512], ps[:, slot, :], t.work[:, 1024 + k * 512:1536 + k * 512],
               ALU.mult).then_inc(s["u_evac"], 2)

        g = (f_ - 1) * FIT
        hidden(n0, (n0 + 1) % U_SLOTS, g + 1, m - 1, 0)
        with dve.Fori(0, (FIT - 1) // 2) as i:
            for k in range(2):
                hidden(i * 4 + (n0 + 2 + 2 * k), (n0 + 3 + 2 * k) % U_SLOTS, i * 2 + (g + 2 + k),
                       i * 2 + (m + k), (1 + k) % 2)
        ffn_residual(f_, 0.5)

    norm("ffn1")
    swiglu(1, "ffn1")

    norm("mix1")
    dve.wait_ge(s["norm_out"], KT * (NORM["mix1"] + 1))
    h3, d3 = tiles(t.h[:, :]), tiles(t.page[0])
    tt(d3[:, :, 1:T], h3[:, :, 0:T - 1], h3[:, :, 1:T], ALU.subtract)
    link(ts(d3[:, :, 0:1], h3[:, :, 0:1], -1.0, None, ALU.mult))
    for i, mu in enumerate((0, 2, 3, 1, 4, 5)):
        for k in range(KT):
            c = slice(k * T, (k + 1) * T)
            ins = stt(t.page[1 + i][:, c], t.page[0][:, c], par(t, "rwkv_mu_2", 8 * mu + k), t.h[:, c],
                      ALU.mult, ALU.add)
        ins.then_inc(s["rw_mix"], 1)
    n = SEG["rw_v"]
    dve.wait_ge(s["u_evac"], n)
    for k in range(KT):
        c = slice(k * T, (k + 1) * T)
        ins = ts(t.page[1][:, c], t.page[8][:, c], par(t, "rwkv_k_k_2", k), None, ALU.mult)
        if k % 2:
            ins.then_inc(s["rw_kk"], 1)
    dve.wait_ge(s["lora_out"], 2)
    for k in range(KT):
        c = slice(k * T, (k + 1) * T)
        link(ts(t.page[4][:, c], t.page[12][:, c], 1.0, par(t, "rwkv_k_a_2", k), ALU.subtract, ALU.mult))
        link(stt(t.page[8][:, c], t.page[4][:, c], 1.0, t.page[8][:, c], ALU.add, ALU.mult))
    for q in range(4):
        c = slice(q * 512, (q + 1) * 512)
        dve.wait_ge(s["rw_kkvar"], q + 1)
        link(ts(t.page[2][:, c], t.page[2][:, c], 1e-12, None, ALU.max))
        link(dve.reciprocal(t.page[2][:, c], t.page[2][:, c]))
        link(tt(t.page[1][:, c], t.page[1][:, c], t.page[2][:, c], ALU.mult))
    dve.wait_ge(s["lora_out"], 3)
    for k in range(KT):
        c = slice(k * T, (k + 1) * T)
        ins = stt(t.work[:, c], t.page[7][:, c], par(t, "rwkv_r_k_2", k), t.page[8][:, c], ALU.mult, ALU.mult)
    ins.then_inc(s["rw_bonus_in"], 1)
    for k in range(KT):
        c = slice(k * T, (k + 1) * T)
        ins = dve.tensor_tensor_scan(t.page[2][:, c], reset, t.page[11][:, c], 0.0, ALU.mult, ALU.add)
    link(ins)
    tt(t.page[3], t.page[2], t.page[11], ALU.subtract).then_inc(s["rw_cum"], 1)
    link(tt(t.page[5], t.page[1], t.page[12], ALU.mult))
    for q in range(4):
        c = slice(q * 512, (q + 1) * 512)
        dve.wait_ge(s["rw_bonus_sum"], q + 1)
        ins = tt(t.page[0][:, c], ps[:, q, :], t.page[9][:, c], ALU.mult)
    ins.then_inc(s["rw_act"], 1)
    dve.wait_ge(s["rw_exp"], 1)
    tt(t.page[3], t.page[3], t.page[1], ALU.mult)
    dve.wait_ge(s["rw_exp"], 2)
    tt(t.page[5], t.page[5], t.page[4], ALU.mult)
    tt(t.page[6], t.page[8], t.page[4], ALU.mult)
    dve.wait_ge(s["rw_exp"], 3)
    dve.tensor_copy(t.pc[:, :].rearrange("p (a b) -> p a b", b=1),
                    t.page[10].rearrange("p (a b) -> p a b", b=CH)[:, :, CH - 1:CH])
    tt(t.page[7], t.page[7], t.page[10], ALU.mult).then_inc(s["rw_dec"], 1)

    def matrices(q, j):
        bank = 2 * (q % 2)
        return ps[:, bank:bank + 2, j * 256:(j + 1) * 256].rearrange("p e (b c) -> p e b c", b=2)

    def view(ap):
        return ap.rearrange("p (e b c) -> p e b c", e=2, b=2)

    def mask(name):
        return cst(t, name).unsqueeze(1).unsqueeze(1).broadcast_to([P, 2, 2, P])

    def chunk_matrices(c):
        buf, xt = inv_buf(t, c), inv_xt(t, c)
        q = 3 * c
        dve.wait_ge(s["rw_m"], q + 1)
        link(tt(view(buf.lt), matrices(q, 0), mask("strict"), ALU.mult))
        link(tt(view(buf.x), matrices(q, 1), mask("lower1"), ALU.mult))
        tt(view(buf.x), mask("ident"), view(buf.x), ALU.subtract)
        link(tt(view(xt), view(buf.lt), mask("upper1"), ALU.mult))
        tt(view(xt), mask("ident"), view(xt), ALU.subtract).then_inc(s["rw_m_sb"], 1)
        dve.wait_ge(s["rw_m"], q + 2)
        tt(view(stack(RW_MT(t), c)), matrices(q + 1, 0), mask("strict"), ALU.mult)
        tt(view(stack(RW_RBT(t), c)), matrices(q + 1, 1), mask("incl"), ALU.mult).then_inc(s["rw_m_sb"], 1)
        dve.wait_ge(s["rw_m"], q + 3)
        tt(view(stack(RW_RKT(t), c)), matrices(q + 2, 0), mask("incl"), ALU.mult).then_inc(s["rw_m_sb"], 1)

    dve.wait_ge(s["rw_t_sb"], 12)
    for c0 in range(0, KT, 2):
        chunk_matrices(c0)
        chunk_matrices(c0 + 1)
        for lv in range(len(LEVELS) - 1):
            for c in (c0, c0 + 1):
                buf, xt = inv_buf(t, c), inv_xt(t, c)
                dve.wait_ge(s["rw_z"], inv_at(c, lv) + 1)
                if lv < len(LEVELS) - 2:
                    tt(buf.x, buf.x, ps[:, 4 + 2 * (c % 2), :], ALU.subtract)
                tt(xt, xt, ps[:, 5 + 2 * (c % 2), :], ALU.subtract).then_inc(s["rw_z_sb"], 1)

    dve.memset(t.page[5][:, 0:1024], 0.0)
    dve.memset(t.page[6][:, 0:1024], 0.0).then_inc(s["rw_zero"], 1)
    state, delta = t.page[6][:, 0:1024], t.page[6][:, 1024:2048]
    for n_ in range(NCH):
        po = slice(CH * (n_ % 2), CH * (n_ % 2 + 1))
        dve.wait_ge(s["rw_rhs"], n_ + 1)
        ts(t.page[5][po, 0:512], ps[po, 0, :], -1.0, None, ALU.mult).then_inc(s["rw_rhs_sb"], 1)
        dve.wait_ge(s["rw_u"], n_ + 1)
        dve.tensor_copy(t.page[5][po, 1024:1536], ps[po, 2, :]).then_inc(s["rw_u_sb"], 1)
        if n_ == NCH - 1:
            break
        dve.wait_ge(s["rw_ds"], n_ + 1)
        blocks = lambda ap: ap.rearrange("p (c i) -> p c i", i=P)
        link(tt(blocks(delta), ps[:, 0:2, :].rearrange("p a (c i) -> p (a c) i", i=P),
                cst(t, "head_ones").unsqueeze(1).broadcast_to([P, KT, P]), ALU.mult))
        link(tt(state, state, delta, ALU.add))
        pc = t.pc[:, :].rearrange("p (c n) -> p c n", n=NCH)[:, :, n_:n_ + 1].broadcast_to([P, KT, P])
        tt(blocks(state), blocks(state), pc, ALU.mult).then_inc(s["rw_s"], 1)
    for q in range(4):
        c = slice(q * 512, (q + 1) * 512)
        dve.wait_ge(s["rw_mean"], q + 1)
        stt(t.page[8][:, c], ps[:, q, :], -1.0 / RW_D, t.page[8][:, c], ALU.mult, ALU.add).then_inc(s["rw_cent"], 1)
    for q in range(4):
        c = slice(q * 512, (q + 1) * 512)
        dve.wait_ge(s["rw_var"], q + 1)
        link(ts(t.page[2][:, c], ps[:, q, :], 1.0 / RW_D, GN_EPS, ALU.mult, ALU.add))
        dve.reciprocal(t.page[2][:, c], t.page[2][:, c]).then_inc(s["rw_varsb"], 1)
    for q in range(4):
        c = slice(q * 512, (q + 1) * 512)
        dve.wait_ge(s["rw_std"], q + 1)
        link(tt(t.page[8][:, c], t.page[8][:, c], t.page[2][:, c], ALU.mult))
        for k in (2 * q, 2 * q + 1):
            ck = slice(k * T, (k + 1) * T)
            ins = ts(t.page[8][:, ck], t.page[8][:, ck], par(t, "rwkv_ln_w_2", k), par(t, "rwkv_ln_b_2", k),
                     ALU.mult, ALU.add)
        link(ins)
        link(tt(t.page[8][:, c], t.page[8][:, c], t.page[0][:, c], ALU.add))
        ins = tt(t.page[7][:, c], t.page[8][:, c], t.page[13][:, c], ALU.mult)
    ins.then_inc(s["rw_out"], 1)
    residual("rw_o")

    norm("mem2")

    def memory_attention(i):
        norm(f"x{i}")
        attention(NA_H + CA_H + XA_H * i, XA_H, XA_D ** -0.5)
        residual(f"xo{i}")

    memory_attention(0)
    norm("ffn2")
    swiglu(2, "ffn2")
    norm("ffn3")
    swiglu(3, "ffn3")

    norm("mix2")
    n = SEG["gm_s"]
    dve.wait_ge(s["u_in"][n % U_SLOTS], (n // U_SLOTS + 1) * 16)
    cols = lambda ap: ap.rearrange("p (g c) -> p g c", g=GM_G)
    tt(cols(t.page[4]), cols(t.u[n % U_SLOTS][:, :]), cst(t, "causal").unsqueeze(1).broadcast_to([P, GM_G, P]),
       ALU.mult).then_inc(s["gm_mask"], 1)
    dve.wait_ge(s["gm_vnorm"], 1)
    link(ts(t.stat[:, 18:20], t.stat[:, 16:18], 1.0 / GM_W, EPS, ALU.mult, ALU.add))
    dve.reciprocal(t.stat[:, 18:20], t.stat[:, 18:20]).then_inc(s["gm_vvar"], 1)
    dve.wait_ge(s["rows_in"], 32)
    dve.wait_ge(s["gm_vstd"], 1)
    for b in range(TB):
        ins = stt(t.page[2 + b], t.page[2 + b], t.stat[:, 18 + b:19 + b], t.page[6], ALU.mult, ALU.mult)
    ins.then_inc(s["gm_vout"], 1)
    for q in range(8):
        dve.wait_ge(s["gm_mix"], q + 1)
        tmp = t.work[:, (q % 2) * 512:(q % 2 + 1) * 512]
        bias = t.page[5][:, q * 256:(q + 1) * 256].rearrange("p (g c) -> p g c", g=2)
        ins = tt(tmp.rearrange("p (g b c) -> p g b c", g=2, b=2),
                 ps[:, 4 + q % 2, :].rearrange("p (g b c) -> p g b c", g=2, b=2),
                 bias.unsqueeze(2).broadcast_to([P, 2, 2, P]), ALU.add)
        if q == 0:
            ins.then_inc(s["u_evac"], 1)
            dve.wait_ge(s["u_evac"], n + 1)
        else:
            link(ins)
        tt(t.pages[:, 7 * FP + q * 512:7 * FP + (q + 1) * 512], tmp, t.pages[:, q * 512:(q + 1) * 512],
           ALU.mult).then_inc(s["gm_mixed"], 1)
    for p in range(4):
        n = SEG["gm_o"] + 2 * p
        c = slice(p * 512, (p + 1) * 512)
        dve.wait_ge(s["u_done"], n + 2)
        tt(t.x[:, c], ps[:, n % U_SLOTS, :], t.x[:, c], ALU.add).then_inc(s["u_evac"], 2)
    memory_attention(1)
    norm("ffn4")
    swiglu(4, "ffn4")
    norm("fin2")


def pool_program(pool, t, s):
    pool.memset(t.zrow[:], 0.0).then_inc(s["zero_row"], 1)
    pool.wait_ge(s["consts_in"], 32)
    pool.wait_ge(s["bias_in"], 16 * 4 * NA_H)
    for page in (14, 15):
        table = t.page[page].rearrange("p (n c) -> p n c", c=NA_COLS)
        window = t.const[:, C_WINDOW:C_WINDOW + NA_COLS].unsqueeze(1).broadcast_to([P, 32, NA_COLS])
        pool.tensor_tensor(table, table, window, ALU.add).then_inc(s["pool_chain"], 1)
        pool.wait_ge(s["pool_chain"], page - 13)
        pool.tensor_scalar(t.page[page], t.page[page], NA_D ** 0.5, None, ALU.mult).then_inc(s["bias_ready"], 1)
    for c0 in range(0, KT, 2):
        for lv in range(len(LEVELS) - 1):
            for c in (c0, c0 + 1):
                q, buf = inv_at(c, lv), inv_buf(t, c)
                if lv == 0:
                    pool.wait_ge(s["rw_m_sb"], 3 * c + 1)
                else:
                    pool.wait_ge(s["rw_y"], q - 1)
                m = LEVELS[len(LEVELS) - 2 - lv]
                v = lambda ap: ap.rearrange("p (n c) -> p n c", c=P)
                pool.tensor_tensor(v(buf.lm), v(buf.lt), cst(t, f"upper{m}").unsqueeze(1).broadcast_to([P, 4, P]),
                                   ALU.mult).then_inc(s["rw_lm"], 1)


def constants():
    i = np.arange(P)
    r, c = i[:, None], i[None, :]
    out = np.zeros((P, N_CONST), np.float32)

    def put(name, mask):
        out[:, CCOL[name]:CCOL[name] + P] = mask

    put("ident", r == c)
    put("flip", r + c == P - 1)
    put("ones", np.ones((P, P)))
    put("head_ones", r // RW_D == c // RW_D)
    for m in LEVELS:
        pair = (r // (2 * m) == c // (2 * m)) & (r // m != c // m)
        put(f"pair{m}", pair)
        put(f"upper{m}", pair & (r < c))
    put("lower1", (r // 2 == c // 2) & (r > c))
    put("strict", (r // CH == c // CH) & (r < c))
    put("incl", (r // CH == c // CH) & (r <= c))
    put("causal", r <= c)
    out[:, C_RESET:C_RESET + T] = (np.arange(T) % CH != 0)[None, :]
    q, k = (P - 1 - np.arange(P))[:, None] % NA_COLS, np.arange(NA_COLS)[None, :]
    start = np.clip(q - NA_WIN // 2, 0, NA_COLS - NA_WIN)
    out[:, C_WINDOW:] = np.where((k >= start) & (k < start + NA_WIN), 0.0, NEG)
    return out


def feature_major(x):
    n, d = x.shape
    return np.ascontiguousarray(x.T.reshape(d // P, P, n).transpose(1, 0, 2).reshape(P, -1))


def k_blocks(w, cols=256):
    k, n = w.shape
    b = w.reshape(k // P, P, n // cols, cols).transpose(2, 1, 0, 3).reshape(n // cols, P, -1)
    return [np.pad(x, ((0, 0), (0, 2048 - x.shape[1]))) for x in b]


def up_blocks(w):
    a, b = k_blocks(w[:, :FF]), k_blocks(w[:, FF:])
    return [x for pair in zip(a, b) for x in pair]


def weight_stream(i):
    rkv = i["rwkv_w_rkv_2"][0]
    w1, a1, g1 = i["rwkv_w1_2"][0], i["rwkv_a1_2"][0], i["rwkv_g1_2"][0]
    w2, a2, g2 = i["rwkv_w2_2"][0], i["rwkv_a2_2"][0], i["rwkv_g2_2"][0]
    lora_a = k_blocks(np.concatenate([w1, a1, g1[:, :P]], 1))
    lora_b = k_blocks(np.pad(g1[:, P:], ((0, 0), (0, 2 * P - g1.shape[1]))), P)
    lora_c = [np.pad(np.concatenate([w2, a2], 1), ((0, P - w2.shape[0]), (0, 0)))]
    g2p = np.pad(g2, ((0, 2 * P - g2.shape[0]), (0, 0)))
    lora_d = [np.concatenate([g2p[:P], g2p[P:]], 1)]
    gm_o = k_blocks(i["gmlp_w_o_2"][0][:D]), k_blocks(i["gmlp_w_o_2"][0][D:])
    gm_s = i["gmlp_w_s_2"][0].transpose(2, 0, 1).reshape(P, -1)
    kv, kv2, uv = i["w_mem_kv"][0], i["mem_w_kv_2"], i["gmlp_w_uv_2"][0]
    parts = {
        "mem_k": k_blocks(kv[:, :512]), "mem_v": k_blocks(kv[:, 512:]), "w_in": k_blocks(i["w_in"][0]),
        "na_o": k_blocks(i["w_na_o"][0]), "ca_o": k_blocks(i["w_ca_o"][0]), "hg_o": k_blocks(i["w_hg_o"][0]),
        "w_out": k_blocks(i["w_out"][0]), "ffn0": up_blocks(i["w_up"][0]),
        "ffn1": up_blocks(i["ffn1_w_in_2"][0]), "ffn2": up_blocks(i["ffn2_w_in_2"][0]),
        "ffn3": up_blocks(i["ffn1_w_in_2"][1]), "ffn4": up_blocks(i["ffn2_w_in_2"][1]),
        "rw_r": k_blocks(rkv[:, :D]), "rw_k": k_blocks(rkv[:, D:2 * D]), "rw_v": k_blocks(rkv[:, 2 * D:]),
        "lora": lora_a + lora_b + lora_c + lora_d, "rw_o": k_blocks(i["rwkv_w_o_2"][0]),
        "mem2_k": k_blocks(kv2[:, :D]), "mem2_v": k_blocks(kv2[:, D:]),
        "xq0": k_blocks(i["xattn_wq_2"][0]), "xo0": k_blocks(i["xattn_wo_2"][0]),
        "xq1": k_blocks(i["xattn_wq_2"][1]), "xo1": k_blocks(i["xattn_wo_2"][1]),
        "gm_u": k_blocks(uv[:, :GM_W]), "gm_v": k_blocks(uv[:, GM_W:]), "gm_s": [gm_s],
        "gm_o": [x for pair in zip(*gm_o) for x in pair],
    }
    blocks = []
    for name, n in SEGMENTS:
        assert len(parts[name]) == n, name
        blocks += parts[name]
    return np.stack(blocks)


def down_stream(i):
    ws = [i["w_down"][0], i["ffn1_w_out_2"][0], i["ffn2_w_out_2"][0], i["ffn1_w_out_2"][1], i["ffn2_w_out_2"][1]]
    return np.concatenate([w.reshape(FIT, 2, P, D).transpose(0, 2, 1, 3).reshape(FIT, P, 2 * D) for w in ws])


def param_table(i):
    cols = [i[name].reshape(-1, P).T for name, _ in PARAMS]
    assert [c.shape[1] for c in cols] == [n for _, n in PARAMS]
    return np.concatenate(cols, 1)


def kernel(**inputs):
    import concourse.bacc as bacc
    from concourse.bass_utils import run_bass_kernel_spmd

    i = {k: np.asarray(v) for k, v in inputs.items()}
    arrays = {
        "in_u_stream": weight_stream(i), "in_d_stream": down_stream(i), "in_params": param_table(i),
        "in_consts": constants(), "in_x": feature_major(i["x"][0]), "in_mem": feature_major(i["mem"][0]),
        "in_mem2": feature_major(i["mem_2"][0]), "in_rpb": i["na_rpb"][0], "in_gmlp_b": i["gmlp_b_s_2"][0],
        "in_gmlp_gain": i["gmlp_v_norm_2"],
    }
    arrays = {k: np.ascontiguousarray(v) for k, v in arrays.items()}
    nc = bacc.Bacc("TRN2", target_bir_lowering=False, num_devices=1, dynamic_dma_scratch_size=1024)
    ap = {k: nc.dram_tensor(k, v.shape, F32, kind="ExternalInput").ap() for k, v in arrays.items()}
    out = nc.dram_tensor("out", (P, FP), F32, kind="ExternalOutput").ap()
    rpb = ap["in_rpb"]
    n_dr, n_dc = rpb.shape[1:]
    kh = T // NA_COLS

    def bias_window(h, row):
        at = h * n_dr * n_dc + (n_dr // 2 - row) * n_dc + n_dc // 2 - (NA_COLS - 1)
        return bass.AP(tensor=rpb.tensor, offset=at, ap=[[1, NA_COLS], [n_dc, kh], [1, NA_COLS]])

    a = Bag()
    a.u_stream, a.d_stream, a.params, a.consts = (ap[f"in_{n}"] for n in ("u_stream", "d_stream", "params", "consts"))
    a.x_t, a.mem_t, a.mem2_t, a.bias_window, a.out = ap["in_x"], ap["in_mem"], ap["in_mem2"], bias_window, out
    a.bias_rows = ap["in_gmlp_b"].rearrange("(o g) c -> o (g c)", o=1).broadcast_to([P, GM_W])
    a.gain_rows = ap["in_gmlp_gain"].broadcast_to([P, GM_W])
    build(nc, a)
    got = run_bass_kernel_spmd(nc, [arrays], core_ids=[0]).results[0]["out"]
    return got.reshape(P, KT, T).transpose(2, 1, 0).reshape(1, T, D)
```

```python
from contextlib import ExitStack

import numpy as np

import concourse.bass as bass
from concourse import mybir

F32 = mybir.dt.float32
F32R = mybir.dt.float32r
I32 = mybir.dt.int32
ALU = mybir.AluOpType
ACT = mybir.ActivationFunctionType
AX = mybir.AxisListType.X

P = 128
D = 1024
KT = D // P
T = 256
TB = T // P
FF = 2816
FIT = FF // 256
FP = KT * T
HG_H, HG_D = 8, 128
NA_H, NA_D, NA_COLS, NA_WIN = 8, 64, 64, 16
CA_H, CA_D = 4, 128
XA_H, XA_D = 4, 256
RW_H, RW_D, CH = 16, 64, 64
NCH = T // CH
GM_W, GM_G = 2048, 16
EPS = 1e-6
GN_EPS = 64e-5
F_FLOOR = 1e-12
NEG = -1e30
LEVELS = (32, 16, 8, 4, 2, 1)
BANKS = 4
RAW_SLOTS = 2
PIECE_SLOTS = 4
N_FFN = 5
AHEAD = 2
N_PAGES = 16

PARAMS = [
    ("norm_mix", 8), ("norm_ffn", 8), ("norm_final", 8), ("mem_norm", 8), ("hg_lb_logits", 16),
    ("hg_gnorm", 1), ("conv_w", 132), ("conv_b", 44), ("mem_norm_2", 8), ("ffn1_norm_2", 16),
    ("mix_norm_2", 16), ("xattn_norm_2", 16), ("ffn2_norm_2", 16), ("final_norm_2", 8),
    ("rwkv_mu_2", 48), ("rwkv_w0_2", 8), ("rwkv_a0_2", 8), ("rwkv_k_k_2", 8), ("rwkv_k_a_2", 8),
    ("rwkv_r_k_2", 8), ("rwkv_ln_w_2", 8), ("rwkv_ln_b_2", 8),
]
PCOL = {}
_at = 0
for _name, _n in PARAMS:
    PCOL[_name] = _at
    _at += _n
N_PARAM = _at

CONSTS = ["ident", "flip", "ones", "head_ones"] + [f"pair{m}" for m in LEVELS] + [f"upper{m}" for m in LEVELS] + [
    "lower1", "strict", "incl", "causal"]
CCOL = {name: 128 * i for i, name in enumerate(CONSTS)}
C_RESET = 128 * len(CONSTS)
C_WINDOW = C_RESET + T
N_CONST = C_WINDOW + NA_COLS

SEGMENTS = [
    ("mem_k", 2, 2), ("mem_v", 2, 2), ("w_in", 40, 40), ("na_o", 4, 2), ("ca_o", 4, 2), ("hg_o", 4, 4),
    ("w_out", 4, 4), ("ffn0", 22, 33), ("ffn1", 22, 33), ("rw_r", 4, 4), ("rw_k", 4, 4), ("rw_v", 4, 4),
    ("lora", 0, 3), ("rw_o", 4, 4), ("mem2_k", 4, 4), ("mem2_v", 4, 4), ("xq0", 4, 4), ("xo0", 4, 4),
    ("ffn2", 22, 33), ("ffn3", 22, 33), ("gm_u", 8, 8), ("gm_v", 8, 8), ("gm_o", 4, 8),
    ("xq1", 4, 4), ("xo1", 4, 4), ("ffn4", 22, 33),
]
SEG, BLK = {}, {}
_seg = _blk = 0
for _name, _banks, _blocks in SEGMENTS:
    SEG[_name], BLK[_name] = _seg, _blk
    _seg += _banks
    _blk += _blocks
N_BLK = _blk

OPERAND = {n: i for i, n in enumerate(
    ["mem", "mix0", "hg", "merged", "ffn0", "ffn1", "rw0", "rw1", "rw2", "rw3", "rw4", "rw5", "lora", "rw_o", "mem2",
     "x0", "ffn2", "ffn3", "mix2", "gm0", "gm1", "x1", "ffn4"])}
RW_ORDER = [0, 1, "b0", "b1", 2, "b2", "b3", 3, "b4", "b5", 4, "b6", "b7", 5, "b8", "b9", "b10", "b11"]
NORM = {n: i for i, n in enumerate(
    ["mem", "mix0", "ffn0", "fin0", "ffn1", "mix1", "mem2", "x0", "ffn2", "ffn3", "mix2", "x1", "ffn4", "fin2"])}
XUP = {n: i for i, n in enumerate(
    ["w_out", "ffn0", "ffn1", "rw_o", "xo0", "ffn2", "ffn3", "gm_o", "xo1", "ffn4"])}
SEM_NAMES = """
consts_in x_in mem_in mem2_in bias_in rows_in out_done piece_done high_done low_done op_high op_low u_evac
att_low zero_row inner_zero hidden_made hidden_high att_high norm_sq norm_sum norm_var norm_std norm_out x_up
gate_ready hidden_ready conv_mid gelu_ready dve_chain pool_chain att_scores att_max att_exp att_prob
att_turned att_turned_sb att_out lb_zero lb_exp bias_ready conv_done hg_sig hg_silu hg_floor hg_log rw_kk
rw_zero lora_mm gm_vvar hg_expo hg_exp hg_gh hg_sc hg_kept hg_av hg_o hg_sq hg_var hg_varsb hg_std hg_out
merged lora_mid lora_out rw_mix rw_act rw_kk2 rw_kksum rw_kkvar rw_bonus_in rw_bonus_sum rw_cum rw_exp rw_dec
rw_t rw_t_sb rw_m rw_m_sb rw_lm rw_y rw_y_sb rw_z rw_z_sb rw_rhs rw_rhs_sb rw_u rw_u_sb rw_ds rw_s rw_yt
rw_yt_sb rw_mean rw_cent rw_sq rw_var rw_varsb rw_std rw_out gm_vnorm gm_vstd gm_vout gm_mask gm_mix gm_mixed
""".split()


class Bag:
    pass


class Link:

    def __init__(self, eng, sem):
        self.eng, self.sem, self.n, self.iv = eng, sem, 0, 0

    def __call__(self, ins):
        self.n += 1
        ins.then_inc(self.sem, 1)
        self.eng.wait_ge(self.sem, self.n + self.iv)

    def loop(self, i, per):
        self.iv, self.start, self.per = i * per, self.n, per

    def end(self, trips):
        assert self.n - self.start == self.per, (self.n - self.start, self.per)
        self.n, self.iv = self.start + trips * self.per, 0


def build(nc, a):
    ctx = ExitStack()
    with ctx:
        def sb(name, shape):
            return ctx.enter_context(nc.sbuf_tensor(name, shape, F32))

        t = Bag()
        def both(name, pages=1):
            at = -(-nc.sbuf_base // 32) * 32
            plain = sb(name, [P, pages * FP])
            split = [nc.alloc_sbuf_tensor_at(f"{name}_r{i}", [P, FP], F32R, offset=at + 4 * FP * i)[:, :]
                     for i in range(pages)]
            return plain, split

        t.x = sb("x", [P, FP])
        t.h, (t.h_r,) = both("h")
        t.sq, (t.sq_r,) = both("sq")
        t.work, (t.work_r,) = both("work")
        t.raw = [sb(f"raw{i}", [P, 2048]) for i in range(RAW_SLOTS)]
        t.wh = [ctx.enter_context(nc.sbuf_tensor(f"wh{i}", [P, 1024], F32R)) for i in range(PIECE_SLOTS)]
        t.wl = [ctx.enter_context(nc.sbuf_tensor(f"wl{i}", [P, 1024], F32R)) for i in range(PIECE_SLOTS)]
        t.pages, t.page_r = both("pages", N_PAGES)
        t.page = [t.pages[:, i * FP:(i + 1) * FP] for i in range(N_PAGES)]
        t.const = sb("const", [P, N_CONST])
        t.param = sb("param", [P, N_PARAM])
        t.rstd = sb("rstd", [P, T])
        t.stat = sb("stat", [P, 48])
        t.lb = sb("lb", [P, 48])
        t.pc = sb("pc", [P, KT * NCH])
        t.zrow = ctx.enter_context(nc.sbuf_tensor("zrow", [P, P], mybir.dt.bfloat16))
        t.ps = ctx.enter_context(nc.psum_tensor("ps", [P, 8, 512], F32))
        s = {n: ctx.enter_context(nc.semaphore(n)) for n in SEM_NAMES}
        s["raw_in"] = [ctx.enter_context(nc.semaphore(f"raw_in{i}")) for i in range(RAW_SLOTS)]
        block = ctx.enter_context(nc.Block())

        @block.sync
        def _(sp):
            load_program(sp, a, t, s)

        @block.tensor
        def _(pe):
            tensor_program(pe, t, s)

        @block.scalar
        def _(act):
            scalar_program(act, a, t, s)

        @block.vector
        def _(dve):
            vector_program(dve, t, s)

        @block.gpsimd
        def _(pool):
            pool_program(pool, t, s)


def cst(t, name, rows=P):
    return t.const[0:rows, CCOL[name]:CCOL[name] + 128]


def par(t, name, i=0, n=1):
    c = PCOL[name] + i
    return t.param[:, c:c + n]


def tiles(ap, n=KT):
    return ap.rearrange("p (n t) -> p n t", n=n)


def load_program(sp, a, t, s):
    def load(n, slot, first=False):
        if not first:
            sp.wait_ge(s["low_done"], n * 2 - 2)
        src = a.stream[n] if isinstance(n, int) else a.stream[bass.ds(n, 1)].rearrange("a p n -> p (a n)")
        sp.dma_start(t.raw[slot][:], src).then_inc(s["raw_in"][slot], 16)

    sp.dma_start(t.const[:], a.consts).then_inc(s["consts_in"], 16)
    sp.dma_start(t.param[:], a.params).then_inc(s["consts_in"], 16)
    sp.dma_start(t.page[0], a.mem_t).then_inc(s["mem_in"], 16)
    for n in range(RAW_SLOTS):
        load(n, n, first=True)
    sp.dma_start(t.x[:], a.x_t).then_inc(s["x_in"], 16)
    for row in range(T // NA_COLS):
        part = slice(NA_COLS * (1 - row % 2), NA_COLS * (2 - row % 2))
        dst = t.page[14 + row // 2][part, :].rearrange("p (h r c) -> p h r c", h=NA_H, r=4)
        for h in range(NA_H):
            sp.dma_start(dst[:, h], a.bias_window(h, row)).then_inc(s["bias_in"], 16)
    rounds = N_BLK // RAW_SLOTS
    with sp.Fori(1, rounds) as i:
        for k in range(RAW_SLOTS):
            load(i * RAW_SLOTS + k, k)
    for n in range(rounds * RAW_SLOTS, N_BLK):
        load(n, n % RAW_SLOTS)


def tensor_program(pe, t, s):
    ps = t.ps

    def split_mm(out, w, act, start, stop, weights_move=False):
        for q, (x, y) in enumerate(((0, 0), (0, 1), (1, 0))):
            left, right = (act[y], w[x]) if weights_move else (w[x], act[y])
            mm = pe.matmul(out, left, right, start=start and q == 0, stop=stop and q == 2, skip_group_check=True)
        return mm

    def piece(b, hf):
        pe.wait_ge(s["low_done"], b * 2 + (hf + 1))
        i = (2 * block0(b) + hf) % PIECE_SLOTS
        return t.wh[i], t.wl[i]

    def bank_free(n):
        if not isinstance(n, int) or n >= BANKS:
            pe.wait_ge(s["u_evac"], n - (BANKS - 1))

    def up_block(n, bank, b, act):
        bank_free(n)
        for hf in range(2):
            w = piece(b, hf)
            for j in range(2):
                for kk in range(4):
                    k = 4 * hf + kk
                    cols = slice(kk * 256 + j * P, kk * 256 + (j + 1) * P)
                    mm = split_mm(ps[:, bank, j * T:(j + 1) * T], [x[:, cols] for x in w],
                                  [x[:, k * T:(k + 1) * T] for x in act],
                                  start=hf == 0 and j == 0 and kk == 0, stop=k == KT - 1)
            mm.then_inc(s["piece_done"], 1)

    def token_block(n, bank, b, act):
        bank_free(n)
        for hf in range(2):
            w = piece(b, hf)
            for tb in range(TB):
                for kk in range(4):
                    k = 4 * hf + kk
                    mm = split_mm(ps[:, bank, tb * 256:(tb + 1) * 256], [x[:, kk * 256:(kk + 1) * 256] for x in w],
                                  [x[:, k * T + tb * P:k * T + (tb + 1) * P] for x in act],
                                  start=hf == 0 and tb == 0 and kk == 0, stop=k == KT - 1, weights_move=True)
            mm.then_inc(s["piece_done"], 1)

    def half_project(seg, act):
        for n in range(4):
            bank_free(SEG[seg] + n)
            w = piece(BLK[seg] + n // 2, n % 2)
            for j in range(2):
                for k in range(4):
                    mm = split_mm(ps[:, (SEG[seg] + n) % BANKS, j * T:(j + 1) * T],
                                  [x[:, k * 256 + j * P:k * 256 + (j + 1) * P] for x in w],
                                  [x[:, k * T:(k + 1) * T] for x in act], start=j == 0 and k == 0, stop=k == 3)
            mm.then_inc(s["piece_done"], 1)

    def project(seg, act, first=0, n=4, groups=1, token=False):
        n0, b0 = SEG[seg] + first, BLK[seg] + first
        body = token_block if token else up_block
        if groups > 1:
            with pe.Fori(0, groups) as i:
                for k in range(n):
                    body(i * n + (n0 + k), (n0 + k) % BANKS, At(i * n + (b0 + k), b0 + k), act)
            return
        for k in range(n):
            body(n0 + k, (n0 + k) % BANKS, b0 + k, act)

    def operand(name):
        pe.wait_ge(s["op_low"], 4 * (OPERAND[name] + 1))

    def norm_sum(name):
        i = NORM[name]
        for k in range(KT):
            if k % 4 == 0:
                pe.wait_ge(s["norm_sq"], 2 * i + k // 4 + 1)
            mm = pe.matmul(ps[:, 4, 0:T], cst(t, "ones"), t.sq[:, k * T:(k + 1) * T], start=k == 0, stop=k == KT - 1)
        mm.then_inc(s["norm_sum"], 1)

    norm_parts = (t.sq_r, t.h_r)

    def ffn(f, seg, name):
        norm_sum(name)
        operand(name)
        n, b = SEG[seg], BLK[seg]

        def down(step, blk, buf):
            pe.wait_ge(s["hidden_ready"], step + (f * FIT + 1))
            hid = hidden_parts(t, buf)
            for k in range(2):
                w = piece(blk, k)
                for j in range(KT):
                    mm = split_mm(ps[:, 4 + j // 2, (j % 2) * T:(j % 2 + 1) * T], [x[:, j * P:(j + 1) * P] for x in w],
                                  [x[:, k * T:(k + 1) * T] for x in hid], start=False, stop=False)
                mm.then_inc(s["piece_done"], 1)

        up_block(n, n % BANKS, b, norm_parts)
        up_block(n + 1, (n + 1) % BANKS, b + 1, norm_parts)
        if f == 0:
            pe.wait_ge(s["zero_row"], 1)
        for bank in range(4, 8):
            pe.matmul(ps[:, bank, :], t.zrow[:, :], t.zrow[:, 0:1].broadcast_to([P, 512]), start=True, stop=True,
                      skip_group_check=True)
        with pe.Fori(0, (FIT - 1) // 2) as i:
            for k in range(2):
                r = b + 2 + 3 * k
                for j in range(2):
                    m = n + 2 + 2 * k + j
                    up_block(i * 4 + m, m % BANKS, At(i * 6 + (r + j), r + j), norm_parts)
                down(i * 2 + k, At(i * 6 + (r + 2), r + 2), k)
        down(FIT - 1, b + 3 * FIT - 1, 0)

    def attention(g0, heads, q, k, v, kcs, dcs, dst_rows, bias=None):
        def scores(g):
            h = g - g0
            if g >= 2:
                pe.wait_ge(s["att_exp"], g - 1)
            for qb in range(TB):
                if bias:
                    pe.matmul(ps[:, 4 + g % 2, qb * 256:(qb + 1) * 256], cst(t, "flip"), bias(h, qb),
                              start=True, stop=False, skip_group_check=True)
                for c in range(kcs):
                    mm = pe.matmul(ps[:, 4 + g % 2, qb * 256:(qb + 1) * 256], q(h, c)[:, qb * P:(qb + 1) * P],
                                   k(h, c), start=c == 0 and not bias, stop=c == kcs - 1, skip_group_check=bool(bias))
            mm.then_inc(s["att_scores"], 1)

        def turn(g):
            pe.wait_ge(s["att_prob"], g + 1)
            if g >= 1:
                pe.wait_ge(s["att_turned_sb"], g)
            for qb in range(TB):
                for mb in range(TB):
                    mm = pe.transpose(ps[:, 6, mb * 256 + qb * P:mb * 256 + (qb + 1) * P],
                                      att_buf(t, g)[:, qb * 256 + mb * P:qb * 256 + (mb + 1) * P], cst(t, "ident"))
            mm.then_inc(s["att_turned"], 1)

        def mix(g):
            h = g - g0
            pe.wait_ge(s["att_turned_sb"], g + 1)
            if g >= 1:
                pe.wait_ge(s["att_low"], g)
            for c in range(dcs):
                for mb in range(TB):
                    mm = pe.matmul(ps[dst_rows(h), 7, c * T:(c + 1) * T], v(h, c, mb),
                                   att_turned(t, g)[:, mb * T:(mb + 1) * T], start=mb == 0, stop=mb == TB - 1)
            mm.then_inc(s["att_out"], 1)

        scores(g0)
        for g in range(g0, g0 + heads):
            if g + 1 < g0 + heads:
                scores(g + 1)
            turn(g)
            mix(g)

    pe.wait_ge(s["consts_in"], 32)
    norm_sum("mem")
    operand("mem")
    mem_parts = (t.page_r[2], t.page_r[1])
    project("mem_k", mem_parts, n=2)
    project("mem_v", mem_parts, n=2, token=True)

    norm_sum("mix0")
    operand("mix0")
    project("w_in", norm_parts)
    project("w_in", norm_parts, first=4, token=True)
    project("w_in", norm_parts, first=8, groups=4)
    project("w_in", norm_parts, first=24, n=2, token=True)
    project("w_in", norm_parts, first=26, n=2)
    project("w_in", norm_parts, first=28, groups=3)

    half = FP // 2
    pe.wait_ge(s["u_evac"], SEG["w_in"] + 28)
    pe.wait_ge(s["bias_ready"], 2)
    pr = lambda h: slice(NA_D * (h % 2), NA_D * (h % 2 + 1))
    attention(0, NA_H,
              lambda h, c: t.page[5][pr(h), h // 2 * T:(h // 2 + 1) * T],
              lambda h, c: t.page[5][pr(h), half + h // 2 * T:half + (h // 2 + 1) * T],
              lambda h, c, mb: t.page[6][:, mb * 512 + h * NA_D:mb * 512 + (h + 1) * NA_D],
              1, 1, pr, lambda h, qb: t.page[14 + qb][:, h * 256:(h + 1) * 256])
    whole = lambda h: slice(0, P)
    attention(NA_H, CA_H,
              lambda h, c: t.page[6][:, half + h * T:half + (h + 1) * T],
              lambda h, c: t.page[10][:, h * T:(h + 1) * T],
              lambda h, c, mb: t.page[10][:, half + mb * 512 + h * CA_D:half + mb * 512 + (h + 1) * CA_D],
              1, 1, whole)
    pe.wait_ge(s["att_low"], NA_H + CA_H)
    half_project("na_o", (t.sq_r[:, 0:half], t.h_r[:, 0:half]))
    half_project("ca_o", (t.sq_r[:, half:FP], t.h_r[:, half:FP]))

    for i, (level, hh) in enumerate(HG_STEPS):
        pe.wait_ge(s["hg_gh"], i + 1)
        if i >= 2:
            pe.wait_ge(s["hg_kept"], i - 1)
        keys, queries = hg_buf(t, i)
        if level == "same":
            queries = t.page[0][:, hh * 1024:(hh + 1) * 1024]
        for j in range(8):
            h, b = j // 2, j % 2
            qb = 1 - b if level == 128 else b
            mm = pe.matmul(ps[:, 4 + 2 * (i % 2) + j // 4, (j % 4) * P:(j % 4 + 1) * P],
                           keys[:, h * T + b * P:h * T + (b + 1) * P], queries[:, h * T + qb * P:h * T + (qb + 1) * P],
                           start=True, stop=True)
        mm.then_inc(s["hg_sc"], 1)
    pe.wait_ge(s["hg_kept"], len(HG_STEPS))
    for h in range(HG_H):
        for qb in range(TB):
            for b in range(TB):
                kept = (t.page[14] if b == qb else t.page[15])[:, (h * 2 + b) * P:(h * 2 + b + 1) * P]
                mm = pe.matmul(ps[:, 4 + h // 2, (h % 2) * T + qb * P:(h % 2) * T + (qb + 1) * P],
                               t.page[1][:, b * D + h * HG_D:b * D + (h + 1) * HG_D], kept, start=b == 0, stop=b == 1)
        if h % 2:
            mm.then_inc(s["hg_av"], 1)
    for q in range(4):
        pe.wait_ge(s["hg_sq"], q + 1)
        pe.matmul(ps[:, q, :], cst(t, "ones"), t.page[6][:, q * 512:(q + 1) * 512],
                  start=True, stop=True).then_inc(s["hg_var"], 1)
    operand("hg")
    project("hg_o", (t.page_r[6], t.page_r[5]))
    operand("merged")
    project("w_out", (t.page_r[11], t.page_r[10]))

    ffn(0, "ffn0", "ffn0")
    norm_sum("fin0")
    ffn(1, "ffn1", "ffn1")

    norm_sum("mix1")
    for i, seg in enumerate(("rw_r", "rw_k", "rw_v")):
        operand(f"rw{i}")
        project(seg, mix_parts(t, i))
    b = BLK["lora"]
    wh, wl = zip(piece(b, 0), piece(b, 1))
    for i in range(3, 6):
        operand(f"rw{i}")
    first = [[x[k // 4][:, (k % 4) * 256:(k % 4) * 256 + 256] for k in range(KT)] for x in (wh, wl)]
    gate2 = piece(b + 1, 0)
    for bank, i, w in ((4, 3, [[x[:, 0:P] for x in y] for y in first]),
                       (5, 4, [[x[:, 0:P] for x in y] for y in first]),
                       (6, 5, [[x[:, P:] for x in y] for y in first]),
                       (7, 5, [[x[:, k * P:(k + 1) * P] for k in range(KT)] for x in gate2])):
        act = mix_parts(t, i)
        for k in range(KT):
            mm = split_mm(ps[:, bank, 0:T], (w[0][k], w[1][k]), [x[:, k * T:(k + 1) * T] for x in act],
                          start=k == 0, stop=k == KT - 1)
    mm.then_inc(s["piece_done"], 3)
    operand("lora")
    inner = (t.sq_r, t.work_r)
    for which in range(3):
        if which:
            pe.wait_ge(s["lora_out"], which)
        w = piece(b + 1, 1) if which < 2 else (*piece(b + 2, 0), *piece(b + 2, 1))
        for j in range(KT):
            out = ps[:, 4 + j // 2, (j % 2) * T:(j % 2 + 1) * T]
            cols = slice(j * P, (j + 1) * P)
            if which < 2:
                mm = split_mm(out, [x[:, cols] for x in w], [x[:, which * T:(which + 1) * T] for x in inner],
                              start=True, stop=True)
            else:
                for c in range(2):
                    mm = split_mm(out, [x[:, cols] for x in w[2 * c:2 * c + 2]],
                                  [x[:, (2 + c) * T:(3 + c) * T] for x in inner], start=c == 0, stop=c == 1)
        if which == 0:
            mm.then_inc(s["lora_mm"], 1)
        else:
            mm.then_inc(s["piece_done"], which)

    for q in range(4):
        pe.wait_ge(s["rw_kk2"], q + 1)
        if q == 0:
            pe.wait_ge(s["u_evac"], SEG["rw_o"])
        pe.matmul(ps[:, q, :], cst(t, "head_ones"), t.sq[:, q * 512:(q + 1) * 512],
                  start=True, stop=True).then_inc(s["rw_kksum"], 1)
    for q in range(4):
        if q == 0:
            pe.wait_ge(s["rw_bonus_in"], 1)
        pe.matmul(ps[:, q, :], cst(t, "head_ones"), t.work[:, q * 512:(q + 1) * 512],
                  start=True, stop=True).then_inc(s["rw_bonus_sum"], 1)

    for q in range(12):
        src = (t.page[9], t.page[5], t.page[6])[q // 4]
        b, c0 = q % 4 // 2, q % 2 * 4
        if q == 0:
            pe.wait_ge(s["lora_out"], 3)
            pe.wait_ge(s["rw_dec"], 1)
        if q >= 4:
            pe.wait_ge(s["rw_t_sb"], q - 3)
        for c in range(4):
            mm = pe.transpose(ps[:, 4 + q % 4, c * P:(c + 1) * P],
                              src[:, (c0 + c) * T + b * P:(c0 + c) * T + (b + 1) * P], cst(t, "ident"))
        mm.then_inc(s["rw_t"], 1)

    A, B, K, R = t.page[3], t.page[5], t.page[6], t.page[7]

    def chunk_matrices(c):
        for p, pair in enumerate((((B, A), (A, B)), ((K, A), (B, R)), ((K, R),))):
            q = 3 * c + p
            if q == 0:
                pe.wait_ge(s["rw_act"], 1)
            if q >= 2:
                pe.wait_ge(s["rw_m_sb"], q - 1)
            for e in range(2):
                hp = slice(RW_D * e, RW_D * (e + 1))
                for j, (left, right) in enumerate(pair):
                    for b in range(TB):
                        tok = slice(c * T + b * P, c * T + (b + 1) * P)
                        mm = pe.matmul(ps[:, 2 * (q % 2) + e, (2 * j + b) * P:(2 * j + b + 1) * P],
                                       left[hp, tok], right[hp, tok], start=True, stop=True)
            mm.then_inc(s["rw_m"], 1)

    def invert_y(c, lv):
        q, buf = inv_at(c, lv), inv_buf(t, c)
        if lv == 0:
            pe.wait_ge(s["rw_m_sb"], 3 * c + 3)
        else:
            pe.wait_ge(s["rw_z_sb"], q - 1)
        pe.wait_ge(s["rw_lm"], q + 1)
        if q == 0:
            pe.wait_ge(s["rw_t_sb"], 12)
        for j in range(4):
            mm = pe.matmul(ps[:, 4 + 2 * (c % 2), j * P:(j + 1) * P], buf.lm[:, j * P:(j + 1) * P],
                           buf.x[:, j * P:(j + 1) * P], start=True, stop=True)
        mm.then_inc(s["rw_y"], 1)

    def invert_z(c, lv):
        q, buf, xt = inv_at(c, lv), inv_buf(t, c), inv_xt(t, c)
        pe.wait_ge(s["rw_y_sb"], q + 1)
        if lv < len(LEVELS) - 2:
            for j in range(4):
                pe.matmul(ps[:, 4 + 2 * (c % 2), j * P:(j + 1) * P], xt[:, j * P:(j + 1) * P],
                          buf.y[:, j * P:(j + 1) * P], start=True, stop=True)
        for j in range(4):
            mm = pe.matmul(ps[:, 5 + 2 * (c % 2), j * P:(j + 1) * P], buf.y[:, j * P:(j + 1) * P],
                           xt[:, j * P:(j + 1) * P], start=True, stop=True)
        mm.then_inc(s["rw_z"], 1)

    for c in range(0, KT, 2):
        chunk_matrices(c)
        chunk_matrices(c + 1)
        for lv in range(len(LEVELS) - 1):
            invert_y(c, lv)
            invert_y(c + 1, lv)
            invert_z(c, lv)
            invert_z(c + 1, lv)

    rhs, usb, st = t.page[5][:, 0:1024], t.page[5][:, 1024:], t.page[6][:, 0:1024]
    vt, bt, kt_ = t.page[1], t.page[2], t.page[4]

    def mat(base, c, e, b):
        page = base[c // 4]
        at_ = ((c % 4) * 4 + e * 2 + b) * P
        return page[:, at_:at_ + P]

    pe.wait_ge(s["rw_z_sb"], 8 * (len(LEVELS) - 1))
    pe.wait_ge(s["rw_m_sb"], 24)
    pe.wait_ge(s["rw_zero"], 1)
    for n_ in range(NCH):
        b, po = n_ // 2, slice(CH * (n_ % 2), CH * (n_ % 2 + 1))
        if n_ > 0:
            pe.wait_ge(s["rw_s"], n_)
        for c in range(KT):
            out = ps[po, c // 4, (c % 4) * P:(c % 4 + 1) * P]
            tok = slice(c * T + n_ * CH, c * T + (n_ + 1) * CH)
            pe.matmul(out, A[:, tok], st[:, c * P:(c + 1) * P], start=True, stop=False, skip_group_check=True)
            for e in range(2):
                mm = pe.matmul(out[:, e * CH:(e + 1) * CH], mat(RW_MT(t), c, e, b)[:, po],
                               vt[:, b * D + c * P + e * RW_D:b * D + c * P + (e + 1) * RW_D],
                               start=False, stop=e == 1, skip_group_check=True)
        mm.then_inc(s["rw_rhs"], 1)
        for c in range(KT):
            pe.matmul(ps[:, 4 + c // 2, (c % 2) * T + n_ * CH:(c % 2) * T + (n_ + 1) * CH],
                      st[:, c * P:(c + 1) * P], R[:, c * T + n_ * CH:c * T + (n_ + 1) * CH],
                      start=n_ == 0 and c % 2 == 0, stop=False, skip_group_check=True)
        pe.wait_ge(s["rw_rhs_sb"], 2 * (n_ + 1))
        for c in range(KT):
            for e in range(2):
                cols = slice(c * P + e * RW_D, c * P + (e + 1) * RW_D)
                mm = pe.matmul(ps[po, 2 + c // 4, (c % 4) * P + e * CH:(c % 4) * P + (e + 1) * CH],
                               mat(RW_TT(t), c, e, b)[:, po], rhs[:, cols], start=True, stop=True,
                               skip_group_check=True)
        mm.then_inc(s["rw_u"], 1)
        pe.wait_ge(s["rw_u_sb"], 2 * (n_ + 1))
        if n_ < NCH - 1:
            for c in range(KT):
                out = ps[:, c // 4, (c % 4) * P:(c % 4 + 1) * P]
                cols = slice(c * P, (c + 1) * P)
                full = slice(b * D + c * P, b * D + (c + 1) * P)
                pe.matmul(out, bt[po, full], usb[po, cols], start=True, stop=False, skip_group_check=True)
                mm = pe.matmul(out, kt_[po, full], vt[po, full], start=False, stop=True, skip_group_check=True)
            mm.then_inc(s["rw_ds"], 1)
        if n_ % 2:
            for c in range(KT):
                for e in range(2):
                    out = ps[e * RW_D:(e + 1) * RW_D, 4 + c // 2, (c % 2) * T + b * P:(c % 2) * T + (b + 1) * P]
                    cols = slice(c * P + e * RW_D, c * P + (e + 1) * RW_D)
                    pe.matmul(out, vt[:, b * D + cols.start:b * D + cols.stop], mat(RW_RKT(t), c, e, b),
                              start=False, stop=False, skip_group_check=True)
                    mm = pe.matmul(out, usb[:, cols], mat(RW_RBT(t), c, e, b), start=False,
                                   stop=False, skip_group_check=True)
    mm.then_inc(s["rw_yt"], 1)
    for q in range(4):
        pe.wait_ge(s["rw_yt_sb"], q + 1)
        pe.matmul(ps[:, q, :], cst(t, "head_ones"), t.page[8][:, q * 512:(q + 1) * 512],
                  start=True, stop=True).then_inc(s["rw_mean"], 1)
    for q in range(4):
        pe.wait_ge(s["rw_sq"], q + 1)
        pe.matmul(ps[:, q, :], cst(t, "head_ones"), t.sq[:, q * 512:(q + 1) * 512],
                  start=True, stop=True).then_inc(s["rw_var"], 1)
    operand("rw_o")
    project("rw_o", (t.page_r[10], t.page_r[7]))

    norm_sum("mem2")
    operand("mem2")
    mem_parts = (t.page_r[4], t.page_r[3])
    project("mem2_k", mem_parts)
    project("mem2_v", mem_parts, token=True)

    def memory_attention(i, name):
        norm_sum(name)
        operand(name)
        project(f"xq{i}", norm_parts)
        pe.wait_ge(s["u_evac"], SEG[f"xq{i}"] + 4)
        attention(NA_H + CA_H + XA_H * i, XA_H,
                  lambda h, c: t.page[0][:, (2 * h + c) * T:(2 * h + c + 1) * T],
                  lambda h, c: t.page[14][:, (2 * h + c) * T:(2 * h + c + 1) * T],
                  lambda h, c, mb: t.page[15][:, mb * D + h * XA_D + c * P:mb * D + h * XA_D + (c + 1) * P],
                  2, 2, whole)
        pe.wait_ge(s["att_low"], NA_H + CA_H + XA_H * (i + 1))
        project(f"xo{i}", (t.page_r[2], t.page_r[1]))

    memory_attention(0, "x0")
    ffn(2, "ffn2", "ffn2")
    ffn(3, "ffn3", "ffn3")

    norm_sum("mix2")
    operand("mix2")
    project("gm_u", norm_parts, groups=2)
    project("gm_v", norm_parts, groups=2, token=True)
    pe.wait_ge(s["gm_mask"], 1)
    for q in range(8):
        if q < 2:
            pe.wait_ge(s["gm_vout"], 1)
        else:
            pe.wait_ge(s["gm_mixed"], q - 1)
        for j in range(4):
            g, b = 2 * q + j // 2, j % 2
            mm = pe.matmul(ps[:, 4 + q % 2, j * P:(j + 1) * P],
                           t.page[2 + b][:, g * P:(g + 1) * P], t.page[4][:, g * P:(g + 1) * P],
                           start=True, stop=True)
        mm.then_inc(s["gm_mix"], 1)
    operand("gm1")
    for q in range(4):
        n, b = SEG["gm_o"] + q, BLK["gm_o"] + 2 * q
        bank_free(n)
        for k4 in range(4):
            w = piece(b + k4 // 2, k4 % 2)
            for j in range(2):
                for kk in range(4):
                    k = 4 * k4 + kk
                    mm = split_mm(ps[:, n % BANKS, j * T:(j + 1) * T],
                                  [x[:, kk * 256 + j * P:kk * 256 + (j + 1) * P] for x in w],
                                  [t.page_r[first + k // KT][:, k % KT * T:(k % KT + 1) * T] for first in (10, 7)],
                                  start=k4 == 0 and j == 0 and kk == 0, stop=k == 2 * KT - 1)
            mm.then_inc(s["piece_done"], 1)
    memory_attention(1, "x1")
    ffn(4, "ffn4", "ffn4")
    norm_sum("fin2")


class At:

    def __init__(self, number, first):
        self.number, self.first = number, first

    def __mul__(self, k):
        return self.number * k

    def __add__(self, k):
        return At(self.number + k, self.first + k)


def block0(b):
    return b if isinstance(b, int) else b.first


def hidden_parts(t, k):
    return t.page_r[2][:, k * 512:(k + 1) * 512], t.work_r[:, k * 512:(k + 1) * 512]


def mix_parts(t, i):
    return t.page_r[10 + i], t.page_r[1 + i]


HG_STEPS = [(level, hh) for level in (64, *LEVELS, 128, "same") for hh in range(2)]


def hg_buf(t, i):
    buf = t.page[13] if i % 2 == 0 else t.sq[:, :]
    return buf[:, 1024:2048], buf[:, 0:1024]


def att_buf(t, g):
    return t.page[13][:, (g % 2) * 512:(g % 2 + 1) * 512]


def att_turned(t, g):
    return t.page[13][:, 1024 + (g % 2) * 512:1024 + (g % 2 + 1) * 512]


def inv_at(c, lv):
    return c // 2 * 2 * (len(LEVELS) - 1) + 2 * lv + c % 2


def inv_buf(t, c):
    buf = t.sq[:, :] if c % 2 == 0 else t.work[:, :]
    parts = Bag()
    parts.lt, parts.lm, parts.x, parts.y = (buf[:, i:i + 512] for i in range(0, 2048, 512))
    return parts


def stack(pages, c):
    return pages[c // 4][:, (c % 4) * 512:(c % 4 + 1) * 512]


def RW_MT(t):
    return t.page[8], t.page[9]


def RW_RBT(t):
    return t.page[10], t.page[11]


def RW_RKT(t):
    return t.page[12], t.page[14]


def RW_TT(t):
    return t.page[15], t.h[:, :]


def inv_xt(t, c):
    return stack(RW_TT(t), c)


def norm_table(t, s):
    x, h, seg = t.x[:, :], t.h[:, :], SEG
    up = lambda n, f: (s["x_up"], 4 * f + 2, 2)
    rows = {
        "mem": (t.page[0], (s["mem_in"], 16, 0), ("mem_norm", 0), t.page[1]),
        "mix0": (x, (s["x_in"], 16, 0), ("norm_mix", 0), h),
        "ffn0": (x, (s["u_evac"], seg["w_out"] + 2, 2), ("norm_ffn", 0), h),
        "fin0": (x, (s["x_up"], 2, 2), ("norm_final", 0), x),
        "ffn1": (x, (s["norm_out"], KT * NORM["fin0"] + 4, 4), ("ffn1_norm_2", 0), h),
        "mix1": (x, (s["x_up"], 4 + 2, 2), ("mix_norm_2", 0), h),
        "mem2": (t.page[3], (s["mem2_in"], 16, 0), ("mem_norm_2", 0), t.page[3]),
        "x0": (x, (s["u_evac"], seg["rw_o"] + 2, 2), ("xattn_norm_2", 0), h),
        "ffn2": (x, (s["u_evac"], seg["xo0"] + 2, 2), ("ffn2_norm_2", 0), h),
        "ffn3": (x, (s["x_up"], 8 + 2, 2), ("ffn1_norm_2", 8), h),
        "mix2": (x, (s["x_up"], 12 + 2, 2), ("mix_norm_2", 8), h),
        "x1": (x, (s["u_evac"], seg["gm_o"] + 2, 2), ("xattn_norm_2", 8), h),
        "ffn4": (x, (s["u_evac"], seg["xo1"] + 2, 2), ("ffn2_norm_2", 8), h),
        "fin2": (x, (s["x_up"], 16 + 2, 2), ("final_norm_2", 0), h),
    }
    return rows


def NORM_HIGH(t, name):
    return {"mem": t.page_r[2], "mem2": t.page_r[4]}.get(name, t.sq_r)


def NORM_LOW(t, name):
    return {"mem": t.page_r[1], "mem2": t.page_r[3]}.get(name, t.h_r)


def scalar_program(act, a, t, s):
    ps = t.ps
    norms = norm_table(t, s)
    f = act.activation

    def high(b):
        b0 = block0(b) + AHEAD
        if isinstance(b, int) and b0 >= N_BLK:
            return
        b = b + AHEAD
        act.wait_ge(s["raw_in"][b0 % 2], (b0 // 2 + 1) * 16 if isinstance(b, int) else b * 8 + (16 - b0 % 2 * 8))
        for hf in range(2):
            if not isinstance(b, int) or b0 >= 2:
                act.wait_ge(s["piece_done"], b * 2 + (hf - 3))
            f(t.wh[(2 * b0 + hf) % PIECE_SLOTS][:], t.raw[b0 % 2][:, hf * 1024:(hf + 1) * 1024],
              ACT.Copy).then_inc(s["high_done"], 1)

    def highs(seg, first=0, n=4):
        for k in range(n):
            high(BLK[seg] + first + k)

    def operand_high(name, src, dst, ready, width=512):
        for q in range(4):
            c = slice(q * width, (q + 1) * width)
            ready(q)
            f(dst[:, c], src[:, c], ACT.Copy).then_inc(s["op_high"], 1)

    def norm_ready(name):
        return lambda q: act.wait_ge(s["norm_out"], KT * NORM[name] + 2 * (q + 1))

    def norm(name):
        i = NORM[name]
        src, (sem, first, step), _, _ = norms[name]
        if i:
            act.wait_ge(s["norm_sum"], i)
        for hf in range(2):
            act.wait_ge(sem, first + step * hf)
            f(t.sq[:, hf * 1024:(hf + 1) * 1024], src[:, hf * 1024:(hf + 1) * 1024], ACT.Square).then_inc(s["norm_sq"], 1)
        act.wait_ge(s["norm_var"], i + 1)
        f(t.rstd[:], t.rstd[:], ACT.Sqrt).then_inc(s["norm_std"], 1)
        if name in OPERAND:
            dst, out = norms[name][3], NORM_HIGH(t, name)
            operand_high(name, dst, out, norm_ready(name))

    def take(n, bank, b, dst, func=ACT.Copy):
        act.wait_ge(s["piece_done"], b * 2 + 2)
        src = ps[:, bank, :]
        if len(dst.shape) == 3:
            src = src.rearrange("p (b c) -> p b c", b=dst.shape[1])
        f(dst, src, func).then_inc(s["u_evac"], 1)

    def take_run(seg, page, first=0, n=4, func=ACT.Copy):
        for k in range(n):
            high(BLK[seg] + first + k)
            take(SEG[seg] + first + k, (SEG[seg] + first + k) % BANKS, BLK[seg] + first + k,
                 page[:, k * 512:(k + 1) * 512], func)

    def take_groups(seg, page0, first, groups, func=ACT.Copy):
        n0, b0 = SEG[seg] + first, BLK[seg] + first
        with act.Fori(0, groups) as i:
            for k in range(4):
                b = At(i * 4 + (b0 + k), b0 + k)
                high(b)
                take(None, (n0 + k) % BANKS, b,
                     t.pages[:, bass.ds(i * FP + (page0 * FP + k * 512), 512)], func)

    def take_tokens(seg, region, width, first=0, n=4, func=ACT.Copy):
        for k in range(n):
            high(BLK[seg] + first + k)
            dst = region.rearrange("p (b c) -> p b c", b=TB)[:, :, k * 256:(k + 1) * 256]
            take(SEG[seg] + first + k, (SEG[seg] + first + k) % BANKS, BLK[seg] + first + k, dst, func)

    def attention(g0, heads, scale, cols, dst):
        def exp(g):
            buf, st = att_buf(t, g), (g % 2) * 8
            act.wait_ge(s["att_max"], g + 1)
            if g >= 2:
                act.wait_ge(s["att_turned"], g - 1)
            for qb in range(TB):
                src = ps[:, 4 + g % 2, qb * 256:(qb + 1) * 256]
                ins = f(buf[:, qb * 256:(qb + 1) * 256], src, ACT.Exp, bias=t.stat[:, st + 2 + qb:st + 3 + qb],
                        scale=scale, accum_out=t.stat[:, st + 4 + qb:st + 5 + qb])
            ins.then_inc(s["att_exp"], 1)

        exp(g0)
        for g in range(g0, g0 + heads):
            if g + 1 < g0 + heads:
                exp(g + 1)
            act.wait_ge(s["att_turned"], g + 1)
            if g >= 2:
                act.wait_ge(s["att_out"], g - 1)
            f(att_turned(t, g), ps[:, 6, :], ACT.Copy).then_inc(s["att_turned_sb"], 1)
            act.wait_ge(s["att_out"], g + 1)
            out = dst(g - g0)
            rows = slice(out[0], out[1])
            f(out[2], ps[rows, 7, 0:cols], ACT.Copy).then_inc(s["att_high"], 1)

    act.wait_ge(s["consts_in"], 32)
    for b in range(-AHEAD, 0):
        high(b)
    norm("mem")
    act.wait_ge(s["lb_zero"], 1)
    f(t.lb[:, 16:32], t.lb[:, 0:16], ACT.Exp).then_inc(s["lb_exp"], 1)
    take_run("mem_k", t.page[10], n=2)
    take_tokens("mem_v", t.page[10][:, 1024:2048], 512, n=2)
    norm("mix0")
    take_run("w_in", t.page[0])
    take_tokens("w_in", t.page[1], D, first=4)
    take_groups("w_in", 2, 8, 4)
    take_tokens("w_in", t.page[6][:, 0:1024], 512, first=24, n=2)
    take_run("w_in", t.page[6][:, 1024:2048], first=26, n=2)

    act.wait_ge(s["u_evac"], SEG["w_in"] + 20)
    for src, dst in ((2, 11), (3, 12)):
        f(t.page[dst], t.page[src], ACT.Sigmoid).then_inc(s["hg_sig"], 1)
        f(t.page[src], t.page[src], ACT.Sigmoid, scale=-1.0).then_inc(s["hg_sig"], 1)
    take_groups("w_in", 7, 28, 3, ACT.Sigmoid)
    f(t.page[0], t.page[0], ACT.Silu).then_inc(s["hg_silu"], 1)
    f(t.page[4], t.page[4], ACT.Silu).then_inc(s["hg_silu"], 1)
    for i in range(2):
        act.wait_ge(s["hg_floor"], i + 1)
        f(t.page[11 + i], t.page[11 + i], ACT.Ln).then_inc(s["hg_log"], 1)

    def na_dst(h):
        lo = NA_D * (h % 2)
        return lo, lo + NA_D, t.sq_r[lo:lo + NA_D, h // 2 * T:(h // 2 + 1) * T]

    attention(0, NA_H, NA_D ** -0.5, T, na_dst)
    attention(NA_H, CA_H, CA_D ** -0.5, T, lambda h: (0, P, t.sq_r[:, 1024 + h * T:1024 + (h + 1) * T]))
    highs("na_o", n=2)
    highs("ca_o", n=2)

    for i, (level, hh) in enumerate(HG_STEPS):
        if level == "same":
            continue
        act.wait_ge(s["hg_expo"], i + 1)
        buf = t.page[13] if i % 2 == 0 else t.sq[:, :]
        f(buf, buf, ACT.Exp).then_inc(s["hg_exp"], 1)
    for q in range(4):
        c = slice(q * 512, (q + 1) * 512)
        act.wait_ge(s["hg_av"], q + 1)
        f(t.page[5][:, c], ps[:, 4 + q, :], ACT.Copy, scale=HG_D ** -0.5).then_inc(s["hg_o"], 1)
        act.wait_ge(s["hg_o"], q + 1)
        f(t.page[6][:, c], t.page[5][:, c], ACT.Square).then_inc(s["hg_sq"], 1)
    for q in range(4):
        act.wait_ge(s["hg_varsb"], q + 1)
        f(t.page[2][:, q * 512:(q + 1) * 512], t.page[2][:, q * 512:(q + 1) * 512], ACT.Sqrt).then_inc(s["hg_std"], 1)

    operand_high("hg", t.page[5], t.page_r[6], lambda q: act.wait_ge(s["hg_out"], q + 1))
    highs("hg_o")
    operand_high("merged", t.page[10], t.page_r[11], lambda q: act.wait_ge(s["merged"], q + 1))
    highs("w_out")

    def hidden_high(fi, st, k):
        act.wait_ge(s["hidden_made"], st + (fi * FIT + 1))
        f(hidden_parts(t, k)[0], t.work[:, k * 512:(k + 1) * 512], ACT.Copy).then_inc(s["hidden_high"], 1)

    def ffn(fi, seg, early, late):
        b = BLK[seg]
        high(b)
        early(0, 0, 0, True)
        high(b + 1)
        late(0, 0, 0, True)

        def two_steps(i, first=False):
            for k in range(2):
                r = b + 2 + 3 * k
                blk = [i * 6 + (r + j) if isinstance(i, int) else At(i * 6 + (r + j), r + j) for j in range(3)]
                step = (i * 2 + (1 + k), i * 4 + (2 + 2 * k), (1 + k) % 2, first and k == 0)
                high(blk[0])
                early(*step)
                high(blk[1])
                late(*step)
                high(blk[2])

        trips = (FIT - 1) // 2
        if fi == 0:
            two_steps(0, first=True)
        last = trips - 1 if fi == N_FFN - 1 else trips
        with act.Fori(int(fi == 0), last) as i:
            two_steps(i)
        if last < trips:
            two_steps(last)
        high(b + 3 * FIT - 1)

    norm("ffn0")
    cw, cb = PCOL["conv_w"] + 44, PCOL["conv_b"]

    def conv_middle(st, tile, k, first):
        bank = (SEG["ffn0"] + 2 * k) % BANKS
        act.wait_ge(s["piece_done"], 2 * BLK["ffn0"] + 4 if isinstance(st, int) and st == 0
                    else st * 6 + (2 * BLK["ffn0"] + 2))
        if not first:
            act.wait_ge(s["hidden_made"], st - 1)
        for j in range(4):
            col = tile + (j % 2 + FF // P * (j // 2))
            if isinstance(col, int):
                w, bias = t.param[:, cw + col:cw + col + 1], t.param[:, cb + col:cb + col + 1]
            else:
                w, bias = t.param[:, bass.ds(col + cw, 1)], t.param[:, bass.ds(col + cb, 1)]
            ins = f(t.page[k][:, j * T:(j + 1) * T], ps[:, bank + j // 2, (j % 2) * T:(j % 2 + 1) * T],
                    ACT.Identity, scale=w, bias=bias)
        ins.then_inc(s["conv_mid"], 1)
        act.wait_ge(s["conv_done"], st + 1)
        f(t.page[k][:, 0:512], t.page[k][:, 0:512], ACT.Gelu_apprx_tanh).then_inc(s["gelu_ready"], 1)
        hidden_high(0, st, k)

    assert SEG["ffn0"] % 2 == 0
    ffn(0, "ffn0", lambda *step: None, conv_middle)
    norm("fin0")

    def swiglu(fi, seg):
        def gate(st, tile, k, first):
            act.wait_ge(s["piece_done"], 2 * BLK[seg] + 2 if isinstance(st, int) and st == 0
                        else st * 6 + 2 * BLK[seg])
            act.wait_ge(s["u_evac"], st * 2 + (SEG[seg] - 2))
            f(t.work[:, 1024 + k * 512:1536 + k * 512], ps[:, (SEG[seg] + 2 * k) % BANKS, :],
              ACT.Silu).then_inc(s["gate_ready"], 1)

        ffn(fi, seg, gate, lambda st, tile, k, first: hidden_high(fi, st, k))

    norm("ffn1")
    swiglu(1, "ffn1")

    norm("mix1")
    for step in RW_ORDER:
        if isinstance(step, int):
            operand_high(f"rw{step}", t.page[1 + step], t.page_r[10 + step],
                         lambda q: act.wait_ge(s["rw_mix"], 4 * step + q + 1))
        else:
            k = int(step[1:])
            high(BLK["rw_r"] + k)
            take(None, (SEG["rw_r"] + k) % BANKS, BLK["rw_r"] + k,
                 t.pages[:, 7 * FP + k * 512:7 * FP + (k + 1) * 512])
    highs("lora", n=1)
    act.wait_ge(s["piece_done"], 2 * BLK["lora"] + 3)
    act.wait_ge(s["inner_zero"], 1)
    f(t.work[0:64, 0:T], ps[0:64, 4, 0:T], ACT.Tanh)
    f(t.work[64:P, T:2 * T], ps[64:P, 5, 0:T], ACT.Copy)
    for j in range(2):
        ins = f(t.work[:, (2 + j) * T:(3 + j) * T], ps[:, 6 + j, 0:T], ACT.Sigmoid)
    ins.then_inc(s["lora_mid"], 1)
    act.wait_ge(s["lora_mid"], 1)
    operand_high("lora", t.work[:, 0:1024], t.sq_r[:, 0:1024], lambda q: None, 256)
    for which, name in ((0, "rwkv_w0_2"), (1, "rwkv_a0_2")):
        if which:
            act.wait_ge(s["piece_done"], 2 * BLK["lora"] + 4)
        else:
            act.wait_ge(s["lora_mm"], 1)
        for j in range(KT):
            ins = f(t.page[11 + which][:, j * T:(j + 1) * T], ps[:, 4 + j // 2, (j % 2) * T:(j % 2 + 1) * T],
                    ACT.Sigmoid, bias=par(t, name, j))
        ins.then_inc(s["lora_out"], 1)
    highs("lora", 1, 2)
    act.wait_ge(s["piece_done"], 2 * BLK["lora"] + 6)
    f(t.page[13][:, 0:1024].rearrange("p (a b) -> p a b", a=2), ps[:, 4:6, :], ACT.Copy)
    f(t.page[13][:, 1024:].rearrange("p (a b) -> p a b", a=2), ps[:, 6:8, :], ACT.Copy).then_inc(s["lora_out"], 1)
    for q in range(4):
        c = slice(q * 512, (q + 1) * 512)
        act.wait_ge(s["rw_kk"], q + 1)
        f(t.sq[:, c], t.page[1][:, c], ACT.Square).then_inc(s["rw_kk2"], 1)
    for q in range(4):
        c = slice(q * 512, (q + 1) * 512)
        act.wait_ge(s["rw_kksum"], q + 1)
        f(t.page[2][:, c], ps[:, q, :], ACT.Sqrt).then_inc(s["rw_kkvar"], 1)
    RATE = float(np.exp(-0.5))
    act.wait_ge(s["rw_cum"], 1)
    f(t.page[3], t.page[3], ACT.Exp, scale=-RATE).then_inc(s["rw_exp"], 1)
    f(t.page[4], t.page[2], ACT.Exp, scale=RATE).then_inc(s["rw_exp"], 1)
    f(t.page[10], t.page[2], ACT.Exp, scale=-RATE).then_inc(s["rw_exp"], 1)
    for q in range(12):
        dst = (t.page[1], t.page[2], t.page[4])[q // 4]
        b, half = q % 4 // 2, q % 2
        act.wait_ge(s["rw_t"], q + 1)
        f(dst[:, b * D + half * 512:b * D + (half + 1) * 512], ps[:, 4 + q % 4, :], ACT.Copy).then_inc(s["rw_t_sb"], 1)
    for c0 in range(0, KT, 2):
        for lv in range(len(LEVELS) - 1):
            for c in (c0, c0 + 1):
                act.wait_ge(s["rw_y"], inv_at(c, lv) + 1)
                f(inv_buf(t, c).y, ps[:, 4 + 2 * (c % 2), :], ACT.Copy).then_inc(s["rw_y_sb"], 1)
    for n_ in range(NCH):
        po = slice(CH * (n_ % 2), CH * (n_ % 2 + 1))
        act.wait_ge(s["rw_rhs"], n_ + 1)
        f(t.page[5][po, 512:1024], ps[po, 1, :], ACT.Copy, scale=-1.0).then_inc(s["rw_rhs_sb"], 1)
        act.wait_ge(s["rw_u"], n_ + 1)
        f(t.page[5][po, 1536:2048], ps[po, 3, :], ACT.Copy).then_inc(s["rw_u_sb"], 1)
    act.wait_ge(s["rw_yt"], 1)
    act.dma_start(t.page[3], a.mem2_t).then_inc(s["mem2_in"], 16)
    act.dma_start(t.page[5], a.bias_rows).then_inc(s["rows_in"], 16)
    act.dma_start(t.page[6], a.gain_rows).then_inc(s["rows_in"], 16)
    act.dma_start(t.page[9], a.mix_weights).then_inc(s["rows_in"], 16)
    for q in range(4):
        f(t.page[8][:, q * 512:(q + 1) * 512], ps[:, 4 + q, :], ACT.Copy).then_inc(s["rw_yt_sb"], 1)
    for q in range(4):
        c = slice(q * 512, (q + 1) * 512)
        act.wait_ge(s["rw_cent"], q + 1)
        f(t.sq[:, c], t.page[8][:, c], ACT.Square).then_inc(s["rw_sq"], 1)
    for q in range(4):
        c = slice(q * 512, (q + 1) * 512)
        act.wait_ge(s["rw_varsb"], q + 1)
        f(t.page[2][:, c], t.page[2][:, c], ACT.Sqrt).then_inc(s["rw_std"], 1)

    operand_high("rw_o", t.page[7], t.page_r[10], lambda q: act.wait_ge(s["rw_out"], q + 1))
    highs("rw_o")
    norm("mem2")
    take_run("mem2_k", t.page[14])
    take_tokens("mem2_v", t.page[15], D)

    def memory_attention(i):
        norm(f"x{i}")
        take_run(f"xq{i}", t.page[0])
        attention(NA_H + CA_H + XA_H * i, XA_H, XA_D ** -0.5, 2 * T,
                  lambda h: (0, P, t.page_r[2][:, h * 512:(h + 1) * 512]))
        highs(f"xo{i}")

    memory_attention(0)
    norm("ffn2")
    swiglu(2, "ffn2")
    norm("ffn3")
    swiglu(3, "ffn3")

    norm("mix2")
    take_groups("gm_u", 0, 0, 2, ACT.Gelu_apprx_tanh)
    v2 = t.pages[:, 2 * FP:4 * FP].rearrange("p (b c) -> p b c", b=TB)
    with act.Fori(0, 2) as i:
        for k in range(4):
            b = At(i * 4 + (BLK["gm_v"] + k), BLK["gm_v"] + k)
            high(b)
            take(None, (SEG["gm_v"] + k) % BANKS, b, v2[:, :, bass.ds(i * 1024 + k * 256, 256)], ACT.Gelu_apprx_tanh)
    act.wait_ge(s["u_evac"], SEG["gm_v"] + 8)
    for b in range(TB):
        ins = f((t.sq, t.work)[b][:, :], t.page[2 + b], ACT.Square, accum_out=t.stat[:, 16 + b:17 + b])
    ins.then_inc(s["gm_vnorm"], 1)
    act.wait_ge(s["gm_vvar"], 1)
    f(t.stat[:, 18:20], t.stat[:, 18:20], ACT.Sqrt).then_inc(s["gm_vstd"], 1)
    for page in range(2):
        operand_high(f"gm{page}", t.page[7 + page], t.page_r[10 + page],
                     lambda q: act.wait_ge(s["gm_mixed"], 4 * page + q + 1))
    highs("gm_o", n=8)
    memory_attention(1)
    norm("ffn4")
    swiglu(4, "ffn4")
    norm("fin2")
    act.wait_ge(s["norm_out"], KT * len(NORM))
    act.dma_start(a.out, t.h[:, :]).then_inc(s["out_done"], 16)
    act.wait_ge(s["out_done"], 16)


def vector_program(dve, t, s):
    ps = t.ps
    norms = norm_table(t, s)
    link = Link(dve, s["dve_chain"])
    ts, tt, stt = dve.tensor_scalar, dve.tensor_tensor, dve.scalar_tensor_tensor

    def low(b):
        b0 = block0(b) + AHEAD
        if isinstance(b, int) and b0 >= N_BLK:
            return
        b = b + AHEAD
        for hf in range(2):
            i = (2 * b0 + hf) % PIECE_SLOTS
            dve.wait_ge(s["high_done"], b * 2 + (hf + 1))
            tt(t.wl[i][:], t.raw[b0 % 2][:, hf * 1024:(hf + 1) * 1024], t.wh[i][:].bitcast(F32),
               ALU.subtract).then_inc(s["low_done"], 1)

    def lows(seg, first=0, n=4):
        for k in range(n):
            low(BLK[seg] + first + k)

    def low_groups(seg, first, groups):
        with dve.Fori(0, groups) as i:
            for k in range(4):
                low(At(i * 4 + (BLK[seg] + first + k), BLK[seg] + first + k))

    def operand_low(name, src, high, dst, width=512):
        for q in range(4):
            c = slice(q * width, (q + 1) * width)
            dve.wait_ge(s["op_high"], 4 * OPERAND[name] + q + 1)
            tt(dst[:, c], src[:, c], high[:, c].bitcast(F32), ALU.subtract).then_inc(s["op_low"], 1)

    def norm(name):
        i = NORM[name]
        src, _, gain, dst = norms[name]
        dve.wait_ge(s["norm_sum"], i + 1)
        link(ts(t.rstd[:], ps[:, 4, 0:T], 1.0 / D, EPS, ALU.mult, ALU.add))
        dve.reciprocal(t.rstd[:], t.rstd[:]).then_inc(s["norm_var"], 1)
        dve.wait_ge(s["norm_std"], i + 1)
        for k in range(KT):
            c = slice(k * T, (k + 1) * T)
            stt(dst[:, c], src[:, c], par(t, gain[0], gain[1] + k), t.rstd[:],
                ALU.mult, ALU.mult).then_inc(s["norm_out"], 1)
        if name in OPERAND:
            operand_low(name, dst, NORM_HIGH(t, name), NORM_LOW(t, name))

    def residual(seg):
        for k in range(4):
            n = SEG[seg] + k
            low(BLK[seg] + k)
            dve.wait_ge(s["piece_done"], 2 * (BLK[seg] + k) + 2)
            c = slice(k * 512, (k + 1) * 512)
            tt(t.x[:, c], ps[:, n % BANKS, :], t.x[:, c], ALU.add).then_inc(s["u_evac"], 1)

    def ffn_residual(f_, scale):
        dve.wait_ge(s["piece_done"], 2 * (BLK[f"ffn{f_}"] + 3 * FIT))
        for q in range(4):
            c = slice(q * 512, (q + 1) * 512)
            stt(t.x[:, c], ps[:, 4 + q, :], scale, t.x[:, c], ALU.mult, ALU.add).then_inc(s["x_up"], 1)

    def attention(g0, heads, scale, cols, dst):
        def pre(g):
            st = (g % 2) * 8
            src = ps[:, 4 + g % 2, :].rearrange("p (b m) -> p b m", b=TB)
            dve.wait_ge(s["att_scores"], g + 1)
            link(dve.tensor_reduce(t.stat[:, st:st + 2], src, AX, ALU.max))
            ts(t.stat[:, st + 2:st + 4], t.stat[:, st:st + 2], -scale, None,
               ALU.mult).then_inc(s["att_max"], 1)

        def low_out(g):
            lo, hi, high_, low_ = dst(g - g0)
            dve.wait_ge(s["att_high"], g + 1)
            tt(low_, ps[lo:hi, 7, 0:cols], high_.bitcast(F32), ALU.subtract).then_inc(s["att_low"], 1)

        pre(g0)
        for g in range(g0, g0 + heads):
            if g + 1 < g0 + heads:
                pre(g + 1)
            st, buf = (g % 2) * 8, att_buf(t, g)
            dve.wait_ge(s["att_exp"], g + 1)
            link(dve.reciprocal(t.stat[:, st + 6:st + 8], t.stat[:, st + 4:st + 6]))
            for qb in range(TB):
                c = slice(qb * 256, (qb + 1) * 256)
                ins = ts(buf[:, c], buf[:, c], t.stat[:, st + 6 + qb:st + 7 + qb], None, ALU.mult)
            ins.then_inc(s["att_prob"], 1)
            if g > g0:
                low_out(g - 1)
        low_out(g0 + heads - 1)

    for b in range(-AHEAD, 0):
        low(b)
    dve.wait_ge(s["consts_in"], 32)
    logits = par(t, "hg_lb_logits", 0, 16)
    tt(t.lb[:, 0:16], logits, logits, ALU.subtract).then_inc(s["lb_zero"], 1)
    norm("mem")
    dve.wait_ge(s["lb_exp"], 1)
    link(dve.reciprocal(t.lb[:, 32:48], t.lb[:, 16:32]))
    link(tt(t.lb[:, 16:32], t.lb[:, 16:32], t.lb[:, 32:48], ALU.mult))
    link(tt(t.lb[:, 0:16], t.lb[:, 16:32], t.lb[:, 16:32], ALU.subtract))
    link(ts(t.lb[:, 0:16], t.lb[:, 0:16], 0.0, 1.0, ALU.max, ALU.min))
    link(ts(t.lb[:, 16:32], t.lb[:, 0:16], -1.0, 1.0, ALU.mult, ALU.add))
    lows("mem_k", n=4)
    norm("mix0")
    lows("w_in", n=8)
    low_groups("w_in", 8, 4)
    lows("w_in", 24, 4)

    for d in range(2):
        dve.wait_ge(s["hg_sig"], 2 * d + 1)
        fp = t.page[11 + d]
        for h in range(HG_H):
            c = slice(h * T, (h + 1) * T)
            ins = ts(fp[:, c], fp[:, c], t.lb[:, 16 + 8 * d + h:17 + 8 * d + h], t.lb[:, 8 * d + h:8 * d + h + 1],
                     ALU.mult, ALU.add)
        link(ins)
        ts(fp, fp, F_FLOOR, None, ALU.max).then_inc(s["hg_floor"], 1)
        dve.wait_ge(s["hg_sig"], 2 * d + 2)
        kp = t.page[2 + d]
        for h in range(HG_H):
            c = slice(h * T, (h + 1) * T)
            ins = ts(kp[:, c], kp[:, c], t.lb[:, 16 + 8 * d + h:17 + 8 * d + h], None, ALU.mult)
        link(ins)
    low_groups("w_in", 28, 3)
    reset = t.const[:, C_RESET:C_RESET + T]
    for d in range(2):
        dve.wait_ge(s["hg_log"], d + 1)
        for h in range(HG_H):
            c = t.page[11 + d][:, h * T:(h + 1) * T]
            if d:
                c = c[:, ::-1]
            ins = dve.tensor_tensor_scan(c, reset, c, 0.0, ALU.mult, ALU.add)
        link(ins)


    def na_dst(h):
        lo, c = NA_D * (h % 2), slice(h // 2 * T, (h // 2 + 1) * T)
        return lo, lo + NA_D, t.sq_r[lo:lo + NA_D, c], t.h_r[lo:lo + NA_D, c]

    def ca_dst(h):
        c = slice(1024 + h * T, 1024 + (h + 1) * T)
        return 0, P, t.sq_r[:, c], t.h_r[:, c]

    attention(0, NA_H, NA_D ** -0.5, T, na_dst)
    attention(NA_H, CA_H, CA_D ** -0.5, T, ca_dst)
    for seg, gate in (("na_o", 8), ("ca_o", 9)):
        for k in range(4):
            n = SEG[seg] + k
            c = slice(k * 512, (k + 1) * 512)
            if k % 2 == 0:
                low(BLK[seg] + k // 2)
            dve.wait_ge(s["piece_done"], 2 * BLK[seg] + k + 1)
            dst = t.page[10] if seg == "na_o" else t.work
            tt(dst[:, c], ps[:, n % BANKS, :], t.page[gate][:, c], ALU.mult).then_inc(s["u_evac"], 1)
            dve.wait_ge(s["u_evac"], n + 1)
            if seg == "ca_o":
                link(tt(t.page[10][:, c], t.page[10][:, c], t.work[:, c], ALU.add))

    def expo(i):
        level, hh = HG_STEPS[i]
        if level == "same":
            return
        half = slice(hh * 1024, (hh + 1) * 1024)
        eg, eh = hg_buf(t, i)
        cf, cb = t.page[11][:, half], t.page[12][:, half]
        if i >= 2:
            dve.wait_ge(s["hg_sc"], i - 1)
        if level == 128:
            v = lambda ap: ap.rearrange("p (h c m) -> p h c m", h=4, c=NCH)
            cf, cb, eg, eh = v(cf), v(cb), v(eg), v(eh)
            tf = lambda c: cf[:, :, c, CH - 1:CH].broadcast_to([P, 4, CH])
            tb = lambda c: cb[:, :, c, 0:1].broadcast_to([P, 4, CH])
            tt(eg[:, :, 0], tf(0), cf[:, :, 0], ALU.subtract)
            tt(eg[:, :, 1], tf(1), cf[:, :, 1], ALU.subtract)
            tt(eg[:, :, 2], tb(2), cb[:, :, 2], ALU.subtract)
            link(tt(eg[:, :, 3], tb(3), cb[:, :, 3], ALU.subtract))
            tt(eg[:, :, 0], eg[:, :, 0], tf(1), ALU.add)
            tt(eg[:, :, 3], eg[:, :, 3], tb(2), ALU.add)
            tt(eh[:, :, 0], cb[:, :, 0], tb(1), ALU.add)
            dve.tensor_copy(eh[:, :, 1], cb[:, :, 1])
            dve.tensor_copy(eh[:, :, 2], cf[:, :, 2])
            tt(eh[:, :, 3], cf[:, :, 3], tf(2), ALU.add).then_inc(s["hg_expo"], 1)
            return
        v = lambda ap: ap.rearrange("p (g two m) -> p g two m", two=2, m=level)
        n = 1024 // (2 * level)
        cf, cb, eg, eh = v(cf), v(cb), v(eg), v(eh)
        lastf = cf[:, :, 0, level - 1:level].broadcast_to([P, n, level])
        firstb = cb[:, :, 1, 0:1].broadcast_to([P, n, level])
        tt(eg[:, :, 0], lastf, cf[:, :, 0], ALU.subtract)
        tt(eg[:, :, 1], firstb, cb[:, :, 1], ALU.subtract)
        if level == CH:
            dve.tensor_copy(eh[:, :, 0], cb[:, :, 0])
            dve.tensor_copy(eh[:, :, 1], cf[:, :, 1]).then_inc(s["hg_expo"], 1)
        else:
            tt(eh[:, :, 0], cb[:, :, 0], firstb, ALU.subtract)
            tt(eh[:, :, 1], cf[:, :, 1], lastf, ALU.subtract).then_inc(s["hg_expo"], 1)

    def decayed(i):
        level, hh = HG_STEPS[i]
        half = slice(hh * 1024, (hh + 1) * 1024)
        eg, eh = hg_buf(t, i)
        if level == "same":
            dve.wait_ge(s["hg_sc"], i - 1)
            tt(eg, t.page[2][:, half], t.page[3][:, half], ALU.add).then_inc(s["hg_gh"], 1)
            return
        dve.wait_ge(s["hg_exp"], i + 1)
        v = lambda ap: ap.rearrange("p (g two m) -> p g two m", two=2, m=level)
        tt(eh, eh, t.page[0][:, half], ALU.mult)
        eg = v(eg)
        tt(eg[:, :, 0], eg[:, :, 0], v(t.page[2][:, half])[:, :, 0], ALU.mult)
        tt(eg[:, :, 1], eg[:, :, 1], v(t.page[3][:, half])[:, :, 1], ALU.mult).then_inc(s["hg_gh"], 1)

    def keep(i):
        level, hh = HG_STEPS[i]
        half = slice(hh * 1024, (hh + 1) * 1024)
        bank = 4 + 2 * (i % 2)
        dve.wait_ge(s["hg_sc"], i + 1)
        if level in (64, 128):
            dst = t.page[14 if level == 64 else 15][:, half]
            dve.tensor_copy(dst.rearrange("p (a c) -> p a c", a=2), ps[:, bank:bank + 2, :]).then_inc(s["hg_kept"], 1)
        else:
            mask = cst(t, "ident" if level == "same" else f"pair{level}").bitcast(I32)
            dve.copy_predicated(t.page[14][:, half].rearrange("p (n c) -> p n c", n=8),
                                mask.unsqueeze(1).broadcast_to([P, 8, P]),
                                ps[:, bank:bank + 2, :].rearrange("p a (n c) -> p (a n) c", c=P)).then_inc(s["hg_kept"], 1)

    dve.wait_ge(s["hg_silu"], 2)
    expo(0)
    for i in range(len(HG_STEPS)):
        if i + 1 < len(HG_STEPS):
            expo(i + 1)
        decayed(i)
        if i:
            keep(i - 1)
            dve.wait_ge(s["hg_kept"], i)
    keep(len(HG_STEPS) - 1)
    for q in range(4):
        c = slice(q * 512, (q + 1) * 512)
        dve.wait_ge(s["hg_var"], q + 1)
        link(ts(t.page[2][:, c], ps[:, q, :], 1.0 / HG_D, EPS, ALU.mult, ALU.add))
        dve.reciprocal(t.page[2][:, c], t.page[2][:, c]).then_inc(s["hg_varsb"], 1)
    for q in range(4):
        c = slice(q * 512, (q + 1) * 512)
        dve.wait_ge(s["hg_std"], q + 1)
        link(tt(t.page[5][:, c], t.page[5][:, c], t.page[2][:, c], ALU.mult))
        stt(t.page[5][:, c], t.page[5][:, c], par(t, "hg_gnorm"), t.page[4][:, c],
            ALU.mult, ALU.mult).then_inc(s["hg_out"], 1)
    operand_low("hg", t.page[5], t.page_r[6], t.page_r[5])
    for k in range(4):
        n = SEG["hg_o"] + k
        c = slice(k * 512, (k + 1) * 512)
        low(BLK["hg_o"] + k)
        dve.wait_ge(s["piece_done"], 2 * (BLK["hg_o"] + k) + 2)
        tt(t.work[:, c], ps[:, n % BANKS, :], t.page[7][:, c], ALU.mult).then_inc(s["u_evac"], 1)
        dve.wait_ge(s["u_evac"], n + 1)
        tt(t.page[10][:, c], t.page[10][:, c], t.work[:, c], ALU.add).then_inc(s["merged"], 1)
    operand_low("merged", t.page[10], t.page_r[11], t.page_r[10])
    residual("w_out")

    def hidden(fi, st, k, make):
        if not isinstance(st, int) or st >= 2:
            dve.wait_ge(s["piece_done"], st * 6 + (2 * BLK[f"ffn{fi}"] - 2))
        make(t.work[:, k * 512:(k + 1) * 512])
        dve.wait_ge(s["hidden_high"], st + (fi * FIT + 1))
        high_, low_ = hidden_parts(t, k)
        tt(low_, t.work[:, k * 512:(k + 1) * 512], high_.bitcast(F32), ALU.subtract).then_inc(s["hidden_ready"], 1)

    def ffn(fi, seg, step, links):
        b = BLK[seg]
        low(b)
        low(b + 1)
        step(0, 0, 0)

        def two_steps(i):
            for k in range(2):
                r = b + 2 + 3 * k
                blk = [i * 6 + (r + j) if isinstance(i, int) else At(i * 6 + (r + j), r + j) for j in range(3)]
                low(blk[0])
                low(blk[1])
                step(i * 2 + (1 + k), i * 4 + (2 + 2 * k), (1 + k) % 2)
                low(blk[2])

        trips = (FIT - 1) // 2
        two_steps(0)
        last = trips - 1 if fi == N_FFN - 1 else trips
        with dve.Fori(0, last - 1) as i:
            link.loop(i, 2 * links)
            two_steps_from(i, two_steps)
        link.end(last - 1)
        if last < trips:
            two_steps(last)
        low(b + 3 * FIT - 1)

    def two_steps_from(i, two_steps):
        two_steps(i + 1)

    norm("ffn0")

    def conv_step(st, tile, k):
        bank = (SEG["ffn0"] + 2 * k) % BANKS
        dve.wait_ge(s["conv_mid"], st + 1)
        for tap in (0, 2):
            for j in range(4):
                col = tile + (j % 2 + FF // P * (j // 2)) + (PCOL["conv_w"] + 44 * tap)
                w = t.param[:, col:col + 1] if isinstance(col, int) else t.param[:, bass.ds(col, 1)]
                u = ps[:, bank + j // 2, (j % 2) * T:(j % 2 + 1) * T]
                c = t.page[k][:, j * T:(j + 1) * T]
                o, i_ = (c[:, 1:T], u[:, 0:T - 1]) if tap == 0 else (c[:, 0:T - 1], u[:, 1:T])
                ins = stt(o, i_, w, o, ALU.mult, ALU.add)
            link(ins)
        dve.sem_inc(s["conv_done"], 1)
        dve.sem_inc(s["u_evac"], 2)
        dve.wait_ge(s["gelu_ready"], st + 1)
        hidden(0, st, k, lambda out: tt(out, t.page[k][:, 0:512], t.page[k][:, 512:1024],
                                        ALU.mult).then_inc(s["hidden_made"], 1))

    ffn(0, "ffn0", conv_step, 2)
    ffn_residual(0, 1.0)
    norm("fin0")

    def swiglu(fi, seg):
        n0, b = SEG[seg], BLK[seg]

        def step(st, tile, k):
            def make(out):
                dve.wait_ge(s["gate_ready"], st + ((fi - 1) * FIT + 1))
                dve.wait_ge(s["piece_done"], 2 * b + 4 if isinstance(st, int) and st == 0 else st * 6 + (2 * b + 2))
                tt(out, ps[:, (n0 + 2 * k + 1) % BANKS, :], t.work[:, 1024 + k * 512:1536 + k * 512],
                   ALU.mult).then_inc(s["hidden_made"], 1)
                dve.wait_ge(s["hidden_made"], st + (fi * FIT + 1))
                dve.sem_inc(s["u_evac"], 2)

            hidden(fi, st, k, make)

        ffn(fi, seg, step, 0)
        ffn_residual(fi, 0.5)

    norm("ffn1")
    swiglu(1, "ffn1")

    norm("mix1")
    dve.wait_ge(s["norm_out"], KT * (NORM["mix1"] + 1))
    h3, d3 = tiles(t.h[:, :]), tiles(t.page[0])
    tt(d3[:, :, 1:T], h3[:, :, 0:T - 1], h3[:, :, 1:T], ALU.subtract)
    link(ts(d3[:, :, 0:1], h3[:, :, 0:1], -1.0, None, ALU.mult))
    link(dve.memset(t.work[64:P, 0:T], 0.0))
    dve.memset(t.work[0:64, T:2 * T], 0.0).then_inc(s["inner_zero"], 1)
    for step in RW_ORDER:
        if not isinstance(step, int):
            low(BLK["rw_r"] + int(step[1:]))
            continue
        mu = (0, 2, 3, 1, 4, 5)[step]
        for k in range(KT):
            c = slice(k * T, (k + 1) * T)
            ins = stt(t.page[1 + step][:, c], t.page[0][:, c], par(t, "rwkv_mu_2", 8 * mu + k), t.h[:, c],
                      ALU.mult, ALU.add)
            if k % 2:
                ins.then_inc(s["rw_mix"], 1)
        operand_low(f"rw{step}", t.page[1 + step], t.page_r[10 + step], t.page_r[1 + step])
    low(BLK["lora"])
    operand_low("lora", t.work[:, 0:1024], t.sq_r[:, 0:1024], t.work_r[:, 0:1024], 256)
    low(BLK["lora"] + 1)
    low(BLK["lora"] + 2)
    dve.wait_ge(s["u_evac"], SEG["rw_o"])
    for k in range(KT):
        c = slice(k * T, (k + 1) * T)
        ins = ts(t.page[1][:, c], t.page[8][:, c], par(t, "rwkv_k_k_2", k), None, ALU.mult)
        if k % 2:
            ins.then_inc(s["rw_kk"], 1)
    dve.wait_ge(s["lora_out"], 2)
    for k in range(KT):
        c = slice(k * T, (k + 1) * T)
        link(ts(t.page[4][:, c], t.page[12][:, c], 1.0, par(t, "rwkv_k_a_2", k), ALU.subtract, ALU.mult))
        link(stt(t.page[8][:, c], t.page[4][:, c], 1.0, t.page[8][:, c], ALU.add, ALU.mult))
    for q in range(4):
        c = slice(q * 512, (q + 1) * 512)
        dve.wait_ge(s["rw_kkvar"], q + 1)
        link(ts(t.page[2][:, c], t.page[2][:, c], 1e-12, None, ALU.max))
        link(dve.reciprocal(t.page[2][:, c], t.page[2][:, c]))
        link(tt(t.page[1][:, c], t.page[1][:, c], t.page[2][:, c], ALU.mult))
    dve.wait_ge(s["lora_out"], 3)
    for k in range(KT):
        c = slice(k * T, (k + 1) * T)
        ins = stt(t.work[:, c], t.page[7][:, c], par(t, "rwkv_r_k_2", k), t.page[8][:, c], ALU.mult, ALU.mult)
    ins.then_inc(s["rw_bonus_in"], 1)
    for k in range(KT):
        c = slice(k * T, (k + 1) * T)
        ins = dve.tensor_tensor_scan(t.page[2][:, c], reset, t.page[11][:, c], 0.0, ALU.mult, ALU.add)
    link(ins)
    tt(t.page[3], t.page[2], t.page[11], ALU.subtract).then_inc(s["rw_cum"], 1)
    link(tt(t.page[5], t.page[1], t.page[12], ALU.mult))
    for q in range(4):
        c = slice(q * 512, (q + 1) * 512)
        dve.wait_ge(s["rw_bonus_sum"], q + 1)
        ins = tt(t.page[0][:, c], ps[:, q, :], t.page[9][:, c], ALU.mult)
    ins.then_inc(s["rw_act"], 1)
    dve.wait_ge(s["rw_exp"], 1)
    tt(t.page[3], t.page[3], t.page[1], ALU.mult)
    dve.wait_ge(s["rw_exp"], 2)
    tt(t.page[5], t.page[5], t.page[4], ALU.mult)
    tt(t.page[6], t.page[8], t.page[4], ALU.mult)
    dve.wait_ge(s["rw_exp"], 3)
    dve.tensor_copy(t.pc[:, :].rearrange("p (a b) -> p a b", b=1),
                    t.page[10].rearrange("p (a b) -> p a b", b=CH)[:, :, CH - 1:CH])
    tt(t.page[7], t.page[7], t.page[10], ALU.mult).then_inc(s["rw_dec"], 1)

    def matrices(q, j):
        bank = 2 * (q % 2)
        return ps[:, bank:bank + 2, j * 256:(j + 1) * 256].rearrange("p e (b c) -> p e b c", b=2)

    def view(ap):
        return ap.rearrange("p (e b c) -> p e b c", e=2, b=2)

    def mask(name):
        return cst(t, name).unsqueeze(1).unsqueeze(1).broadcast_to([P, 2, 2, P])

    def chunk_matrices(c):
        buf, xt = inv_buf(t, c), inv_xt(t, c)
        q = 3 * c
        dve.wait_ge(s["rw_m"], q + 1)
        link(tt(view(buf.lt), matrices(q, 0), mask("strict"), ALU.mult))
        link(tt(view(buf.x), matrices(q, 1), mask("lower1"), ALU.mult))
        tt(view(buf.x), mask("ident"), view(buf.x), ALU.subtract)
        link(tt(view(xt), view(buf.lt), mask("upper1"), ALU.mult))
        tt(view(xt), mask("ident"), view(xt), ALU.subtract).then_inc(s["rw_m_sb"], 1)
        dve.wait_ge(s["rw_m"], q + 2)
        tt(view(stack(RW_MT(t), c)), matrices(q + 1, 0), mask("strict"), ALU.mult)
        tt(view(stack(RW_RBT(t), c)), matrices(q + 1, 1), mask("incl"), ALU.mult).then_inc(s["rw_m_sb"], 1)
        dve.wait_ge(s["rw_m"], q + 3)
        tt(view(stack(RW_RKT(t), c)), matrices(q + 2, 0), mask("incl"), ALU.mult).then_inc(s["rw_m_sb"], 1)

    dve.wait_ge(s["rw_t_sb"], 12)
    for c0 in range(0, KT, 2):
        chunk_matrices(c0)
        chunk_matrices(c0 + 1)
        for lv in range(len(LEVELS) - 1):
            for c in (c0, c0 + 1):
                buf, xt = inv_buf(t, c), inv_xt(t, c)
                dve.wait_ge(s["rw_z"], inv_at(c, lv) + 1)
                if lv < len(LEVELS) - 2:
                    tt(buf.x, buf.x, ps[:, 4 + 2 * (c % 2), :], ALU.subtract)
                tt(xt, xt, ps[:, 5 + 2 * (c % 2), :], ALU.subtract).then_inc(s["rw_z_sb"], 1)

    dve.memset(t.page[5][:, 0:1024], 0.0)
    dve.memset(t.page[6][:, 0:1024], 0.0).then_inc(s["rw_zero"], 1)
    state, delta = t.page[6][:, 0:1024], t.page[6][:, 1024:2048]
    for n_ in range(NCH):
        po = slice(CH * (n_ % 2), CH * (n_ % 2 + 1))
        dve.wait_ge(s["rw_rhs"], n_ + 1)
        ts(t.page[5][po, 0:512], ps[po, 0, :], -1.0, None, ALU.mult).then_inc(s["rw_rhs_sb"], 1)
        dve.wait_ge(s["rw_u"], n_ + 1)
        dve.tensor_copy(t.page[5][po, 1024:1536], ps[po, 2, :]).then_inc(s["rw_u_sb"], 1)
        if n_ == NCH - 1:
            break
        dve.wait_ge(s["rw_ds"], n_ + 1)
        blocks = lambda ap: ap.rearrange("p (c i) -> p c i", i=P)
        link(tt(blocks(delta), ps[:, 0:2, :].rearrange("p a (c i) -> p (a c) i", i=P),
                cst(t, "head_ones").unsqueeze(1).broadcast_to([P, KT, P]), ALU.mult))
        link(tt(state, state, delta, ALU.add))
        pc = t.pc[:, :].rearrange("p (c n) -> p c n", n=NCH)[:, :, n_:n_ + 1].broadcast_to([P, KT, P])
        tt(blocks(state), blocks(state), pc, ALU.mult).then_inc(s["rw_s"], 1)
    for q in range(4):
        c = slice(q * 512, (q + 1) * 512)
        dve.wait_ge(s["rw_mean"], q + 1)
        stt(t.page[8][:, c], ps[:, q, :], -1.0 / RW_D, t.page[8][:, c], ALU.mult, ALU.add).then_inc(s["rw_cent"], 1)
    for q in range(4):
        c = slice(q * 512, (q + 1) * 512)
        dve.wait_ge(s["rw_var"], q + 1)
        link(ts(t.page[2][:, c], ps[:, q, :], 1.0 / RW_D, GN_EPS, ALU.mult, ALU.add))
        dve.reciprocal(t.page[2][:, c], t.page[2][:, c]).then_inc(s["rw_varsb"], 1)
    for q in range(4):
        c = slice(q * 512, (q + 1) * 512)
        dve.wait_ge(s["rw_std"], q + 1)
        link(tt(t.page[8][:, c], t.page[8][:, c], t.page[2][:, c], ALU.mult))
        for k in (2 * q, 2 * q + 1):
            ck = slice(k * T, (k + 1) * T)
            ins = ts(t.page[8][:, ck], t.page[8][:, ck], par(t, "rwkv_ln_w_2", k), par(t, "rwkv_ln_b_2", k),
                     ALU.mult, ALU.add)
        link(ins)
        link(tt(t.page[8][:, c], t.page[8][:, c], t.page[0][:, c], ALU.add))
        tt(t.page[7][:, c], t.page[8][:, c], t.page[13][:, c], ALU.mult).then_inc(s["rw_out"], 1)
    operand_low("rw_o", t.page[7], t.page_r[10], t.page_r[7])
    residual("rw_o")

    norm("mem2")
    lows("mem2_k")
    lows("mem2_v")

    def memory_attention(i):
        norm(f"x{i}")
        lows(f"xq{i}")
        attention(NA_H + CA_H + XA_H * i, XA_H, XA_D ** -0.5, 512,
                  lambda h: (0, P, t.page_r[2][:, h * 512:(h + 1) * 512], t.page_r[1][:, h * 512:(h + 1) * 512]))
        residual(f"xo{i}")

    memory_attention(0)
    norm("ffn2")
    swiglu(2, "ffn2")
    norm("ffn3")
    swiglu(3, "ffn3")

    norm("mix2")
    dve.wait_ge(s["rows_in"], 48)
    cols = lambda ap: ap.rearrange("p (g c) -> p g c", g=GM_G)
    tt(cols(t.page[4]), cols(t.page[9]), cst(t, "causal").unsqueeze(1).broadcast_to([P, GM_G, P]),
       ALU.mult).then_inc(s["gm_mask"], 1)
    low_groups("gm_u", 0, 2)
    low_groups("gm_v", 0, 2)
    dve.wait_ge(s["gm_vnorm"], 1)
    link(ts(t.stat[:, 18:20], t.stat[:, 16:18], 1.0 / GM_W, EPS, ALU.mult, ALU.add))
    dve.reciprocal(t.stat[:, 18:20], t.stat[:, 18:20]).then_inc(s["gm_vvar"], 1)
    dve.wait_ge(s["gm_vstd"], 1)
    for b in range(TB):
        ins = stt(t.page[2 + b], t.page[2 + b], t.stat[:, 18 + b:19 + b], t.page[6], ALU.mult, ALU.mult)
    ins.then_inc(s["gm_vout"], 1)
    for q in range(8):
        dve.wait_ge(s["gm_mix"], q + 1)
        tmp = t.work[:, (q % 2) * 512:(q % 2 + 1) * 512]
        bias = t.page[5][:, q * 256:(q + 1) * 256].rearrange("p (g c) -> p g c", g=2)
        ins = tt(tmp.rearrange("p (g b c) -> p g b c", g=2, b=2),
                 ps[:, 4 + q % 2, :].rearrange("p (g b c) -> p g b c", g=2, b=2),
                 bias.unsqueeze(2).broadcast_to([P, 2, 2, P]), ALU.add)
        link(ins)
        tt(t.pages[:, 7 * FP + q * 512:7 * FP + (q + 1) * 512], tmp, t.pages[:, q * 512:(q + 1) * 512],
           ALU.mult).then_inc(s["gm_mixed"], 1)
    for page in range(2):
        operand_low(f"gm{page}", t.page[7 + page], t.page_r[10 + page], t.page_r[7 + page])
    for q in range(4):
        c = slice(q * 512, (q + 1) * 512)
        lows("gm_o", 2 * q, 2)
        dve.wait_ge(s["piece_done"], 2 * (BLK["gm_o"] + 2 * q) + 4)
        tt(t.x[:, c], ps[:, (SEG["gm_o"] + q) % BANKS, :], t.x[:, c], ALU.add).then_inc(s["u_evac"], 1)
    memory_attention(1)
    norm("ffn4")
    swiglu(4, "ffn4")
    norm("fin2")


def pool_program(pool, t, s):
    pool.memset(t.zrow[:], 0.0).then_inc(s["zero_row"], 1)
    pool.wait_ge(s["consts_in"], 32)
    pool.wait_ge(s["bias_in"], 16 * 4 * NA_H)
    for page in (14, 15):
        table = t.page[page].rearrange("p (n c) -> p n c", c=NA_COLS)
        window = t.const[:, C_WINDOW:C_WINDOW + NA_COLS].unsqueeze(1).broadcast_to([P, 32, NA_COLS])
        pool.tensor_tensor(table, table, window, ALU.add).then_inc(s["pool_chain"], 1)
        pool.wait_ge(s["pool_chain"], page - 13)
        pool.tensor_scalar(t.page[page], t.page[page], NA_D ** 0.5, None, ALU.mult).then_inc(s["bias_ready"], 1)
    for c0 in range(0, KT, 2):
        for lv in range(len(LEVELS) - 1):
            for c in (c0, c0 + 1):
                q, buf = inv_at(c, lv), inv_buf(t, c)
                if lv == 0:
                    pool.wait_ge(s["rw_m_sb"], 3 * c + 1)
                else:
                    pool.wait_ge(s["rw_y"], q - 1)
                m = LEVELS[len(LEVELS) - 2 - lv]
                v = lambda ap: ap.rearrange("p (n c) -> p n c", c=P)
                pool.tensor_tensor(v(buf.lm), v(buf.lt), cst(t, f"upper{m}").unsqueeze(1).broadcast_to([P, 4, P]),
                                   ALU.mult).then_inc(s["rw_lm"], 1)


def constants():
    i = np.arange(P)
    r, c = i[:, None], i[None, :]
    out = np.zeros((P, N_CONST), np.float32)

    def put(name, mask):
        out[:, CCOL[name]:CCOL[name] + P] = mask

    put("ident", r == c)
    put("flip", r + c == P - 1)
    put("ones", np.ones((P, P)))
    put("head_ones", r // RW_D == c // RW_D)
    for m in LEVELS:
        pair = (r // (2 * m) == c // (2 * m)) & (r // m != c // m)
        put(f"pair{m}", pair)
        put(f"upper{m}", pair & (r < c))
    put("lower1", (r // 2 == c // 2) & (r > c))
    put("strict", (r // CH == c // CH) & (r < c))
    put("incl", (r // CH == c // CH) & (r <= c))
    put("causal", r <= c)
    out[:, C_RESET:C_RESET + T] = (np.arange(T) % CH != 0)[None, :]
    q, k = (P - 1 - np.arange(P))[:, None] % NA_COLS, np.arange(NA_COLS)[None, :]
    start = np.clip(q - NA_WIN // 2, 0, NA_COLS - NA_WIN)
    out[:, C_WINDOW:] = np.where((k >= start) & (k < start + NA_WIN), 0.0, NEG)
    return out


def feature_major(x):
    n, d = x.shape
    return np.ascontiguousarray(x.T.reshape(d // P, P, n).transpose(1, 0, 2).reshape(P, -1))


def k_blocks(w, cols=256):
    k, n = w.shape
    b = w.reshape(k // P, P, n // cols, cols).transpose(2, 1, 0, 3).reshape(n // cols, P, -1)
    return [np.pad(x, ((0, 0), (0, 2048 - x.shape[1]))) for x in b]


def half_blocks(w):
    b = w.reshape(4, P, -1, 2, 256).transpose(2, 1, 3, 0, 4)
    return list(b.reshape(b.shape[0], P, 2048))


def ffn_blocks(up, down):
    a, b = k_blocks(up[:, :FF]), k_blocks(up[:, FF:])
    c = list(down.reshape(FIT, 2, P, D).transpose(0, 2, 1, 3).reshape(FIT, P, 2 * D))
    blocks = [a[0], b[0]]
    for k in range(1, FIT):
        blocks += [a[k], b[k], c[k - 1]]
    return blocks + [c[-1]]


def weight_stream(i):
    rkv = i["rwkv_w_rkv_2"][0]
    w1, a1, g1 = i["rwkv_w1_2"][0], i["rwkv_a1_2"][0], i["rwkv_g1_2"][0]
    w2, a2, g2 = i["rwkv_w2_2"][0], i["rwkv_a2_2"][0], i["rwkv_g2_2"][0]
    lora_a = k_blocks(np.concatenate([w1, a1, g1[:, :P]], 1))
    g1p = np.pad(g1[:, P:], ((0, 0), (0, 2 * P - g1.shape[1])))
    lora_b = [np.concatenate([g1p.reshape(KT, P, P).transpose(1, 0, 2).reshape(P, D), np.concatenate([w2, a2], 0)], 1)]
    g2p = np.pad(g2, ((0, 2 * P - g2.shape[0]), (0, 0)))
    lora_c = [np.concatenate([g2p[:P], g2p[P:]], 1)]
    gm_o = k_blocks(i["gmlp_w_o_2"][0][:D]), k_blocks(i["gmlp_w_o_2"][0][D:])
    kv, kv2, uv = i["w_mem_kv"][0], i["mem_w_kv_2"], i["gmlp_w_uv_2"][0]
    up1, down1, up2, down2 = (i[n] for n in ("ffn1_w_in_2", "ffn1_w_out_2", "ffn2_w_in_2", "ffn2_w_out_2"))
    parts = {
        "mem_k": k_blocks(kv[:, :512]), "mem_v": k_blocks(kv[:, 512:]), "w_in": k_blocks(i["w_in"][0]),
        "na_o": half_blocks(i["w_na_o"][0]), "ca_o": half_blocks(i["w_ca_o"][0]), "hg_o": k_blocks(i["w_hg_o"][0]),
        "w_out": k_blocks(i["w_out"][0]), "ffn0": ffn_blocks(i["w_up"][0], i["w_down"][0]),
        "ffn1": ffn_blocks(up1[0], down1[0]), "ffn2": ffn_blocks(up2[0], down2[0]),
        "ffn3": ffn_blocks(up1[1], down1[1]), "ffn4": ffn_blocks(up2[1], down2[1]),
        "rw_r": k_blocks(rkv[:, :D]), "rw_k": k_blocks(rkv[:, D:2 * D]), "rw_v": k_blocks(rkv[:, 2 * D:]),
        "lora": lora_a + lora_b + lora_c, "rw_o": k_blocks(i["rwkv_w_o_2"][0]),
        "mem2_k": k_blocks(kv2[:, :D]), "mem2_v": k_blocks(kv2[:, D:]),
        "xq0": k_blocks(i["xattn_wq_2"][0]), "xo0": k_blocks(i["xattn_wo_2"][0]),
        "xq1": k_blocks(i["xattn_wq_2"][1]), "xo1": k_blocks(i["xattn_wo_2"][1]),
        "gm_u": k_blocks(uv[:, :GM_W]), "gm_v": k_blocks(uv[:, GM_W:]),
        "gm_o": [x for pair in zip(*gm_o) for x in pair],
    }
    blocks = []
    for name, _, n in SEGMENTS:
        assert len(parts[name]) == n, name
        blocks += parts[name]
    return np.stack(blocks)


def param_table(i):
    cols = [i[name].reshape(-1, P).T for name, _ in PARAMS]
    assert [c.shape[1] for c in cols] == [n for _, n in PARAMS]
    return np.concatenate(cols, 1)


def kernel(**inputs):
    import concourse.bacc as bacc
    from concourse.bass_utils import run_bass_kernel_spmd

    i = {k: np.asarray(v) for k, v in inputs.items()}
    arrays = {
        "in_stream": weight_stream(i), "in_params": param_table(i),
        "in_consts": constants(), "in_x": feature_major(i["x"][0]), "in_mem": feature_major(i["mem"][0]),
        "in_mem2": feature_major(i["mem_2"][0]), "in_rpb": i["na_rpb"][0], "in_gmlp_b": i["gmlp_b_s_2"][0],
        "in_gmlp_gain": i["gmlp_v_norm_2"], "in_gmlp_w": i["gmlp_w_s_2"][0].transpose(2, 0, 1).reshape(P, -1),
    }
    arrays = {k: np.ascontiguousarray(v) for k, v in arrays.items()}
    nc = bacc.Bacc("TRN2", target_bir_lowering=False, num_devices=1, dynamic_dma_scratch_size=1024)
    ap = {k: nc.dram_tensor(k, v.shape, F32, kind="ExternalInput").ap() for k, v in arrays.items()}
    out = nc.dram_tensor("out", (P, FP), F32, kind="ExternalOutput").ap()
    rpb = ap["in_rpb"]
    n_dr, n_dc = rpb.shape[1:]
    kh = T // NA_COLS

    def bias_window(h, row):
        at = h * n_dr * n_dc + (n_dr // 2 - row) * n_dc + n_dc // 2 - (NA_COLS - 1)
        return bass.AP(tensor=rpb.tensor, offset=at, ap=[[1, NA_COLS], [n_dc, kh], [1, NA_COLS]])

    a = Bag()
    a.stream, a.params, a.consts, a.mix_weights = (ap[f"in_{n}"] for n in ("stream", "params", "consts", "gmlp_w"))
    a.x_t, a.mem_t, a.mem2_t, a.bias_window, a.out = ap["in_x"], ap["in_mem"], ap["in_mem2"], bias_window, out
    a.bias_rows = ap["in_gmlp_b"].rearrange("(o g) c -> o (g c)", o=1).broadcast_to([P, GM_W])
    a.gain_rows = ap["in_gmlp_gain"].broadcast_to([P, GM_W])
    build(nc, a)
    got = run_bass_kernel_spmd(nc, [arrays], core_ids=[0]).results[0]["out"]
    return got.reshape(P, KT, T).transpose(2, 1, 0).reshape(1, T, D)
```

```python
from contextlib import ExitStack

import numpy as np

import concourse.bass as bass
from concourse import mybir

F32 = mybir.dt.float32
F32R = mybir.dt.float32r
I32 = mybir.dt.int32
ALU = mybir.AluOpType
ACT = mybir.ActivationFunctionType
AX = mybir.AxisListType.X

P = 128
D = 1024
KT = D // P
T = 256
TB = T // P
FF = 2816
FIT = FF // 256
FP = KT * T
HG_H, HG_D = 8, 128
NA_H, NA_D, NA_COLS, NA_WIN = 8, 64, 64, 16
CA_H, CA_D = 4, 128
XA_H, XA_D = 4, 256
RW_H, RW_D, CH = 16, 64, 64
NCH = T // CH
GM_W, GM_G = 2048, 16
EPS = 1e-6
GN_EPS = 64e-5
F_FLOOR = 1e-12
NEG = -1e30
LEVELS = (32, 16, 8, 4, 2, 1)
BANKS = 4
RAW_SLOTS = 2
PIECE_SLOTS = 4
N_FFN = 5
AHEAD = 2
N_PAGES = 16
COL_EPS, COL_GN_EPS = 40, 41

PARAMS = [
    ("norm_mix", 8), ("norm_ffn", 8), ("norm_final", 8), ("mem_norm", 8), ("hg_lb_logits", 16),
    ("hg_gnorm", 1), ("conv_w", 132), ("conv_b", 44), ("mem_norm_2", 8), ("ffn1_norm_2", 16),
    ("mix_norm_2", 16), ("xattn_norm_2", 16), ("ffn2_norm_2", 16), ("final_norm_2", 8),
    ("rwkv_mu_2", 48), ("rwkv_w0_2", 8), ("rwkv_a0_2", 8), ("rwkv_k_k_2", 8), ("rwkv_k_a_2", 8),
    ("rwkv_r_k_2", 8), ("rwkv_ln_w_2", 8), ("rwkv_ln_b_2", 8),
]
PCOL = {}
_at = 0
for _name, _n in PARAMS:
    PCOL[_name] = _at
    _at += _n
N_PARAM = _at

CONSTS = ["ident", "flip", "ones", "head_ones"] + [f"pair{m}" for m in LEVELS] + [f"upper{m}" for m in LEVELS] + [
    "lower1", "strict", "incl", "causal"]
CCOL = {name: 128 * i for i, name in enumerate(CONSTS)}
C_RESET = 128 * len(CONSTS)
C_WINDOW = C_RESET + T
N_CONST = C_WINDOW + NA_COLS

SEGMENTS = [
    ("mem_k", 2, 2), ("mem_v", 2, 2), ("w_in", 40, 40), ("na_o", 4, 2), ("ca_o", 4, 2), ("hg_o", 4, 4),
    ("w_out", 4, 4), ("ffn0", 22, 33), ("ffn1", 22, 33), ("rw_r", 4, 4), ("rw_k", 4, 4), ("rw_v", 4, 4),
    ("lora", 0, 3), ("rw_o", 4, 4), ("mem2_k", 4, 4), ("mem2_v", 4, 4), ("xq0", 4, 4), ("xo0", 4, 4),
    ("ffn2", 22, 33), ("ffn3", 22, 33), ("gm_u", 8, 8), ("gm_v", 8, 8), ("gm_o", 4, 8),
    ("xq1", 4, 4), ("xo1", 4, 4), ("ffn4", 22, 33),
]
SEG, BLK = {}, {}
_seg = _blk = 0
for _name, _banks, _blocks in SEGMENTS:
    SEG[_name], BLK[_name] = _seg, _blk
    _seg += _banks
    _blk += _blocks
N_BLK = _blk

OPERAND = {n: i for i, n in enumerate(
    ["mem", "mix0", "hg", "merged", "ffn0", "ffn1", "rw0", "rw1", "rw2", "rw3", "rw4", "rw5", "lora", "rw_o", "mem2",
     "x0", "ffn2", "ffn3", "mix2", "gm0", "gm1", "x1", "ffn4"])}
RW_ORDER = [0, 1, "b0", "b1", 2, "b2", "b3", 3, "b4", "b5", 4, "b6", "b7", 5, "b8", "b9", "b10", "b11"]
NORM = {n: i for i, n in enumerate(
    ["mem", "mix0", "ffn0", "fin0", "ffn1", "mix1", "mem2", "x0", "ffn2", "ffn3", "mix2", "x1", "ffn4", "fin2"])}
LATE = ("ffn0", "ffn1", "x0", "ffn2", "ffn3", "x1", "ffn4")
PLAIN = {n: i for i, n in enumerate(n for n in NORM if n not in LATE)}
SEM_NAMES = """
consts_in x_in mem_in mem2_in bias_in rows_in out_done piece_done high_done low_done op_high op_low u_evac
att_low zero_row inner_zero hidden_made hidden_high att_high att_gates norm_sq norm_part acc_done norm_sum
norm_var norm_std norm_out x_up gate_ready gate_scaled hidden_ready conv_mid gelu_ready dve_chain pool_chain
att_scores att_max att_exp att_prob att_turned att_turned_sb att_out lb_zero lb_exp bias_ready conv_done
hg_sig hg_silu hg_floor hg_log rw_kk rw_zero lora_mm gm_vvar hg_expo hg_exp hg_gh hg_keys hg_sc hg_kept hg_av
hg_o hg_sq hg_var hg_varsb hg_std hg_out merged lora_mid lora_out rw_mix rw_act rw_kk2 rw_kksum rw_kkfloor
rw_kkln rw_kkvar rw_bonus_in rw_bonus_sum rw_cum rw_exp rw_dec rw_t rw_t_sb rw_m rw_m_sb rw_lm rw_y rw_y_sb
rw_z rw_z_sb rw_rhs rw_rhs_sb rw_u rw_u_sb rw_ds rw_s rw_yt rw_yt_sb rw_mean rw_cent rw_sq rw_var rw_varsb
rw_std rw_out gm_vnorm gm_vstd gm_vout gm_mask gm_mix gm_mixed
""".split()


class Bag:
    pass


class Link:

    def __init__(self, eng, sem):
        self.eng, self.sem, self.n, self.iv = eng, sem, 0, 0

    def __call__(self, ins):
        self.n += 1
        ins.then_inc(self.sem, 1)
        self.eng.wait_ge(self.sem, self.n + self.iv)

    def loop(self, i, per):
        self.iv, self.start, self.per = i * per, self.n, per

    def end(self, trips):
        assert self.n - self.start == self.per, (self.n - self.start, self.per)
        self.n, self.iv = self.start + trips * self.per, 0


def build(nc, a):
    ctx = ExitStack()
    with ctx:
        def sb(name, shape):
            return ctx.enter_context(nc.sbuf_tensor(name, shape, F32))

        t = Bag()
        def both(name, pages=1):
            at = -(-nc.sbuf_base // 32) * 32
            plain = sb(name, [P, pages * FP])
            split = [nc.alloc_sbuf_tensor_at(f"{name}_r{i}", [P, FP], F32R, offset=at + 4 * FP * i)[:, :]
                     for i in range(pages)]
            return plain, split

        t.x = sb("x", [P, FP])
        t.h, (t.h_r,) = both("h")
        t.sq, (t.sq_r,) = both("sq")
        t.work, (t.work_r,) = both("work")
        t.raw = [sb(f"raw{i}", [P, 2048]) for i in range(RAW_SLOTS)]
        t.wh = [ctx.enter_context(nc.sbuf_tensor(f"wh{i}", [P, 1024], F32R)) for i in range(PIECE_SLOTS)]
        t.wl = [ctx.enter_context(nc.sbuf_tensor(f"wl{i}", [P, 1024], F32R)) for i in range(PIECE_SLOTS)]
        t.pages, t.page_r = both("pages", N_PAGES)
        t.page = [t.pages[:, i * FP:(i + 1) * FP] for i in range(N_PAGES)]
        t.const = sb("const", [P, N_CONST])
        t.param = sb("param", [P, N_PARAM])
        t.rstd = sb("rstd", [P, T])
        t.stat = sb("stat", [P, 48])
        t.lb = sb("lb", [P, 48])
        t.pc = sb("pc", [P, KT * NCH])
        t.zrow = ctx.enter_context(nc.sbuf_tensor("zrow", [P, P], mybir.dt.bfloat16))
        t.ps = ctx.enter_context(nc.psum_tensor("ps", [P, 8, 512], F32))
        s = {n: ctx.enter_context(nc.semaphore(n)) for n in SEM_NAMES}
        s["raw_in"] = [ctx.enter_context(nc.semaphore(f"raw_in{i}")) for i in range(RAW_SLOTS)]
        block = ctx.enter_context(nc.Block())

        @block.sync
        def _(sp):
            load_program(sp, a, t, s)

        @block.tensor
        def _(pe):
            tensor_program(pe, t, s)

        @block.scalar
        def _(act):
            scalar_program(act, a, t, s)

        @block.vector
        def _(dve):
            vector_program(dve, t, s)

        @block.gpsimd
        def _(pool):
            pool_program(pool, t, s)


def cst(t, name, rows=P):
    return t.const[0:rows, CCOL[name]:CCOL[name] + 128]


def par(t, name, i=0, n=1):
    c = PCOL[name] + i
    return t.param[:, c:c + n]


def tiles(ap, n=KT):
    return ap.rearrange("p (n t) -> p n t", n=n)


def load_program(sp, a, t, s):
    def load(n, slot, first=False):
        if not first:
            sp.wait_ge(s["low_done"], n * 2 - 2)
        src = a.stream[n] if isinstance(n, int) else a.stream[bass.ds(n, 1)].rearrange("a p n -> p (a n)")
        sp.dma_start(t.raw[slot][:], src).then_inc(s["raw_in"][slot], 16)

    sp.dma_start(t.page[0], a.mem_t).then_inc(s["mem_in"], 16)
    sp.dma_start(t.param[:], a.params).then_inc(s["consts_in"], 16)
    sp.dma_start(t.const[:], a.consts).then_inc(s["consts_in"], 16)
    for n in range(RAW_SLOTS):
        load(n, n, first=True)
    sp.dma_start(t.x[:], a.x_t).then_inc(s["x_in"], 16)
    for row in range(T // NA_COLS):
        part = slice(NA_COLS * (1 - row % 2), NA_COLS * (2 - row % 2))
        dst = t.page[14 + row // 2][part, :].rearrange("p (h r c) -> p h r c", h=NA_H, r=4)
        for h in range(NA_H):
            sp.dma_start(dst[:, h], a.bias_window(h, row)).then_inc(s["bias_in"], 16)
    rounds = N_BLK // RAW_SLOTS
    with sp.Fori(1, rounds) as i:
        for k in range(RAW_SLOTS):
            load(i * RAW_SLOTS + k, k)
    for n in range(rounds * RAW_SLOTS, N_BLK):
        load(n, n % RAW_SLOTS)


def tensor_program(pe, t, s):
    ps = t.ps

    def split_mm(out, w, act, start, stop, weights_move=False):
        for q, (x, y) in enumerate(((0, 0), (0, 1), (1, 0))):
            left, right = (act[y], w[x]) if weights_move else (w[x], act[y])
            mm = pe.matmul(out, left, right, start=start and q == 0, stop=stop and q == 2, skip_group_check=True)
        return mm

    def piece(b, hf):
        pe.wait_ge(s["low_done"], b * 2 + (hf + 1))
        i = (2 * block0(b) + hf) % PIECE_SLOTS
        return t.wh[i], t.wl[i]

    def bank_free(n):
        if not isinstance(n, int) or n >= BANKS:
            pe.wait_ge(s["u_evac"], n - (BANKS - 1))

    def up_block(n, bank, b, act, name=None):
        bank_free(n)
        for hf in range(2):
            w = piece(b, hf)
            for kk in range(4):
                k = 4 * hf + kk
                operand_part(name, k)
                for j in range(2):
                    cols = slice(kk * 256 + j * P, kk * 256 + (j + 1) * P)
                    mm = split_mm(ps[:, bank, j * T:(j + 1) * T], [x[:, cols] for x in w],
                                  [x[:, k * T:(k + 1) * T] for x in act],
                                  start=hf == 0 and j == 0 and kk == 0, stop=k == KT - 1)
            mm.then_inc(s["piece_done"], 1)

    def token_block(n, bank, b, act, name=None):
        bank_free(n)
        for hf in range(2):
            w = piece(b, hf)
            for kk in range(4):
                k = 4 * hf + kk
                operand_part(name, k)
                for tb in range(TB):
                    mm = split_mm(ps[:, bank, tb * 256:(tb + 1) * 256], [x[:, kk * 256:(kk + 1) * 256] for x in w],
                                  [x[:, k * T + tb * P:k * T + (tb + 1) * P] for x in act],
                                  start=hf == 0 and tb == 0 and kk == 0, stop=k == KT - 1, weights_move=True)
            mm.then_inc(s["piece_done"], 1)

    def half_project(seg, act, first):
        for n in range(first, first + 2):
            bank_free(SEG[seg] + n)
            w = piece(BLK[seg] + n // 2, n % 2)
            for j in range(2):
                for k in range(4):
                    mm = split_mm(ps[:, (SEG[seg] + n) % BANKS, j * T:(j + 1) * T],
                                  [x[:, k * 256 + j * P:k * 256 + (j + 1) * P] for x in w],
                                  [x[:, k * T:(k + 1) * T] for x in act], start=j == 0 and k == 0, stop=k == 3)
            mm.then_inc(s["piece_done"], 1)

    def project(seg, act, first=0, n=4, groups=1, token=False, name=None):
        n0, b0 = SEG[seg] + first, BLK[seg] + first
        body = token_block if token else up_block
        if groups > 1:
            with pe.Fori(0, groups) as i:
                for k in range(n):
                    body(i * n + (n0 + k), (n0 + k) % BANKS, At(i * n + (b0 + k), b0 + k), act)
            return
        for k in range(n):
            body(n0 + k, (n0 + k) % BANKS, b0 + k, act, None if k else name)

    def operand_part(name, k):
        if name and k % 2 == 0:
            pe.wait_ge(s["op_low"], 4 * OPERAND[name] + (k // 2 + 1))

    def operand(name):
        pe.wait_ge(s["op_low"], 4 * (OPERAND[name] + 1))

    def norm_sum(name):
        for hf in range(2):
            pe.wait_ge(s["norm_part"], 2 * NORM[name] + hf + 1)
            mm = pe.matmul(ps[:, 4, 0:T], cst(t, "ones"), t.work[:, (2 + hf) * T:(3 + hf) * T], start=hf == 0, stop=hf == 1)
        mm.then_inc(s["norm_sum"], 1)

    norm_parts = (t.sq_r, t.h_r)

    def ffn(f, seg, name):
        n, b = SEG[seg], BLK[seg]

        def down(step, blk, buf):
            pe.wait_ge(s["hidden_ready"], step + (f * FIT + 1))
            hid = hidden_parts(t, buf)
            for k in range(2):
                w = piece(blk, k)
                for j in range(KT):
                    mm = split_mm(ps[:, 4 + j // 2, (j % 2) * T:(j % 2 + 1) * T], [x[:, j * P:(j + 1) * P] for x in w],
                                  [x[:, k * T:(k + 1) * T] for x in hid], start=False, stop=False)
                mm.then_inc(s["piece_done"], 1)

        up_block(n, n % BANKS, b, norm_parts, name)
        norm_sum(name)
        up_block(n + 1, (n + 1) % BANKS, b + 1, norm_parts)
        pe.wait_ge(s["norm_var"], NORM[name] + 1)
        if f == 0:
            pe.wait_ge(s["zero_row"], 1)
        for bank in range(4, 8):
            pe.matmul(ps[:, bank, :], t.zrow[:, :], t.zrow[:, 0:1].broadcast_to([P, 512]), start=True, stop=True,
                      skip_group_check=True)
        with pe.Fori(0, (FIT - 1) // 2) as i:
            for k in range(2):
                r = b + 2 + 3 * k
                for j in range(2):
                    m = n + 2 + 2 * k + j
                    up_block(i * 4 + m, m % BANKS, At(i * 6 + (r + j), r + j), norm_parts)
                down(i * 2 + k, At(i * 6 + (r + 2), r + 2), k)
        last = b + 3 * FIT - 1
        pe.wait_ge(s["hidden_ready"], (f + 1) * FIT)
        parts, hid = (piece(last, 0), piece(last, 1)), hidden_parts(t, 0)
        for j in range(KT):
            for k in range(2):
                mm = split_mm(ps[:, 4 + j // 2, (j % 2) * T:(j % 2 + 1) * T], [x[:, j * P:(j + 1) * P] for x in parts[k]],
                              [x[:, k * T:(k + 1) * T] for x in hid], start=False, stop=False)
            if j % 2:
                mm.then_inc(s["acc_done"], 1)
        pe.wait_ge(s["acc_done"], 4 * (f + 1))
        pe.sem_inc(s["piece_done"], 2)

    def attention(g0, heads, q, k, v, kcs, dcs, dst_rows, bias=None):
        def scores(g):
            h = g - g0
            if g >= 2:
                pe.wait_ge(s["att_exp"], g - 1)
            for qb in range(TB):
                if bias:
                    pe.matmul(ps[:, 4 + g % 2, qb * 256:(qb + 1) * 256], cst(t, "flip"), bias(h, qb),
                              start=True, stop=False, skip_group_check=True)
                for c in range(kcs):
                    mm = pe.matmul(ps[:, 4 + g % 2, qb * 256:(qb + 1) * 256], q(h, c)[:, qb * P:(qb + 1) * P],
                                   k(h, c), start=c == 0 and not bias, stop=c == kcs - 1, skip_group_check=bool(bias))
            mm.then_inc(s["att_scores"], 1)

        def turn(g):
            pe.wait_ge(s["att_prob"], g + 1)
            if g >= 1:
                pe.wait_ge(s["att_turned_sb"], g)
            for qb in range(TB):
                for mb in range(TB):
                    mm = pe.transpose(ps[:, 6, mb * 256 + qb * P:mb * 256 + (qb + 1) * P],
                                      att_buf(t, g)[:, qb * 256 + mb * P:qb * 256 + (mb + 1) * P], cst(t, "ident"))
            mm.then_inc(s["att_turned"], 1)

        def mix(g):
            h = g - g0
            pe.wait_ge(s["att_turned_sb"], g + 1)
            if g >= 1:
                pe.wait_ge(s["att_low"], g)
            for c in range(dcs):
                for mb in range(TB):
                    mm = pe.matmul(ps[dst_rows(h), 7, c * T:(c + 1) * T], v(h, c, mb),
                                   att_turned(t, g)[:, mb * T:(mb + 1) * T], start=mb == 0, stop=mb == TB - 1)
            mm.then_inc(s["att_out"], 1)

        scores(g0)
        for g in range(g0, g0 + heads):
            if g + 1 < g0 + heads:
                scores(g + 1)
            turn(g)
            mix(g)

    pe.wait_ge(s["consts_in"], 32)
    norm_sum("mem")
    mem_parts = (t.page_r[2], t.page_r[1])
    project("mem_k", mem_parts, n=2, name="mem")
    norm_sum("mix0")
    project("mem_v", mem_parts, n=2, token=True)

    project("w_in", norm_parts, name="mix0")
    project("w_in", norm_parts, first=4, token=True)
    project("w_in", norm_parts, first=8, groups=4)
    project("w_in", norm_parts, first=24, n=2, token=True)
    project("w_in", norm_parts, first=26, n=2)
    project("w_in", norm_parts, first=28)

    half = FP // 2
    pe.wait_ge(s["u_evac"], SEG["w_in"] + 28)
    pe.wait_ge(s["bias_ready"], 2)
    pr = lambda h: slice(NA_D * (h % 2), NA_D * (h % 2 + 1))
    attention(0, NA_H,
              lambda h, c: t.page[5][pr(h), h // 2 * T:(h // 2 + 1) * T],
              lambda h, c: t.page[5][pr(h), half + h // 2 * T:half + (h // 2 + 1) * T],
              lambda h, c, mb: t.page[6][:, mb * 512 + h * NA_D:mb * 512 + (h + 1) * NA_D],
              1, 1, pr, lambda h, qb: t.page[14 + qb][:, h * 256:(h + 1) * 256])
    whole = lambda h: slice(0, P)
    attention(NA_H, CA_H,
              lambda h, c: t.page[6][:, half + h * T:half + (h + 1) * T],
              lambda h, c: t.page[10][:, h * T:(h + 1) * T],
              lambda h, c, mb: t.page[10][:, half + mb * 512 + h * CA_D:half + mb * 512 + (h + 1) * CA_D],
              1, 1, whole)

    for i, (level, hh) in enumerate(HG_STEPS):
        if i < 8:
            project("w_in", norm_parts, first=32 + i, n=1)
        elif i < 12:
            if i == 8:
                pe.wait_ge(s["att_low"], NA_H + CA_H)
            out = (t.work_r if i < 10 else t.page_r[5])
            half_project("na_o" if i < 10 else "ca_o", (out[:, 0:half], out[:, half:FP]), i % 2 * 2)
        pe.wait_ge(s["hg_gh"], i + 1)
        if level != "same":
            pe.wait_ge(s["hg_keys"], i + 1)
        if i >= 2:
            pe.wait_ge(s["hg_kept"], i - 1)
        keys, queries = hg_buf(t, i)
        if level == "same":
            queries = t.page[0][:, hh * 1024:(hh + 1) * 1024]
        for j in range(8):
            h, b = j // 2, j % 2
            qb = 1 - b if level == 128 else b
            mm = pe.matmul(ps[:, 4 + 2 * (i % 2) + j // 4, (j % 4) * P:(j % 4 + 1) * P],
                           keys[:, h * T + b * P:h * T + (b + 1) * P], queries[:, h * T + qb * P:h * T + (qb + 1) * P],
                           start=True, stop=True)
        mm.then_inc(s["hg_sc"], 1)
    pe.wait_ge(s["hg_kept"], len(HG_STEPS))
    for h in range(HG_H):
        for qb in range(TB):
            for b in range(TB):
                kept = (t.page[14] if b == qb else t.page[15])[:, (h * 2 + b) * P:(h * 2 + b + 1) * P]
                mm = pe.matmul(ps[:, 4 + h // 2, (h % 2) * T + qb * P:(h % 2) * T + (qb + 1) * P],
                               t.page[1][:, b * D + h * HG_D:b * D + (h + 1) * HG_D], kept, start=b == 0, stop=b == 1)
        if h % 2:
            mm.then_inc(s["hg_av"], 1)
    for q in range(4):
        pe.wait_ge(s["hg_sq"], q + 1)
        pe.matmul(ps[:, q, :], cst(t, "ones"), t.page[6][:, q * 512:(q + 1) * 512],
                  start=True, stop=True).then_inc(s["hg_var"], 1)
    project("hg_o", (t.page_r[6], t.page_r[5]), name="hg")
    project("w_out", (t.page_r[11], t.page_r[10]), name="merged")

    ffn(0, "ffn0", "ffn0")
    norm_sum("fin0")
    ffn(1, "ffn1", "ffn1")

    norm_sum("mix1")
    for i, seg in enumerate(("rw_r", "rw_k", "rw_v")):
        project(seg, mix_parts(t, i), name=f"rw{i}")
    b = BLK["lora"]
    wh, wl = zip(piece(b, 0), piece(b, 1))
    for i in range(3, 6):
        operand(f"rw{i}")
    first = [[x[k // 4][:, (k % 4) * 256:(k % 4) * 256 + 256] for k in range(KT)] for x in (wh, wl)]
    gate2 = piece(b + 1, 0)
    for bank, i, w in ((4, 3, [[x[:, 0:P] for x in y] for y in first]),
                       (5, 4, [[x[:, 0:P] for x in y] for y in first]),
                       (6, 5, [[x[:, P:] for x in y] for y in first]),
                       (7, 5, [[x[:, k * P:(k + 1) * P] for k in range(KT)] for x in gate2])):
        act = mix_parts(t, i)
        for k in range(KT):
            mm = split_mm(ps[:, bank, 0:T], (w[0][k], w[1][k]), [x[:, k * T:(k + 1) * T] for x in act],
                          start=k == 0, stop=k == KT - 1)
    mm.then_inc(s["piece_done"], 3)
    operand("lora")
    inner = (t.sq_r, t.work_r)
    for which in range(3):
        if which == 2:
            for q in range(4):
                pe.wait_ge(s["rw_kk2"], q + 1)
                if q == 0:
                    pe.wait_ge(s["u_evac"], SEG["rw_o"])
                pe.matmul(ps[:, q, :], cst(t, "head_ones"), t.page[15][:, q * 512:(q + 1) * 512],
                          start=True, stop=True).then_inc(s["rw_kksum"], 1)
        if which:
            pe.wait_ge(s["lora_out"], which)
        w = piece(b + 1, 1) if which < 2 else (*piece(b + 2, 0), *piece(b + 2, 1))
        for j in range(KT):
            out = ps[:, 4 + j // 2, (j % 2) * T:(j % 2 + 1) * T]
            cols = slice(j * P, (j + 1) * P)
            if which < 2:
                mm = split_mm(out, [x[:, cols] for x in w], [x[:, which * T:(which + 1) * T] for x in inner],
                              start=True, stop=True)
            else:
                for c in range(2):
                    mm = split_mm(out, [x[:, cols] for x in w[2 * c:2 * c + 2]],
                                  [x[:, (2 + c) * T:(3 + c) * T] for x in inner], start=c == 0, stop=c == 1)
        if which == 0:
            mm.then_inc(s["lora_mm"], 1)
        else:
            mm.then_inc(s["piece_done"], which)

    for q in range(4):
        if q == 0:
            pe.wait_ge(s["rw_bonus_in"], 1)
        pe.matmul(ps[:, q, :], cst(t, "head_ones"), t.work[:, q * 512:(q + 1) * 512],
                  start=True, stop=True).then_inc(s["rw_bonus_sum"], 1)

    for q in range(12):
        src = (t.page[9], t.page[5], t.page[6])[q // 4]
        b, c0 = q % 4 // 2, q % 2 * 4
        if q == 0:
            pe.wait_ge(s["lora_out"], 3)
            pe.wait_ge(s["rw_dec"], 1)
        if q >= 4:
            pe.wait_ge(s["rw_t_sb"], q - 3)
        for c in range(4):
            mm = pe.transpose(ps[:, 4 + q % 4, c * P:(c + 1) * P],
                              src[:, (c0 + c) * T + b * P:(c0 + c) * T + (b + 1) * P], cst(t, "ident"))
        mm.then_inc(s["rw_t"], 1)

    A, B, K, R = t.page[3], t.page[5], t.page[6], t.page[7]

    def chunk_matrices(c):
        for p, pair in enumerate((((B, A), (A, B)), ((K, A), (B, R)), ((K, R),))):
            q = 3 * c + p
            if q == 0:
                pe.wait_ge(s["rw_act"], 1)
            if q >= 2:
                pe.wait_ge(s["rw_m_sb"], q - 1)
            for e in range(2):
                hp = slice(RW_D * e, RW_D * (e + 1))
                for j, (left, right) in enumerate(pair):
                    for b in range(TB):
                        tok = slice(c * T + b * P, c * T + (b + 1) * P)
                        mm = pe.matmul(ps[:, 2 * (q % 2) + e, (2 * j + b) * P:(2 * j + b + 1) * P],
                                       left[hp, tok], right[hp, tok], start=True, stop=True)
            mm.then_inc(s["rw_m"], 1)

    def invert_y(c, lv):
        q, buf = inv_at(c, lv), inv_buf(t, c)
        if lv == 0:
            pe.wait_ge(s["rw_m_sb"], 3 * c + 3)
        else:
            pe.wait_ge(s["rw_z_sb"], q - 1)
        pe.wait_ge(s["rw_lm"], q + 1)
        if q == 0:
            pe.wait_ge(s["rw_t_sb"], 12)
        for j in range(4):
            mm = pe.matmul(ps[:, 4 + 2 * (c % 2), j * P:(j + 1) * P], buf.lm[:, j * P:(j + 1) * P],
                           buf.x[:, j * P:(j + 1) * P], start=True, stop=True)
        mm.then_inc(s["rw_y"], 1)

    def invert_z(c, lv):
        q, buf, xt = inv_at(c, lv), inv_buf(t, c), inv_xt(t, c)
        pe.wait_ge(s["rw_y_sb"], q + 1)
        if lv < len(LEVELS) - 2:
            for j in range(4):
                pe.matmul(ps[:, 4 + 2 * (c % 2), j * P:(j + 1) * P], xt[:, j * P:(j + 1) * P],
                          buf.y[:, j * P:(j + 1) * P], start=True, stop=True)
        for j in range(4):
            mm = pe.matmul(ps[:, 5 + 2 * (c % 2), j * P:(j + 1) * P], buf.y[:, j * P:(j + 1) * P],
                           xt[:, j * P:(j + 1) * P], start=True, stop=True)
        mm.then_inc(s["rw_z"], 1)

    for c in range(0, KT, 2):
        chunk_matrices(c)
        chunk_matrices(c + 1)
        for lv in range(len(LEVELS) - 1):
            invert_y(c, lv)
            invert_y(c + 1, lv)
            invert_z(c, lv)
            invert_z(c + 1, lv)

    rhs, usb, st = t.page[5][:, 0:1024], t.page[5][:, 1024:], t.page[6][:, 0:1024]
    vt, bt, kt_ = t.page[1], t.page[2], t.page[4]

    def mat(base, c, e, b):
        page = base[c // 4]
        at_ = ((c % 4) * 4 + e * 2 + b) * P
        return page[:, at_:at_ + P]

    pe.wait_ge(s["rw_z_sb"], 8 * (len(LEVELS) - 1))
    pe.wait_ge(s["rw_m_sb"], 24)
    pe.wait_ge(s["rw_zero"], 1)
    for n_ in range(NCH):
        b, po = n_ // 2, slice(CH * (n_ % 2), CH * (n_ % 2 + 1))
        if n_ > 0:
            pe.wait_ge(s["rw_s"], n_)
        for c in range(KT):
            out = ps[po, c // 4, (c % 4) * P:(c % 4 + 1) * P]
            tok = slice(c * T + n_ * CH, c * T + (n_ + 1) * CH)
            pe.matmul(out, A[:, tok], st[:, c * P:(c + 1) * P], start=True, stop=False, skip_group_check=True)
            for e in range(2):
                mm = pe.matmul(out[:, e * CH:(e + 1) * CH], mat(RW_MT(t), c, e, b)[:, po],
                               vt[:, b * D + c * P + e * RW_D:b * D + c * P + (e + 1) * RW_D],
                               start=False, stop=e == 1, skip_group_check=True)
        mm.then_inc(s["rw_rhs"], 1)
        for c in range(KT):
            pe.matmul(ps[:, 4 + c // 2, (c % 2) * T + n_ * CH:(c % 2) * T + (n_ + 1) * CH],
                      st[:, c * P:(c + 1) * P], R[:, c * T + n_ * CH:c * T + (n_ + 1) * CH],
                      start=n_ == 0 and c % 2 == 0, stop=False, skip_group_check=True)
        pe.wait_ge(s["rw_rhs_sb"], 2 * (n_ + 1))
        for c in range(KT):
            for e in range(2):
                cols = slice(c * P + e * RW_D, c * P + (e + 1) * RW_D)
                mm = pe.matmul(ps[po, 2 + c // 4, (c % 4) * P + e * CH:(c % 4) * P + (e + 1) * CH],
                               mat(RW_TT(t), c, e, b)[:, po], rhs[:, cols], start=True, stop=True,
                               skip_group_check=True)
        mm.then_inc(s["rw_u"], 1)
        pe.wait_ge(s["rw_u_sb"], 2 * (n_ + 1))
        if n_ < NCH - 1:
            for c in range(KT):
                out = ps[:, c // 4, (c % 4) * P:(c % 4 + 1) * P]
                cols = slice(c * P, (c + 1) * P)
                full = slice(b * D + c * P, b * D + (c + 1) * P)
                pe.matmul(out, bt[po, full], usb[po, cols], start=True, stop=False, skip_group_check=True)
                mm = pe.matmul(out, kt_[po, full], vt[po, full], start=False, stop=True, skip_group_check=True)
            mm.then_inc(s["rw_ds"], 1)
        if n_ % 2:
            for c in range(KT):
                for e in range(2):
                    out = ps[e * RW_D:(e + 1) * RW_D, 4 + c // 2, (c % 2) * T + b * P:(c % 2) * T + (b + 1) * P]
                    cols = slice(c * P + e * RW_D, c * P + (e + 1) * RW_D)
                    pe.matmul(out, vt[:, b * D + cols.start:b * D + cols.stop], mat(RW_RKT(t), c, e, b),
                              start=False, stop=False, skip_group_check=True)
                    mm = pe.matmul(out, usb[:, cols], mat(RW_RBT(t), c, e, b), start=False,
                                   stop=False, skip_group_check=True)
    mm.then_inc(s["rw_yt"], 1)
    for q in range(4):
        pe.wait_ge(s["rw_yt_sb"], q + 1)
        pe.matmul(ps[:, q, :], cst(t, "head_ones"), t.page[8][:, q * 512:(q + 1) * 512],
                  start=True, stop=True).then_inc(s["rw_mean"], 1)
    for q in range(4):
        pe.wait_ge(s["rw_sq"], q + 1)
        pe.matmul(ps[:, q, :], cst(t, "head_ones"), t.sq[:, q * 512:(q + 1) * 512],
                  start=True, stop=True).then_inc(s["rw_var"], 1)
    project("rw_o", (t.page_r[10], t.page_r[7]), n=2, name="rw_o")
    norm_sum("mem2")
    project("rw_o", (t.page_r[10], t.page_r[7]), first=2, n=2)

    mem_parts = (t.page_r[4], t.page_r[3])
    project("mem2_k", mem_parts, name="mem2")
    project("mem2_v", mem_parts, token=True)

    def memory_attention(i, name):
        project(f"xq{i}", norm_parts, n=1, name=name)
        norm_sum(name)
        project(f"xq{i}", norm_parts, first=1, n=3)
        pe.wait_ge(s["u_evac"], SEG[f"xq{i}"] + 4)
        attention(NA_H + CA_H + XA_H * i, XA_H,
                  lambda h, c: t.page[0][:, (2 * h + c) * T:(2 * h + c + 1) * T],
                  lambda h, c: t.page[14][:, (2 * h + c) * T:(2 * h + c + 1) * T],
                  lambda h, c, mb: t.page[15][:, mb * D + h * XA_D + c * P:mb * D + h * XA_D + (c + 1) * P],
                  2, 2, whole)
        for k in range(4):
            n = SEG[f"xo{i}"] + k
            bank_free(n)
            for hf in range(2):
                w = piece(BLK[f"xo{i}"] + k, hf)
                for kk in range(4):
                    c = 4 * hf + kk
                    if k == 0 and c % 2 == 0:
                        pe.wait_ge(s["att_low"], NA_H + CA_H + XA_H * i + c // 2 + 1)
                    for j in range(2):
                        mm = split_mm(ps[:, n % BANKS, j * T:(j + 1) * T],
                                      [x[:, kk * 256 + j * P:kk * 256 + (j + 1) * P] for x in w],
                                      [t.page_r[q][:, c * T:(c + 1) * T] for q in (2, 1)],
                                      start=c == 0 and j == 0, stop=c == KT - 1)
                mm.then_inc(s["piece_done"], 1)

    memory_attention(0, "x0")
    ffn(2, "ffn2", "ffn2")
    ffn(3, "ffn3", "ffn3")

    norm_sum("mix2")
    operand("mix2")
    project("gm_u", norm_parts, groups=2)
    project("gm_v", norm_parts, groups=2, token=True)
    pe.wait_ge(s["gm_mask"], 1)
    for q in range(8):
        if q < 2:
            pe.wait_ge(s["gm_vout"], 1)
        else:
            pe.wait_ge(s["gm_mixed"], q - 1)
        for j in range(4):
            g, b = 2 * q + j // 2, j % 2
            mm = pe.matmul(ps[:, 4 + q % 2, j * P:(j + 1) * P],
                           t.page[2 + b][:, g * P:(g + 1) * P], t.page[4][:, g * P:(g + 1) * P],
                           start=True, stop=True)
        mm.then_inc(s["gm_mix"], 1)
    for q in range(4):
        n, b = SEG["gm_o"] + q, BLK["gm_o"] + 2 * q
        bank_free(n)
        for k4 in range(4):
            w = piece(b + k4 // 2, k4 % 2)
            for j in range(2):
                for kk in range(4):
                    k = 4 * k4 + kk
                    if q == 0 and j == 0:
                        operand_part(f"gm{k // KT}", k % KT)
                    mm = split_mm(ps[:, n % BANKS, j * T:(j + 1) * T],
                                  [x[:, kk * 256 + j * P:kk * 256 + (j + 1) * P] for x in w],
                                  [t.page_r[first + k // KT][:, k % KT * T:(k % KT + 1) * T] for first in (10, 7)],
                                  start=k4 == 0 and j == 0 and kk == 0, stop=k == 2 * KT - 1)
            mm.then_inc(s["piece_done"], 1)
    memory_attention(1, "x1")
    ffn(4, "ffn4", "ffn4")
    norm_sum("fin2")


class At:

    def __init__(self, number, first):
        self.number, self.first = number, first

    def __mul__(self, k):
        return self.number * k

    def __add__(self, k):
        return At(self.number + k, self.first + k)


def last_down(f):
    return BLK[f"ffn{f}"] + 3 * FIT - 1


def block0(b):
    return b if isinstance(b, int) else b.first


def hidden_parts(t, k):
    return t.page_r[2][:, k * 512:(k + 1) * 512], t.work_r[:, k * 512:(k + 1) * 512]


def mix_parts(t, i):
    return t.page_r[10 + i], t.page_r[1 + i]


HG_STEPS = [(level, hh) for level in (64, *LEVELS, 128, "same") for hh in range(2)]


def hg_buf(t, i):
    buf = t.page[13] if i % 2 == 0 else t.page[6]
    return buf[:, 1024:2048], buf[:, 0:1024]


def att_buf(t, g):
    return t.page[13][:, (g % 2) * 512:(g % 2 + 1) * 512]


def att_turned(t, g):
    return t.page[13][:, 1024 + (g % 2) * 512:1024 + (g % 2 + 1) * 512]


def inv_at(c, lv):
    return c // 2 * 2 * (len(LEVELS) - 1) + 2 * lv + c % 2


def inv_buf(t, c):
    buf = t.sq[:, :] if c % 2 == 0 else t.work[:, :]
    parts = Bag()
    parts.lt, parts.lm, parts.x, parts.y = (buf[:, i:i + 512] for i in range(0, 2048, 512))
    return parts


def stack(pages, c):
    return pages[c // 4][:, (c % 4) * 512:(c % 4 + 1) * 512]


def RW_MT(t):
    return t.page[8], t.page[9]


def RW_RBT(t):
    return t.page[10], t.page[11]


def RW_RKT(t):
    return t.page[12], t.page[14]


def RW_TT(t):
    return t.page[15], t.h[:, :]


def inv_xt(t, c):
    return stack(RW_TT(t), c)


def norm_table(t, s):
    x, h, seg = t.x[:, :], t.h[:, :], SEG
    up = lambda n, f: (s["x_up"], 4 * f + 2, 2)
    rows = {
        "mem": (t.page[0], (s["mem_in"], 16, 0), ("mem_norm", 0), t.page[1]),
        "mix0": (x, (s["x_in"], 16, 0), ("norm_mix", 0), h),
        "ffn0": (x, (s["u_evac"], seg["w_out"] + 2, 2), ("norm_ffn", 0), h),
        "fin0": (x, (s["x_up"], 2, 2), ("norm_final", 0), x),
        "ffn1": (x, (s["norm_out"], KT * PLAIN["fin0"] + 4, 4), ("ffn1_norm_2", 0), h),
        "mix1": (x, (s["x_up"], 4 + 2, 2), ("mix_norm_2", 0), h),
        "mem2": (t.page[3], (s["mem2_in"], 16, 0), ("mem_norm_2", 0), t.page[3]),
        "x0": (x, (s["u_evac"], seg["rw_o"] + 2, 2), ("xattn_norm_2", 0), h),
        "ffn2": (x, (s["u_evac"], seg["xo0"] + 2, 2), ("ffn2_norm_2", 0), h),
        "ffn3": (x, (s["x_up"], 8 + 2, 2), ("ffn1_norm_2", 8), h),
        "mix2": (x, (s["x_up"], 12 + 2, 2), ("mix_norm_2", 8), h),
        "x1": (x, (s["u_evac"], seg["gm_o"] + 2, 2), ("xattn_norm_2", 8), h),
        "ffn4": (x, (s["u_evac"], seg["xo1"] + 2, 2), ("ffn2_norm_2", 8), h),
        "fin2": (x, (s["x_up"], 16 + 2, 2), ("final_norm_2", 0), h),
    }
    return rows


def NORM_HIGH(t, name):
    return {"mem": t.page_r[2], "mem2": t.page_r[4]}.get(name, t.sq_r)


def NORM_LOW(t, name):
    return {"mem": t.page_r[1], "mem2": t.page_r[3]}.get(name, t.h_r)


def scalar_program(act, a, t, s):
    ps = t.ps
    norms = norm_table(t, s)
    f = act.activation

    def high(b):
        b0 = block0(b) + AHEAD
        if isinstance(b, int) and b0 >= N_BLK:
            return
        b = b + AHEAD
        act.wait_ge(s["raw_in"][b0 % 2], (b0 // 2 + 1) * 16 if isinstance(b, int) else b * 8 + (16 - b0 % 2 * 8))
        for hf in range(2):
            if not isinstance(b, int) or b0 >= 2:
                act.wait_ge(s["piece_done"], b * 2 + (hf - 3))
            f(t.wh[(2 * b0 + hf) % PIECE_SLOTS][:], t.raw[b0 % 2][:, hf * 1024:(hf + 1) * 1024],
              ACT.Copy).then_inc(s["high_done"], 1)

    def highs(seg, first=0, n=4):
        for k in range(n):
            high(BLK[seg] + first + k)

    def operand_high(name, src, dst, ready, width=512):
        for q in range(4):
            c = slice(q * width, (q + 1) * width)
            ready(q)
            f(dst[:, c], src[:, c], ACT.Copy).then_inc(s["op_high"], 1)

    def norm_squares(name, dst, halves=(0, 1)):
        i = NORM[name]
        src, (sem, first, step), _, _ = norms[name]
        if i:
            act.wait_ge(s["norm_part"], 2 * i)
        for hf in halves:
            act.wait_ge(sem, first + step * hf)
            c = slice(hf * 1024, (hf + 1) * 1024)
            f(dst[:, c], src[:, c], ACT.Square).then_inc(s["norm_sq"], 1)

    def log_root(dst, src, scale, col, var_read):
        f(dst, src, ACT.Ln, scale=scale, bias=t.stat[:, col:col + 1]).then_inc(s[var_read], 1)

    def norm_root(name):
        act.wait_ge(s["norm_sum"], NORM[name] + 1)
        log_root(t.rstd[:], ps[:, 4, 0:T], 1.0 / D, COL_EPS, "norm_var")
        act.wait_ge(s["norm_var"], NORM[name] + 1)
        f(t.rstd[:], t.rstd[:], ACT.Exp, scale=-0.5).then_inc(s["norm_std"], 1)
        if name in OPERAND and name not in LATE:
            operand_high(name, norms[name][3], NORM_HIGH(t, name),
                         lambda q: act.wait_ge(s["norm_out"], KT * PLAIN[name] + 2 * (q + 1)))

    def norm(name, prev=None):
        norm_squares(name, t.sq)
        if prev is not None:
            high(prev)
        norm_root(name)

    def late_norm(name, prev=None):
        src, (sem, first, step), gain, _ = norms[name]
        for q in range(4):
            act.wait_ge(sem, first + step // 2 * (q - 1))
            for k in (2 * q, 2 * q + 1):
                c = slice(k * T, (k + 1) * T)
                ins = f(t.sq_r[:, c], src[:, c], ACT.Copy, scale=par(t, gain[0], gain[1] + k))
            ins.then_inc(s["op_high"], 1)
            if q == 1:
                norm_squares(name, t.page[12], (0,))
        if prev is not None:
            high(prev)
        norm_squares(name, t.page[12], (1,))

    def take(n, bank, b, dst, func=ACT.Copy):
        act.wait_ge(s["piece_done"], b * 2 + 2)
        src = ps[:, bank, :]
        if len(dst.shape) == 3:
            src = src.rearrange("p (b c) -> p b c", b=dst.shape[1])
        f(dst, src, func).then_inc(s["u_evac"], 1)

    def take_run(seg, page, first=0, n=4, func=ACT.Copy):
        for k in range(n):
            high(BLK[seg] + first + k)
            take(SEG[seg] + first + k, (SEG[seg] + first + k) % BANKS, BLK[seg] + first + k,
                 page[:, k * 512:(k + 1) * 512], func)

    def take_groups(seg, page0, first, groups, func=ACT.Copy):
        n0, b0 = SEG[seg] + first, BLK[seg] + first
        with act.Fori(0, groups) as i:
            for k in range(4):
                b = At(i * 4 + (b0 + k), b0 + k)
                high(b)
                take(None, (n0 + k) % BANKS, b,
                     t.pages[:, bass.ds(i * FP + (page0 * FP + k * 512), 512)], func)

    def take_tokens(seg, region, width, first=0, n=4, func=ACT.Copy):
        for k in range(n):
            high(BLK[seg] + first + k)
            dst = region.rearrange("p (b c) -> p b c", b=TB)[:, :, k * 256:(k + 1) * 256]
            take(SEG[seg] + first + k, (SEG[seg] + first + k) % BANKS, BLK[seg] + first + k, dst, func)

    def attention(g0, heads, scale, cols, dst, chores=()):
        def exp(g):
            buf, st = att_buf(t, g), (g % 2) * 8
            act.wait_ge(s["att_max"], g + 1)
            if g >= 2:
                act.wait_ge(s["att_turned"], g - 1)
            for qb in range(TB):
                src = ps[:, 4 + g % 2, qb * 256:(qb + 1) * 256]
                ins = f(buf[:, qb * 256:(qb + 1) * 256], src, ACT.Exp, bias=t.stat[:, st + 2 + qb:st + 3 + qb],
                        scale=scale, accum_out=t.stat[:, st + 4 + qb:st + 5 + qb])
            ins.then_inc(s["att_exp"], 1)

        exp(g0)
        for g in range(g0, g0 + heads):
            if g + 1 < g0 + heads:
                exp(g + 1)
            act.wait_ge(s["att_turned"], g + 1)
            if g >= 2:
                act.wait_ge(s["att_out"], g - 1)
            f(att_turned(t, g), ps[:, 6, :], ACT.Copy).then_inc(s["att_turned_sb"], 1)
            act.wait_ge(s["att_out"], g + 1)
            out = dst(g - g0)
            rows = slice(out[0], out[1])
            f(out[2], ps[rows, 7, 0:cols], ACT.Copy).then_inc(s["att_high"], 1)
            if g - g0 < len(chores):
                chores[g - g0]()

    norm_squares("mem", t.sq)
    act.wait_ge(s["zero_row"], 1)
    for b in range(-AHEAD, 0):
        high(b)
    norm_root("mem")
    norm_squares("mix0", t.sq)
    act.wait_ge(s["lb_zero"], 1)
    f(t.lb[:, 16:32], t.lb[:, 0:16], ACT.Exp).then_inc(s["lb_exp"], 1)
    take_run("mem_k", t.page[10], n=2)
    norm_root("mix0")
    take_tokens("mem_v", t.page[10][:, 1024:2048], 512, n=2)
    take_run("w_in", t.page[0])
    take_tokens("w_in", t.page[1], D, first=4)
    take_groups("w_in", 2, 8, 4)
    take_tokens("w_in", t.page[6][:, 0:1024], 512, first=24, n=2)
    take_run("w_in", t.page[6][:, 1024:2048], first=26, n=2)

    act.wait_ge(s["u_evac"], SEG["w_in"] + 20)
    for src, dst in ((2, 11), (3, 12)):
        f(t.page[dst], t.page[src], ACT.Sigmoid).then_inc(s["hg_sig"], 1)
        f(t.page[src], t.page[src], ACT.Sigmoid, scale=-1.0).then_inc(s["hg_sig"], 1)
    take_run("w_in", t.page[7], first=28, func=ACT.Sigmoid)
    f(t.page[0], t.page[0], ACT.Silu).then_inc(s["hg_silu"], 1)
    f(t.page[4], t.page[4], ACT.Silu).then_inc(s["hg_silu"], 1)

    def forget_log(i):
        act.wait_ge(s["hg_floor"], i + 1)
        f(t.page[11 + i], t.page[11 + i], ACT.Ln).then_inc(s["hg_log"], 1)

    def na_dst(h):
        lo = NA_D * (h % 2)
        return lo, lo + NA_D, t.work_r[lo:lo + NA_D, h // 2 * T:(h // 2 + 1) * T]

    wait_a_head = lambda: None
    attention(0, NA_H, NA_D ** -0.5, T, na_dst,
              (wait_a_head, lambda: forget_log(0), wait_a_head, lambda: forget_log(1)))
    attention(NA_H, CA_H, CA_D ** -0.5, T, lambda h: (0, P, t.page_r[5][:, h * T:(h + 1) * T]))

    for i, (level, hh) in enumerate(HG_STEPS):
        if level != "same":
            act.wait_ge(s["hg_expo"], i + 1)
            buf = t.page[13] if i % 2 == 0 else t.page[6]
            f(buf, buf, ACT.Exp).then_inc(s["hg_exp"], 1)
        if i < 8:
            take_run("w_in", t.page[8 + i // 4][:, i % 4 * 512:], first=32 + i, n=1)
        elif i < 12:
            highs("na_o" if i < 10 else "ca_o", i % 2, 1)
        if i == 7:
            act.wait_ge(s["u_evac"], SEG["w_in"] + 40)
            for page in (8, 9):
                f(t.page[page], t.page[page], ACT.Sigmoid).then_inc(s["att_gates"], 1)
    for q in range(4):
        c = slice(q * 512, (q + 1) * 512)
        act.wait_ge(s["hg_av"], q + 1)
        f(t.page[5][:, c], ps[:, 4 + q, :], ACT.Copy, scale=HG_D ** -0.5).then_inc(s["hg_o"], 1)
        act.wait_ge(s["hg_o"], q + 1)
        f(t.page[6][:, c], t.page[5][:, c], ACT.Square).then_inc(s["hg_sq"], 1)
    for q in range(4):
        act.wait_ge(s["hg_var"], q + 1)
        log_root(t.page[2][:, q * 512:(q + 1) * 512], ps[:, q, :], 1.0 / HG_D, COL_EPS, "hg_varsb")
    for q in range(4):
        act.wait_ge(s["hg_varsb"], q + 1)
        c = slice(q * 512, (q + 1) * 512)
        f(t.page[2][:, c], t.page[2][:, c], ACT.Exp, scale=-0.5).then_inc(s["hg_std"], 1)

    operand_high("hg", t.page[5], t.page_r[6], lambda q: act.wait_ge(s["hg_out"], q + 1))
    highs("hg_o")
    operand_high("merged", t.page[10], t.page_r[11], lambda q: act.wait_ge(s["merged"], q + 1))
    highs("w_out", n=3)

    def hidden_high(fi, st, k):
        act.wait_ge(s["hidden_made"], st + (fi * FIT + 1))
        f(hidden_parts(t, k)[0], t.work[:, k * 512:(k + 1) * 512], ACT.Copy).then_inc(s["hidden_high"], 1)

    def ffn(fi, seg, early, late, prev=None, end=lambda *step: None):
        b = BLK[seg]
        late_norm(seg, prev)
        high(b)
        norm_root(seg)
        early(0, 0, 0, True)
        high(b + 1)
        late(0, 0, 0, True)
        end(0, 0, 0, True)

        def two_steps(i, first=False):
            for k in range(2):
                r = b + 2 + 3 * k
                blk = [i * 6 + (r + j) if isinstance(i, int) else At(i * 6 + (r + j), r + j) for j in range(3)]
                step = (i * 2 + (1 + k), i * 4 + (2 + 2 * k), (1 + k) % 2, first and k == 0)
                high(blk[0])
                early(*step)
                high(blk[1])
                late(*step)
                high(blk[2])
                end(*step)

        trips = (FIT - 1) // 2
        if fi == 0:
            two_steps(0, first=True)
        last = trips - 1 if fi == N_FFN - 1 else trips
        with act.Fori(int(fi == 0), last) as i:
            two_steps(i)
        if last < trips:
            two_steps(last)

    cw, cb = PCOL["conv_w"] + 44, PCOL["conv_b"]

    def conv_middle(st, tile, k, half):
        act.wait_ge(s["u_evac"], st * 2 + (SEG["ffn0"] + half + 1))
        for j in (2 * half, 2 * half + 1):
            col = tile + (j % 2 + FF // P * (j // 2))
            if isinstance(col, int):
                w, bias = t.param[:, cw + col:cw + col + 1], t.param[:, cb + col:cb + col + 1]
            else:
                w, bias = t.param[:, bass.ds(col + cw, 1)], t.param[:, bass.ds(col + cb, 1)]
            ins = f(t.page[k][:, j * T:(j + 1) * T], t.page[13][:, k * 1024 + j * T:k * 1024 + (j + 1) * T],
                    ACT.Identity, scale=w, bias=bias)
        ins.then_inc(s["conv_mid"], 1)

    def conv_gate(st, tile, k, first):
        if not first:
            act.wait_ge(s["hidden_made"], st - 1)
        conv_middle(st, tile, k, 0)

    def conv_up(st, tile, k, first):
        conv_middle(st, tile, k, 1)
        act.wait_ge(s["conv_done"], st + 1)
        f(t.page[k][:, 0:512], t.page[k][:, 0:512], ACT.Gelu_apprx_tanh).then_inc(s["gelu_ready"], 1)

    assert SEG["ffn0"] % 2 == 0
    ffn(0, "ffn0", conv_gate, conv_up, BLK["w_out"] + 3, lambda st, tile, k, first: hidden_high(0, st, k))
    norm("fin0", last_down(0))

    def swiglu(fi, seg, prev=None):
        def gate(st, tile, k, first):
            act.wait_ge(s["gate_scaled"], st + ((fi - 1) * FIT + 1))
            gate_ = t.work[:, 1024 + k * 512:1536 + k * 512]
            f(gate_, gate_, ACT.Silu).then_inc(s["gate_ready"], 1)

        ffn(fi, seg, gate, lambda st, tile, k, first: hidden_high(fi, st, k), prev)

    swiglu(1, "ffn1")

    norm("mix1", last_down(1))
    for step in RW_ORDER:
        if isinstance(step, int):
            operand_high(f"rw{step}", t.page[1 + step], t.page_r[10 + step],
                         lambda q: act.wait_ge(s["rw_mix"], 4 * step + q + 1))
        else:
            k = int(step[1:])
            high(BLK["rw_r"] + k)
            take(None, (SEG["rw_r"] + k) % BANKS, BLK["rw_r"] + k,
                 t.pages[:, 7 * FP + k * 512:7 * FP + (k + 1) * 512])
    highs("lora", n=1)
    act.wait_ge(s["piece_done"], 2 * BLK["lora"] + 3)
    act.wait_ge(s["inner_zero"], 1)
    f(t.work[0:64, 0:T], ps[0:64, 4, 0:T], ACT.Tanh)
    f(t.work[64:P, T:2 * T], ps[64:P, 5, 0:T], ACT.Copy)
    for j in range(2):
        ins = f(t.work[:, (2 + j) * T:(3 + j) * T], ps[:, 6 + j, 0:T], ACT.Sigmoid)
    ins.then_inc(s["lora_mid"], 1)
    act.wait_ge(s["lora_mid"], 1)
    operand_high("lora", t.work[:, 0:1024], t.sq_r[:, 0:1024], lambda q: None, 256)
    for which, name in ((0, "rwkv_w0_2"), (1, "rwkv_a0_2")):
        if which:
            act.wait_ge(s["piece_done"], 2 * BLK["lora"] + 4)
        else:
            act.wait_ge(s["lora_mm"], 1)
        for j in range(KT):
            ins = f(t.page[11 + which][:, j * T:(j + 1) * T], ps[:, 4 + j // 2, (j % 2) * T:(j % 2 + 1) * T],
                    ACT.Sigmoid, bias=par(t, name, j))
        ins.then_inc(s["lora_out"], 1)
        if which == 0:
            for q in range(4):
                c = slice(q * 512, (q + 1) * 512)
                act.wait_ge(s["rw_kk"], q + 1)
                f(t.page[15][:, c], t.page[1][:, c], ACT.Square).then_inc(s["rw_kk2"], 1)
    RATE = float(np.exp(-0.5))
    act.wait_ge(s["rw_cum"], 1)
    f(t.page[3], t.page[3], ACT.Exp, scale=-RATE).then_inc(s["rw_exp"], 1)
    f(t.page[4], t.page[2], ACT.Exp, scale=RATE).then_inc(s["rw_exp"], 1)
    f(t.page[10], t.page[2], ACT.Exp, scale=-RATE).then_inc(s["rw_exp"], 1)
    for q in range(4):
        act.wait_ge(s["rw_kkfloor"], q + 1)
        f(t.h[:, q * 512:(q + 1) * 512], t.h[:, q * 512:(q + 1) * 512], ACT.Ln).then_inc(s["rw_kkln"], 1)
    for q in range(4):
        act.wait_ge(s["rw_kkln"], q + 1)
        f(t.h[:, q * 512:(q + 1) * 512], t.h[:, q * 512:(q + 1) * 512], ACT.Exp,
          scale=-0.5).then_inc(s["rw_kkvar"], 1)
    act.wait_ge(s["piece_done"], 2 * BLK["lora"] + 6)
    f(t.page[13][:, 0:1024].rearrange("p (a b) -> p a b", a=2), ps[:, 4:6, :], ACT.Copy)
    f(t.page[13][:, 1024:].rearrange("p (a b) -> p a b", a=2), ps[:, 6:8, :], ACT.Copy).then_inc(s["lora_out"], 1)
    highs("lora", 1, 2)
    for q in range(12):
        dst = (t.page[1], t.page[2], t.page[4])[q // 4]
        b, half = q % 4 // 2, q % 2
        act.wait_ge(s["rw_t"], q + 1)
        f(dst[:, b * D + half * 512:b * D + (half + 1) * 512], ps[:, 4 + q % 4, :], ACT.Copy).then_inc(s["rw_t_sb"], 1)
    for c0 in range(0, KT, 2):
        for lv in range(len(LEVELS) - 1):
            for c in (c0, c0 + 1):
                act.wait_ge(s["rw_y"], inv_at(c, lv) + 1)
                f(inv_buf(t, c).y, ps[:, 4 + 2 * (c % 2), :], ACT.Copy).then_inc(s["rw_y_sb"], 1)
    for n_ in range(NCH):
        po = slice(CH * (n_ % 2), CH * (n_ % 2 + 1))
        act.wait_ge(s["rw_rhs"], n_ + 1)
        f(t.page[5][po, 512:1024], ps[po, 1, :], ACT.Copy, scale=-1.0).then_inc(s["rw_rhs_sb"], 1)
        act.wait_ge(s["rw_u"], n_ + 1)
        f(t.page[5][po, 1536:2048], ps[po, 3, :], ACT.Copy).then_inc(s["rw_u_sb"], 1)
    act.wait_ge(s["rw_yt"], 1)
    act.dma_start(t.page[3], a.mem2_t).then_inc(s["mem2_in"], 16)
    act.dma_start(t.page[5], a.bias_rows).then_inc(s["rows_in"], 16)
    act.dma_start(t.page[6], a.gain_rows).then_inc(s["rows_in"], 16)
    act.dma_start(t.page[9], a.mix_weights).then_inc(s["rows_in"], 16)
    for q in range(4):
        f(t.page[8][:, q * 512:(q + 1) * 512], ps[:, 4 + q, :], ACT.Copy).then_inc(s["rw_yt_sb"], 1)
    for q in range(4):
        c = slice(q * 512, (q + 1) * 512)
        act.wait_ge(s["rw_cent"], q + 1)
        f(t.sq[:, c], t.page[8][:, c], ACT.Square).then_inc(s["rw_sq"], 1)
    for q in range(4):
        c = slice(q * 512, (q + 1) * 512)
        act.wait_ge(s["rw_var"], q + 1)
        log_root(t.page[2][:, c], ps[:, q, :], 1.0 / RW_D, COL_GN_EPS, "rw_varsb")
    for q in range(4):
        c = slice(q * 512, (q + 1) * 512)
        act.wait_ge(s["rw_varsb"], q + 1)
        f(t.page[2][:, c], t.page[2][:, c], ACT.Exp, scale=-0.5).then_inc(s["rw_std"], 1)

    operand_high("rw_o", t.page[7], t.page_r[10], lambda q: act.wait_ge(s["rw_out"], q + 1))
    norm_squares("mem2", t.sq)
    highs("rw_o", n=2)
    norm_root("mem2")
    highs("rw_o", 2, 2)
    take_run("mem2_k", t.page[14])
    take_tokens("mem2_v", t.page[15], D)

    def memory_attention(i, prev=None):
        late_norm(f"x{i}", prev)
        highs(f"xq{i}", n=1)
        norm_root(f"x{i}")
        highs(f"xq{i}", 1, 3)
        attention(NA_H + CA_H + XA_H * i, XA_H, XA_D ** -0.5, 2 * T,
                  lambda h: (0, P, t.page_r[2][:, h * 512:(h + 1) * 512]))
        highs(f"xo{i}", n=3)

    memory_attention(0)
    swiglu(2, "ffn2", BLK["xo0"] + 3)
    swiglu(3, "ffn3", last_down(2))

    norm("mix2", last_down(3))
    take_groups("gm_u", 0, 0, 2, ACT.Gelu_apprx_tanh)
    v2 = t.pages[:, 2 * FP:4 * FP].rearrange("p (b c) -> p b c", b=TB)
    with act.Fori(0, 2) as i:
        for k in range(4):
            b = At(i * 4 + (BLK["gm_v"] + k), BLK["gm_v"] + k)
            high(b)
            take(None, (SEG["gm_v"] + k) % BANKS, b, v2[:, :, bass.ds(i * 1024 + k * 256, 256)], ACT.Gelu_apprx_tanh)
    act.wait_ge(s["u_evac"], SEG["gm_v"] + 8)
    for b in range(TB):
        ins = f((t.sq, t.work)[b][:, :], t.page[2 + b], ACT.Square, accum_out=t.stat[:, 16 + b:17 + b])
    ins.then_inc(s["gm_vnorm"], 1)
    act.wait_ge(s["gm_vvar"], 1)
    f(t.stat[:, 18:20], t.stat[:, 18:20], ACT.Sqrt).then_inc(s["gm_vstd"], 1)
    for page in range(2):
        operand_high(f"gm{page}", t.page[7 + page], t.page_r[10 + page],
                     lambda q: act.wait_ge(s["gm_mixed"], 4 * page + q + 1))
    highs("gm_o", n=7)
    memory_attention(1, BLK["gm_o"] + 7)
    swiglu(4, "ffn4", BLK["xo1"] + 3)
    norm("fin2")
    act.wait_ge(s["norm_out"], KT * len(PLAIN))
    act.dma_start(a.out, t.h[:, :]).then_inc(s["out_done"], 16)
    act.wait_ge(s["out_done"], 16)


def vector_program(dve, t, s):
    ps = t.ps
    norms = norm_table(t, s)
    link = Link(dve, s["dve_chain"])
    ts, tt, stt = dve.tensor_scalar, dve.tensor_tensor, dve.scalar_tensor_tensor

    def low(b):
        b0 = block0(b) + AHEAD
        if isinstance(b, int) and b0 >= N_BLK:
            return
        b = b + AHEAD
        for hf in range(2):
            i = (2 * b0 + hf) % PIECE_SLOTS
            dve.wait_ge(s["high_done"], b * 2 + (hf + 1))
            tt(t.wl[i][:], t.raw[b0 % 2][:, hf * 1024:(hf + 1) * 1024], t.wh[i][:].bitcast(F32),
               ALU.subtract).then_inc(s["low_done"], 1)

    def lows(seg, first=0, n=4):
        for k in range(n):
            low(BLK[seg] + first + k)

    def low_groups(seg, first, groups):
        with dve.Fori(0, groups) as i:
            for k in range(4):
                low(At(i * 4 + (BLK[seg] + first + k), BLK[seg] + first + k))

    def operand_low(name, src, high, dst, width=512):
        for q in range(4):
            c = slice(q * width, (q + 1) * width)
            dve.wait_ge(s["op_high"], 4 * OPERAND[name] + q + 1)
            tt(dst[:, c], src[:, c], high[:, c].bitcast(F32), ALU.subtract).then_inc(s["op_low"], 1)

    def norm_parts(name, squares, halves=(0, 1)):
        for hf in halves:
            dve.wait_ge(s["norm_sq"], 2 * NORM[name] + hf + 1)
            dve.tensor_reduce(t.work[:, (2 + hf) * T:(3 + hf) * T],
                              squares[:, hf * 1024:(hf + 1) * 1024].rearrange("p (k t) -> p t k", k=4), AX,
                              ALU.add).then_inc(s["norm_part"], 1)

    def norm_scale(name):
        src, _, gain, dst = norms[name]
        dve.wait_ge(s["norm_std"], NORM[name] + 1)
        for k in range(KT):
            c = slice(k * T, (k + 1) * T)
            stt(dst[:, c], src[:, c], par(t, gain[0], gain[1] + k), t.rstd[:],
                ALU.mult, ALU.mult).then_inc(s["norm_out"], 1)
        if name in OPERAND:
            operand_low(name, dst, NORM_HIGH(t, name), NORM_LOW(t, name))

    def norm(name, prev=None):
        norm_parts(name, t.sq)
        if prev is not None:
            low(prev)
        norm_scale(name)

    def late_quarters(name, quarters):
        src, _, gain, _ = norms[name]
        for q in quarters:
            dve.wait_ge(s["op_high"], 4 * OPERAND[name] + q + 1)
            for k in (2 * q, 2 * q + 1):
                c = slice(k * T, (k + 1) * T)
                ins = stt(t.h_r[:, c], src[:, c], par(t, gain[0], gain[1] + k), t.sq_r[:, c].bitcast(F32),
                          ALU.mult, ALU.subtract)
            ins.then_inc(s["op_low"], 1)
            if q == 1:
                norm_parts(name, t.page[12], (0,))

    def late_norm(name, prev=None):
        late_quarters(name, range(4) if prev is None else (3,))
        if prev is not None:
            low(prev)
        norm_parts(name, t.page[12], (1,))

    def scaled(out, in_, n):
        return tt(out.rearrange("p (n t) -> p n t", n=n), in_,
                  t.rstd[:, :].unsqueeze(1).broadcast_to([P, n, T]), ALU.mult)

    def residual(seg, first=0, n=4, then=None):
        for k in range(first, first + n):
            n_ = SEG[seg] + k
            if k < 3 or not then:
                low(BLK[seg] + k)
            else:
                late_quarters(then, (0, 1))
            dve.wait_ge(s["piece_done"], 2 * (BLK[seg] + k) + 2)
            c = slice(k * 512, (k + 1) * 512)
            tt(t.x[:, c], ps[:, n_ % BANKS, :], t.x[:, c], ALU.add).then_inc(s["u_evac"], 1)
            if then and k == 3:
                late_quarters(then, (2,))

    def ffn_residual(f_, scale, then=None):
        for q in range(4):
            c = slice(q * 512, (q + 1) * 512)
            dve.wait_ge(s["acc_done"], 4 * f_ + q + 1)
            stt(t.x[:, c], ps[:, 4 + q, :], scale, t.x[:, c], ALU.mult, ALU.add).then_inc(s["x_up"], 1)
            if then and q:
                late_quarters(then, (q - 1,))

    def attention(g0, heads, scale, cols, dst, chores=()):
        def pre(g):
            st = (g % 2) * 8
            src = ps[:, 4 + g % 2, :].rearrange("p (b m) -> p b m", b=TB)
            dve.wait_ge(s["att_scores"], g + 1)
            link(dve.tensor_reduce(t.stat[:, st:st + 2], src, AX, ALU.max))
            ts(t.stat[:, st + 2:st + 4], t.stat[:, st:st + 2], -scale, None,
               ALU.mult).then_inc(s["att_max"], 1)

        def low_out(g):
            lo, hi, high_, low_ = dst(g - g0)
            dve.wait_ge(s["att_high"], g + 1)
            tt(low_, ps[lo:hi, 7, 0:cols], high_.bitcast(F32), ALU.subtract).then_inc(s["att_low"], 1)

        pre(g0)
        for g in range(g0, g0 + heads):
            if g + 1 < g0 + heads:
                pre(g + 1)
            st, buf = (g % 2) * 8, att_buf(t, g)
            dve.wait_ge(s["att_exp"], g + 1)
            link(dve.reciprocal(t.stat[:, st + 6:st + 8], t.stat[:, st + 4:st + 6]))
            for qb in range(TB):
                c = slice(qb * 256, (qb + 1) * 256)
                ins = ts(buf[:, c], buf[:, c], t.stat[:, st + 6 + qb:st + 7 + qb], None, ALU.mult)
            ins.then_inc(s["att_prob"], 1)
            if g > g0:
                low_out(g - 1)
            if g - g0 < len(chores):
                chores[g - g0]()
        low_out(g0 + heads - 1)

    norm_parts("mem", t.sq)
    for b in range(-AHEAD, 0):
        low(b)
    dve.wait_ge(s["consts_in"], 32)
    logits = par(t, "hg_lb_logits", 0, 16)
    tt(t.lb[:, 0:16], logits, logits, ALU.subtract).then_inc(s["lb_zero"], 1)
    norm_scale("mem")
    dve.wait_ge(s["lb_exp"], 1)
    link(dve.reciprocal(t.lb[:, 32:48], t.lb[:, 16:32]))
    link(tt(t.lb[:, 16:32], t.lb[:, 16:32], t.lb[:, 32:48], ALU.mult))
    link(tt(t.lb[:, 0:16], t.lb[:, 16:32], t.lb[:, 16:32], ALU.subtract))
    link(ts(t.lb[:, 0:16], t.lb[:, 0:16], 0.0, 1.0, ALU.max, ALU.min))
    link(ts(t.lb[:, 16:32], t.lb[:, 0:16], -1.0, 1.0, ALU.mult, ALU.add))
    norm_parts("mix0", t.sq)
    lows("mem_k", n=2)
    norm_scale("mix0")
    lows("mem_k", 2, 2)
    lows("w_in", n=8)
    low_groups("w_in", 8, 4)
    lows("w_in", 24, 4)

    reset = t.const[:, C_RESET:C_RESET + T]

    def forget(d):
        dve.wait_ge(s["hg_sig"], 2 * d + 1)
        fp = t.page[11 + d]
        for h in range(HG_H):
            c = slice(h * T, (h + 1) * T)
            ins = ts(fp[:, c], fp[:, c], t.lb[:, 16 + 8 * d + h:17 + 8 * d + h], t.lb[:, 8 * d + h:8 * d + h + 1],
                     ALU.mult, ALU.add)
        link(ins)
        ts(fp, fp, F_FLOOR, None, ALU.max).then_inc(s["hg_floor"], 1)

    def keys(d):
        dve.wait_ge(s["hg_sig"], 2 * d + 2)
        kp = t.page[2 + d]
        for h in range(HG_H):
            c = slice(h * T, (h + 1) * T)
            ins = ts(kp[:, c], kp[:, c], t.lb[:, 16 + 8 * d + h:17 + 8 * d + h], None, ALU.mult)
        link(ins)

    def running(d, half):
        dve.wait_ge(s["hg_log"], d + 1)
        for h in range(4 * half, 4 * half + 4):
            c = t.page[11 + d][:, h * T:(h + 1) * T]
            if d:
                c = c[:, ::-1]
            ins = dve.tensor_tensor_scan(c, reset, c, 0.0, ALU.mult, ALU.add)
        link(ins)

    lows("w_in", 28, 4)

    def na_dst(h):
        lo, c = NA_D * (h % 2), h // 2 * T
        return (lo, lo + NA_D, t.work_r[lo:lo + NA_D, c:c + T], t.work_r[lo:lo + NA_D, 1024 + c:1024 + c + T])

    def ca_dst(h):
        return 0, P, t.page_r[5][:, h * T:(h + 1) * T], t.page_r[5][:, 1024 + h * T:1024 + (h + 1) * T]

    attention(0, NA_H, NA_D ** -0.5, T, na_dst,
              (lambda: forget(0), lambda: keys(0), lambda: forget(1), lambda: keys(1),
               lambda: running(0, 0), lambda: running(0, 1), lambda: running(1, 0), lambda: running(1, 1)))
    attention(NA_H, CA_H, CA_D ** -0.5, T, ca_dst)

    def gated(m):
        seg, gate = (("na_o", 8), ("ca_o", 9))[m // 2]
        dve.wait_ge(s["att_gates"], m // 2 + 1)
        for k in (m % 2 * 2, m % 2 * 2 + 1):
            n = SEG[seg] + k
            c = slice(k * 512, (k + 1) * 512)
            dve.wait_ge(s["piece_done"], 2 * BLK[seg] + k + 1)
            dst = t.page[10] if seg == "na_o" else t.work
            tt(dst[:, c], ps[:, n % BANKS, :], t.page[gate][:, c], ALU.mult).then_inc(s["u_evac"], 1)
            dve.wait_ge(s["u_evac"], n + 1)
            if seg == "ca_o":
                link(tt(t.page[10][:, c], t.page[10][:, c], t.work[:, c], ALU.add))

    def expo(i):
        level, hh = HG_STEPS[i]
        if level == "same":
            return
        half = slice(hh * 1024, (hh + 1) * 1024)
        eg, eh = hg_buf(t, i)
        cf, cb = t.page[11][:, half], t.page[12][:, half]
        if i >= 2:
            dve.wait_ge(s["hg_sc"], i - 1)
        if level == 128:
            v = lambda ap: ap.rearrange("p (h c m) -> p h c m", h=4, c=NCH)
            cf, cb, eg, eh = v(cf), v(cb), v(eg), v(eh)
            tf = lambda c: cf[:, :, c, CH - 1:CH].broadcast_to([P, 4, CH])
            tb = lambda c: cb[:, :, c, 0:1].broadcast_to([P, 4, CH])
            tt(eg[:, :, 0], tf(0), cf[:, :, 0], ALU.subtract)
            tt(eg[:, :, 1], tf(1), cf[:, :, 1], ALU.subtract)
            tt(eg[:, :, 2], tb(2), cb[:, :, 2], ALU.subtract)
            link(tt(eg[:, :, 3], tb(3), cb[:, :, 3], ALU.subtract))
            tt(eg[:, :, 0], eg[:, :, 0], tf(1), ALU.add)
            tt(eg[:, :, 3], eg[:, :, 3], tb(2), ALU.add)
            tt(eh[:, :, 0], cb[:, :, 0], tb(1), ALU.add)
            dve.tensor_copy(eh[:, :, 1], cb[:, :, 1])
            dve.tensor_copy(eh[:, :, 2], cf[:, :, 2])
            tt(eh[:, :, 3], cf[:, :, 3], tf(2), ALU.add).then_inc(s["hg_expo"], 1)
            return
        v = lambda ap: ap.rearrange("p (g two m) -> p g two m", two=2, m=level)
        n = 1024 // (2 * level)
        cf, cb, eg, eh = v(cf), v(cb), v(eg), v(eh)
        lastf = cf[:, :, 0, level - 1:level].broadcast_to([P, n, level])
        firstb = cb[:, :, 1, 0:1].broadcast_to([P, n, level])
        tt(eg[:, :, 0], lastf, cf[:, :, 0], ALU.subtract)
        tt(eg[:, :, 1], firstb, cb[:, :, 1], ALU.subtract)
        if level == CH:
            dve.tensor_copy(eh[:, :, 0], cb[:, :, 0])
            dve.tensor_copy(eh[:, :, 1], cf[:, :, 1]).then_inc(s["hg_expo"], 1)
        else:
            tt(eh[:, :, 0], cb[:, :, 0], firstb, ALU.subtract)
            tt(eh[:, :, 1], cf[:, :, 1], lastf, ALU.subtract).then_inc(s["hg_expo"], 1)

    def decayed(i):
        level, hh = HG_STEPS[i]
        half = slice(hh * 1024, (hh + 1) * 1024)
        eg, eh = hg_buf(t, i)
        if level == "same":
            dve.wait_ge(s["hg_sc"], i - 1)
            tt(eg, t.page[2][:, half], t.page[3][:, half], ALU.add).then_inc(s["hg_gh"], 1)
            return
        dve.wait_ge(s["hg_exp"], i + 1)
        tt(eh, eh, t.page[0][:, half], ALU.mult).then_inc(s["hg_gh"], 1)

    def keep(i):
        level, hh = HG_STEPS[i]
        half = slice(hh * 1024, (hh + 1) * 1024)
        bank = 4 + 2 * (i % 2)
        dve.wait_ge(s["hg_sc"], i + 1)
        if level in (64, 128):
            dst = t.page[14 if level == 64 else 15][:, half]
            dve.tensor_copy(dst.rearrange("p (a c) -> p a c", a=2), ps[:, bank:bank + 2, :]).then_inc(s["hg_kept"], 1)
        else:
            mask = cst(t, "ident" if level == "same" else f"pair{level}").bitcast(I32)
            dve.copy_predicated(t.page[14][:, half].rearrange("p (n c) -> p n c", n=8),
                                mask.unsqueeze(1).broadcast_to([P, 8, P]),
                                ps[:, bank:bank + 2, :].rearrange("p a (n c) -> p (a n) c", c=P)).then_inc(s["hg_kept"], 1)

    dve.wait_ge(s["hg_silu"], 2)
    expo(0)
    for i in range(len(HG_STEPS)):
        if i + 1 < len(HG_STEPS):
            expo(i + 1)
        decayed(i)
        if i:
            keep(i - 1)
            dve.wait_ge(s["hg_kept"], i)
        if i < 8:
            lows("w_in", 32 + i, 1)
        elif i < 12:
            lows("na_o" if i < 10 else "ca_o", i % 2, 1)
        if 9 <= i < 13:
            gated(i - 9)
    keep(len(HG_STEPS) - 1)
    for q in range(4):
        c = slice(q * 512, (q + 1) * 512)
        dve.wait_ge(s["hg_std"], q + 1)
        link(tt(t.page[5][:, c], t.page[5][:, c], t.page[2][:, c], ALU.mult))
        stt(t.page[5][:, c], t.page[5][:, c], par(t, "hg_gnorm"), t.page[4][:, c],
            ALU.mult, ALU.mult).then_inc(s["hg_out"], 1)
    operand_low("hg", t.page[5], t.page_r[6], t.page_r[5])
    for k in range(4):
        n = SEG["hg_o"] + k
        c = slice(k * 512, (k + 1) * 512)
        low(BLK["hg_o"] + k)
        dve.wait_ge(s["piece_done"], 2 * (BLK["hg_o"] + k) + 2)
        tt(t.work[:, c], ps[:, n % BANKS, :], t.page[7][:, c], ALU.mult).then_inc(s["u_evac"], 1)
        dve.wait_ge(s["u_evac"], n + 1)
        tt(t.page[10][:, c], t.page[10][:, c], t.work[:, c], ALU.add).then_inc(s["merged"], 1)
    operand_low("merged", t.page[10], t.page_r[11], t.page_r[10])
    residual("w_out", then="ffn0")

    def hidden(fi, st, k, make):
        if not isinstance(st, int) or st >= 2:
            dve.wait_ge(s["piece_done"], st * 6 + (2 * BLK[f"ffn{fi}"] - 2))
        make(t.work[:, k * 512:(k + 1) * 512])
        dve.wait_ge(s["hidden_high"], st + (fi * FIT + 1))
        high_, low_ = hidden_parts(t, k)
        tt(low_, t.work[:, k * 512:(k + 1) * 512], high_.bitcast(F32), ALU.subtract).then_inc(s["hidden_ready"], 1)

    def ffn(fi, seg, early, step, links, prev=None, end=lambda st, k: None):
        b = BLK[seg]
        late_norm(seg, prev)
        low(b)
        dve.wait_ge(s["norm_std"], NORM[seg] + 1)
        early(0, 0)
        low(b + 1)
        step(0, 0, 0)
        end(0, 0)

        def two_steps(i):
            for k in range(2):
                r = b + 2 + 3 * k
                blk = [i * 6 + (r + j) if isinstance(i, int) else At(i * 6 + (r + j), r + j) for j in range(3)]
                low(blk[0])
                early(i * 2 + (1 + k), (1 + k) % 2)
                low(blk[1])
                step(i * 2 + (1 + k), i * 4 + (2 + 2 * k), (1 + k) % 2)
                low(blk[2])
                end(i * 2 + (1 + k), (1 + k) % 2)

        trips = (FIT - 1) // 2
        two_steps(0)
        last = trips - 1 if fi == N_FFN - 1 else trips
        with dve.Fori(0, last - 1) as i:
            link.loop(i, 2 * links)
            two_steps(i + 1)
        link.end(last - 1)
        if last < trips:
            two_steps(last)

    def conv_scale(st, k, half):
        dve.wait_ge(s["piece_done"], 2 * BLK["ffn0"] + 2 + 2 * half if isinstance(st, int) and st == 0
                    else st * 6 + (2 * BLK["ffn0"] + 2 * half))
        scaled(t.page[13][:, k * 1024 + half * 512:k * 1024 + (half + 1) * 512],
               ps[:, (SEG["ffn0"] + 2 * k + half) % BANKS, :].rearrange("p (n t) -> p n t", n=2),
               2).then_inc(s["u_evac"], 1)

    def conv_taps(st, tile, k, half):
        dve.wait_ge(s["conv_mid"], st * 2 + (half + 1))
        for tap in (0, 2):
            for j in (2 * half, 2 * half + 1):
                col = tile + (j % 2 + FF // P * (j // 2)) + (PCOL["conv_w"] + 44 * tap)
                w = t.param[:, col:col + 1] if isinstance(col, int) else t.param[:, bass.ds(col, 1)]
                u = t.page[13][:, k * 1024 + j * T:k * 1024 + (j + 1) * T]
                c = t.page[k][:, j * T:(j + 1) * T]
                o, i_ = (c[:, 1:T], u[:, 0:T - 1]) if tap == 0 else (c[:, 0:T - 1], u[:, 1:T])
                ins = stt(o, i_, w, o, ALU.mult, ALU.add)
            link(ins)

    def conv_step(st, tile, k):
        conv_scale(st, k, 1)
        conv_taps(st, tile, k, 0)
        dve.sem_inc(s["conv_done"], 1)
        conv_taps(st, tile, k, 1)

    def conv_hidden(st, k):
        dve.wait_ge(s["gelu_ready"], st + 1)
        hidden(0, st, k, lambda out: tt(out, t.page[k][:, 0:512], t.page[k][:, 512:1024],
                                        ALU.mult).then_inc(s["hidden_made"], 1))

    ffn(0, "ffn0", lambda st, k: conv_scale(st, k, 0), conv_step, 4, BLK["w_out"] + 3, conv_hidden)
    ffn_residual(0, 1.0)
    norm("fin0", last_down(0))

    def swiglu(fi, seg, prev=None, then=None):
        n0, b = SEG[seg], BLK[seg]

        def gate_scale(st, k):
            dve.wait_ge(s["piece_done"], 2 * b + 2 if isinstance(st, int) and st == 0
                        else st * 6 + 2 * b)
            scaled(t.work[:, 1024 + k * 512:1536 + k * 512],
                   ps[:, (n0 + 2 * k) % BANKS, :].rearrange("p (n t) -> p n t", n=2), 2).then_inc(s["gate_scaled"], 1)

        def step(st, tile, k):
            gate = t.work[:, 1024 + k * 512:1536 + k * 512]
            dve.wait_ge(s["gate_ready"], st + ((fi - 1) * FIT + 1))
            link(scaled(gate, gate.rearrange("p (n t) -> p n t", n=2), 2))

            def make(out):
                dve.wait_ge(s["piece_done"], 2 * b + 4 if isinstance(st, int) and st == 0 else st * 6 + (2 * b + 2))
                tt(out, ps[:, (n0 + 2 * k + 1) % BANKS, :], gate, ALU.mult).then_inc(s["hidden_made"], 1)
                dve.wait_ge(s["hidden_made"], st + (fi * FIT + 1))
                dve.sem_inc(s["u_evac"], 2)

            hidden(fi, st, k, make)

        ffn(fi, seg, gate_scale, step, 1, prev)
        ffn_residual(fi, 0.5, then)

    swiglu(1, "ffn1")

    norm("mix1", last_down(1))
    dve.wait_ge(s["norm_out"], KT * (PLAIN["mix1"] + 1))
    h3, d3 = tiles(t.h[:, :]), tiles(t.page[0])
    tt(d3[:, :, 1:T], h3[:, :, 0:T - 1], h3[:, :, 1:T], ALU.subtract)
    link(ts(d3[:, :, 0:1], h3[:, :, 0:1], -1.0, None, ALU.mult))
    link(dve.memset(t.work[64:P, 0:T], 0.0))
    dve.memset(t.work[0:64, T:2 * T], 0.0).then_inc(s["inner_zero"], 1)
    for step in RW_ORDER:
        if not isinstance(step, int):
            low(BLK["rw_r"] + int(step[1:]))
            continue
        mu = (0, 2, 3, 1, 4, 5)[step]
        for k in range(KT):
            c = slice(k * T, (k + 1) * T)
            ins = stt(t.page[1 + step][:, c], t.page[0][:, c], par(t, "rwkv_mu_2", 8 * mu + k), t.h[:, c],
                      ALU.mult, ALU.add)
            if k % 2:
                ins.then_inc(s["rw_mix"], 1)
        operand_low(f"rw{step}", t.page[1 + step], t.page_r[10 + step], t.page_r[1 + step])
    low(BLK["lora"])
    operand_low("lora", t.work[:, 0:1024], t.sq_r[:, 0:1024], t.work_r[:, 0:1024], 256)
    dve.wait_ge(s["u_evac"], SEG["rw_o"])
    for k in range(KT):
        c = slice(k * T, (k + 1) * T)
        ins = ts(t.page[1][:, c], t.page[8][:, c], par(t, "rwkv_k_k_2", k), None, ALU.mult)
        if k % 2:
            ins.then_inc(s["rw_kk"], 1)
    dve.wait_ge(s["lora_out"], 1)
    for k in range(KT):
        c = slice(k * T, (k + 1) * T)
        ins = dve.tensor_tensor_scan(t.page[2][:, c], reset, t.page[11][:, c], 0.0, ALU.mult, ALU.add)
    link(ins)
    tt(t.page[3], t.page[2], t.page[11], ALU.subtract).then_inc(s["rw_cum"], 1)
    for q in range(4):
        dve.wait_ge(s["rw_kksum"], q + 1)
        ts(t.h[:, q * 512:(q + 1) * 512], ps[:, q, :], 1e-24, None, ALU.max).then_inc(s["rw_kkfloor"], 1)
    dve.wait_ge(s["lora_out"], 2)
    for k in range(KT):
        c = slice(k * T, (k + 1) * T)
        ins = ts(t.page[14][:, c], t.page[12][:, c], 1.0, par(t, "rwkv_k_a_2", k), ALU.subtract, ALU.mult)
    link(ins)
    for k in range(KT):
        c = slice(k * T, (k + 1) * T)
        ins = stt(t.page[8][:, c], t.page[14][:, c], 1.0, t.page[8][:, c], ALU.add, ALU.mult)
    link(ins)
    for q in range(4):
        c = slice(q * 512, (q + 1) * 512)
        dve.wait_ge(s["rw_kkvar"], q + 1)
        ins = tt(t.page[1][:, c], t.page[1][:, c], t.h[:, c], ALU.mult)
    link(ins)
    link(tt(t.page[5], t.page[1], t.page[12], ALU.mult))
    dve.wait_ge(s["lora_out"], 3)
    for k in range(KT):
        c = slice(k * T, (k + 1) * T)
        ins = stt(t.work[:, c], t.page[7][:, c], par(t, "rwkv_r_k_2", k), t.page[8][:, c], ALU.mult, ALU.mult)
    ins.then_inc(s["rw_bonus_in"], 1)
    dve.wait_ge(s["rw_bonus_in"], 1)
    dve.wait_ge(s["rw_exp"], 3)
    tt(t.page[3], t.page[3], t.page[1], ALU.mult)
    tt(t.page[5], t.page[5], t.page[4], ALU.mult)
    tt(t.page[6], t.page[8], t.page[4], ALU.mult)
    dve.tensor_copy(t.pc[:, :].rearrange("p (a b) -> p a b", b=1),
                    t.page[10].rearrange("p (a b) -> p a b", b=CH)[:, :, CH - 1:CH])
    tt(t.page[7], t.page[7], t.page[10], ALU.mult).then_inc(s["rw_dec"], 1)
    for q in range(4):
        c = slice(q * 512, (q + 1) * 512)
        dve.wait_ge(s["rw_bonus_sum"], q + 1)
        ins = tt(t.page[0][:, c], ps[:, q, :], t.page[9][:, c], ALU.mult)
    ins.then_inc(s["rw_act"], 1)
    low(BLK["lora"] + 1)
    low(BLK["lora"] + 2)

    def matrices(q, j):
        bank = 2 * (q % 2)
        return ps[:, bank:bank + 2, j * 256:(j + 1) * 256].rearrange("p e (b c) -> p e b c", b=2)

    def view(ap):
        return ap.rearrange("p (e b c) -> p e b c", e=2, b=2)

    def mask(name):
        return cst(t, name).unsqueeze(1).unsqueeze(1).broadcast_to([P, 2, 2, P])

    def chunk_matrices(c):
        buf, xt = inv_buf(t, c), inv_xt(t, c)
        q = 3 * c
        dve.wait_ge(s["rw_m"], q + 1)
        link(tt(view(buf.lt), matrices(q, 0), mask("strict"), ALU.mult))
        link(tt(view(buf.x), matrices(q, 1), mask("lower1"), ALU.mult))
        tt(view(buf.x), mask("ident"), view(buf.x), ALU.subtract)
        link(tt(view(xt), view(buf.lt), mask("upper1"), ALU.mult))
        tt(view(xt), mask("ident"), view(xt), ALU.subtract).then_inc(s["rw_m_sb"], 1)
        dve.wait_ge(s["rw_m"], q + 2)
        tt(view(stack(RW_MT(t), c)), matrices(q + 1, 0), mask("strict"), ALU.mult)
        tt(view(stack(RW_RBT(t), c)), matrices(q + 1, 1), mask("incl"), ALU.mult).then_inc(s["rw_m_sb"], 1)
        dve.wait_ge(s["rw_m"], q + 3)
        tt(view(stack(RW_RKT(t), c)), matrices(q + 2, 0), mask("incl"), ALU.mult).then_inc(s["rw_m_sb"], 1)

    dve.wait_ge(s["rw_t_sb"], 12)
    for c0 in range(0, KT, 2):
        chunk_matrices(c0)
        chunk_matrices(c0 + 1)
        for lv in range(len(LEVELS) - 1):
            for c in (c0, c0 + 1):
                buf, xt = inv_buf(t, c), inv_xt(t, c)
                dve.wait_ge(s["rw_z"], inv_at(c, lv) + 1)
                if lv < len(LEVELS) - 2:
                    tt(buf.x, buf.x, ps[:, 4 + 2 * (c % 2), :], ALU.subtract)
                tt(xt, xt, ps[:, 5 + 2 * (c % 2), :], ALU.subtract).then_inc(s["rw_z_sb"], 1)

    dve.memset(t.page[5][:, 0:1024], 0.0)
    dve.memset(t.page[6][:, 0:1024], 0.0).then_inc(s["rw_zero"], 1)
    state, delta = t.page[6][:, 0:1024], t.page[6][:, 1024:2048]
    for n_ in range(NCH):
        po = slice(CH * (n_ % 2), CH * (n_ % 2 + 1))
        dve.wait_ge(s["rw_rhs"], n_ + 1)
        ts(t.page[5][po, 0:512], ps[po, 0, :], -1.0, None, ALU.mult).then_inc(s["rw_rhs_sb"], 1)
        dve.wait_ge(s["rw_u"], n_ + 1)
        dve.tensor_copy(t.page[5][po, 1024:1536], ps[po, 2, :]).then_inc(s["rw_u_sb"], 1)
        if n_ == NCH - 1:
            break
        dve.wait_ge(s["rw_ds"], n_ + 1)
        blocks = lambda ap: ap.rearrange("p (c i) -> p c i", i=P)
        link(tt(blocks(delta), ps[:, 0:2, :].rearrange("p a (c i) -> p (a c) i", i=P),
                cst(t, "head_ones").unsqueeze(1).broadcast_to([P, KT, P]), ALU.mult))
        link(tt(state, state, delta, ALU.add))
        pc = t.pc[:, :].rearrange("p (c n) -> p c n", n=NCH)[:, :, n_:n_ + 1].broadcast_to([P, KT, P])
        tt(blocks(state), blocks(state), pc, ALU.mult).then_inc(s["rw_s"], 1)
    for q in range(4):
        c = slice(q * 512, (q + 1) * 512)
        dve.wait_ge(s["rw_mean"], q + 1)
        stt(t.page[8][:, c], ps[:, q, :], -1.0 / RW_D, t.page[8][:, c], ALU.mult, ALU.add).then_inc(s["rw_cent"], 1)
    for q in range(4):
        c = slice(q * 512, (q + 1) * 512)
        dve.wait_ge(s["rw_std"], q + 1)
        link(tt(t.page[8][:, c], t.page[8][:, c], t.page[2][:, c], ALU.mult))
        for k in (2 * q, 2 * q + 1):
            ck = slice(k * T, (k + 1) * T)
            ins = ts(t.page[8][:, ck], t.page[8][:, ck], par(t, "rwkv_ln_w_2", k), par(t, "rwkv_ln_b_2", k),
                     ALU.mult, ALU.add)
        link(ins)
        link(tt(t.page[8][:, c], t.page[8][:, c], t.page[0][:, c], ALU.add))
        tt(t.page[7][:, c], t.page[8][:, c], t.page[13][:, c], ALU.mult).then_inc(s["rw_out"], 1)
    operand_low("rw_o", t.page[7], t.page_r[10], t.page_r[7])
    norm_parts("mem2", t.sq)
    residual("rw_o", 0, 2)
    norm_scale("mem2")
    residual("rw_o", 2, 2)
    lows("mem2_k")
    lows("mem2_v")

    def memory_attention(i, then, prev=None):
        late_norm(f"x{i}", prev)
        lows(f"xq{i}", n=1)
        dve.wait_ge(s["norm_std"], NORM[f"x{i}"] + 1)
        for k in range(4):
            if k:
                low(BLK[f"xq{i}"] + k)
            dve.wait_ge(s["piece_done"], 2 * (BLK[f"xq{i}"] + k) + 2)
            scaled(t.page[0][:, k * 512:(k + 1) * 512],
                   ps[:, (SEG[f"xq{i}"] + k) % BANKS, :].rearrange("p (n t) -> p n t", n=2),
                   2).then_inc(s["u_evac"], 1)
        attention(NA_H + CA_H + XA_H * i, XA_H, XA_D ** -0.5, 512,
                  lambda h: (0, P, t.page_r[2][:, h * 512:(h + 1) * 512], t.page_r[1][:, h * 512:(h + 1) * 512]))
        residual(f"xo{i}", then=then)

    memory_attention(0, "ffn2")
    swiglu(2, "ffn2", BLK["xo0"] + 3, "ffn3")
    swiglu(3, "ffn3", last_down(2))

    norm("mix2", last_down(3))
    dve.wait_ge(s["rows_in"], 48)
    cols = lambda ap: ap.rearrange("p (g c) -> p g c", g=GM_G)
    tt(cols(t.page[4]), cols(t.page[9]), cst(t, "causal").unsqueeze(1).broadcast_to([P, GM_G, P]),
       ALU.mult).then_inc(s["gm_mask"], 1)
    low_groups("gm_u", 0, 2)
    low_groups("gm_v", 0, 2)
    dve.wait_ge(s["gm_vnorm"], 1)
    link(ts(t.stat[:, 18:20], t.stat[:, 16:18], 1.0 / GM_W, EPS, ALU.mult, ALU.add))
    dve.reciprocal(t.stat[:, 18:20], t.stat[:, 18:20]).then_inc(s["gm_vvar"], 1)
    dve.wait_ge(s["gm_vstd"], 1)
    for b in range(TB):
        ins = stt(t.page[2 + b], t.page[2 + b], t.stat[:, 18 + b:19 + b], t.page[6], ALU.mult, ALU.mult)
    ins.then_inc(s["gm_vout"], 1)
    for q in range(8):
        dve.wait_ge(s["gm_mix"], q + 1)
        tmp = t.work[:, (q % 2) * 512:(q % 2 + 1) * 512]
        bias = t.page[5][:, q * 256:(q + 1) * 256].rearrange("p (g c) -> p g c", g=2)
        ins = tt(tmp.rearrange("p (g b c) -> p g b c", g=2, b=2),
                 ps[:, 4 + q % 2, :].rearrange("p (g b c) -> p g b c", g=2, b=2),
                 bias.unsqueeze(2).broadcast_to([P, 2, 2, P]), ALU.add)
        link(ins)
        tt(t.pages[:, 7 * FP + q * 512:7 * FP + (q + 1) * 512], tmp, t.pages[:, q * 512:(q + 1) * 512],
           ALU.mult).then_inc(s["gm_mixed"], 1)
    for page in range(2):
        operand_low(f"gm{page}", t.page[7 + page], t.page_r[10 + page], t.page_r[7 + page])
    for q in range(4):
        c = slice(q * 512, (q + 1) * 512)
        lows("gm_o", 2 * q, 2 if q < 3 else 1)
        dve.wait_ge(s["piece_done"], 2 * (BLK["gm_o"] + 2 * q) + 4)
        tt(t.x[:, c], ps[:, (SEG["gm_o"] + q) % BANKS, :], t.x[:, c], ALU.add).then_inc(s["u_evac"], 1)
    late_quarters("x1", (0, 1, 2))
    memory_attention(1, "ffn4", BLK["gm_o"] + 7)
    swiglu(4, "ffn4", BLK["xo1"] + 3)
    norm("fin2")


def pool_program(pool, t, s):
    for col, value in ((COL_EPS, EPS), (COL_GN_EPS, GN_EPS)):
        pool.memset(t.stat[:, col:col + 1], value)
    pool.memset(t.zrow[:], 0.0).then_inc(s["zero_row"], 1)
    pool.wait_ge(s["consts_in"], 32)
    pool.wait_ge(s["bias_in"], 16 * 4 * NA_H)
    for page in (14, 15):
        table = t.page[page].rearrange("p (n c) -> p n c", c=NA_COLS)
        window = t.const[:, C_WINDOW:C_WINDOW + NA_COLS].unsqueeze(1).broadcast_to([P, 32, NA_COLS])
        pool.tensor_tensor(table, table, window, ALU.add).then_inc(s["pool_chain"], 1)
        pool.wait_ge(s["pool_chain"], page - 13)
        pool.tensor_scalar(t.page[page], t.page[page], NA_D ** 0.5, None, ALU.mult).then_inc(s["bias_ready"], 1)
    for i, (level, hh) in enumerate(HG_STEPS):
        if level == "same":
            continue
        half = slice(hh * 1024, (hh + 1) * 1024)
        v = lambda ap: ap.rearrange("p (g two m) -> p g two m", two=2, m=level)
        eg = v(hg_buf(t, i)[0])
        pool.wait_ge(s["hg_exp"], i + 1)
        pool.tensor_tensor(eg[:, :, 0], eg[:, :, 0], v(t.page[2][:, half])[:, :, 0], ALU.mult)
        pool.tensor_tensor(eg[:, :, 1], eg[:, :, 1], v(t.page[3][:, half])[:, :, 1], ALU.mult).then_inc(s["hg_keys"], 1)
    for c0 in range(0, KT, 2):
        for lv in range(len(LEVELS) - 1):
            for c in (c0, c0 + 1):
                q, buf = inv_at(c, lv), inv_buf(t, c)
                if lv == 0:
                    pool.wait_ge(s["rw_m_sb"], 3 * c + 1)
                else:
                    pool.wait_ge(s["rw_y"], q - 1)
                m = LEVELS[len(LEVELS) - 2 - lv]
                v = lambda ap: ap.rearrange("p (n c) -> p n c", c=P)
                pool.tensor_tensor(v(buf.lm), v(buf.lt), cst(t, f"upper{m}").unsqueeze(1).broadcast_to([P, 4, P]),
                                   ALU.mult).then_inc(s["rw_lm"], 1)


def constants():
    i = np.arange(P)
    r, c = i[:, None], i[None, :]
    out = np.zeros((P, N_CONST), np.float32)

    def put(name, mask):
        out[:, CCOL[name]:CCOL[name] + P] = mask

    put("ident", r == c)
    put("flip", r + c == P - 1)
    put("ones", np.ones((P, P)))
    put("head_ones", r // RW_D == c // RW_D)
    for m in LEVELS:
        pair = (r // (2 * m) == c // (2 * m)) & (r // m != c // m)
        put(f"pair{m}", pair)
        put(f"upper{m}", pair & (r < c))
    put("lower1", (r // 2 == c // 2) & (r > c))
    put("strict", (r // CH == c // CH) & (r < c))
    put("incl", (r // CH == c // CH) & (r <= c))
    put("causal", r <= c)
    out[:, C_RESET:C_RESET + T] = (np.arange(T) % CH != 0)[None, :]
    q, k = (P - 1 - np.arange(P))[:, None] % NA_COLS, np.arange(NA_COLS)[None, :]
    start = np.clip(q - NA_WIN // 2, 0, NA_COLS - NA_WIN)
    out[:, C_WINDOW:] = np.where((k >= start) & (k < start + NA_WIN), 0.0, NEG)
    return out


def feature_major(x):
    n, d = x.shape
    return np.ascontiguousarray(x.T.reshape(d // P, P, n).transpose(1, 0, 2).reshape(P, -1))


def k_blocks(w, cols=256):
    k, n = w.shape
    b = w.reshape(k // P, P, n // cols, cols).transpose(2, 1, 0, 3).reshape(n // cols, P, -1)
    return [np.pad(x, ((0, 0), (0, 2048 - x.shape[1]))) for x in b]


def half_blocks(w):
    b = w.reshape(4, P, -1, 2, 256).transpose(2, 1, 3, 0, 4)
    return list(b.reshape(b.shape[0], P, 2048))


def ffn_blocks(up, down):
    a, b = k_blocks(up[:, :FF]), k_blocks(up[:, FF:])
    c = list(down.reshape(FIT, 2, P, D).transpose(0, 2, 1, 3).reshape(FIT, P, 2 * D))
    blocks = [a[0], b[0]]
    for k in range(1, FIT):
        blocks += [a[k], b[k], c[k - 1]]
    return blocks + [c[-1]]


def weight_stream(i):
    rkv = i["rwkv_w_rkv_2"][0]
    w1, a1, g1 = i["rwkv_w1_2"][0], i["rwkv_a1_2"][0], i["rwkv_g1_2"][0]
    w2, a2, g2 = i["rwkv_w2_2"][0], i["rwkv_a2_2"][0], i["rwkv_g2_2"][0]
    lora_a = k_blocks(np.concatenate([w1, a1, g1[:, :P]], 1))
    g1p = np.pad(g1[:, P:], ((0, 0), (0, 2 * P - g1.shape[1])))
    lora_b = [np.concatenate([g1p.reshape(KT, P, P).transpose(1, 0, 2).reshape(P, D), np.concatenate([w2, a2], 0)], 1)]
    g2p = np.pad(g2, ((0, 2 * P - g2.shape[0]), (0, 0)))
    lora_c = [np.concatenate([g2p[:P], g2p[P:]], 1)]
    gm_o = k_blocks(i["gmlp_w_o_2"][0][:D]), k_blocks(i["gmlp_w_o_2"][0][D:])
    kv, kv2, uv = i["w_mem_kv"][0], i["mem_w_kv_2"], i["gmlp_w_uv_2"][0]
    up1, down1, up2, down2 = (i[n] for n in ("ffn1_w_in_2", "ffn1_w_out_2", "ffn2_w_in_2", "ffn2_w_out_2"))
    parts = {
        "mem_k": k_blocks(kv[:, :512]), "mem_v": k_blocks(kv[:, 512:]), "w_in": k_blocks(i["w_in"][0]),
        "na_o": half_blocks(i["w_na_o"][0]), "ca_o": half_blocks(i["w_ca_o"][0]), "hg_o": k_blocks(i["w_hg_o"][0]),
        "w_out": k_blocks(i["w_out"][0]), "ffn0": ffn_blocks(i["w_up"][0], i["w_down"][0]),
        "ffn1": ffn_blocks(up1[0], down1[0]), "ffn2": ffn_blocks(up2[0], down2[0]),
        "ffn3": ffn_blocks(up1[1], down1[1]), "ffn4": ffn_blocks(up2[1], down2[1]),
        "rw_r": k_blocks(rkv[:, :D]), "rw_k": k_blocks(rkv[:, D:2 * D]), "rw_v": k_blocks(rkv[:, 2 * D:]),
        "lora": lora_a + lora_b + lora_c, "rw_o": k_blocks(i["rwkv_w_o_2"][0]),
        "mem2_k": k_blocks(kv2[:, :D]), "mem2_v": k_blocks(kv2[:, D:]),
        "xq0": k_blocks(i["xattn_wq_2"][0]), "xo0": k_blocks(i["xattn_wo_2"][0]),
        "xq1": k_blocks(i["xattn_wq_2"][1]), "xo1": k_blocks(i["xattn_wo_2"][1]),
        "gm_u": k_blocks(uv[:, :GM_W]), "gm_v": k_blocks(uv[:, GM_W:]),
        "gm_o": [x for pair in zip(*gm_o) for x in pair],
    }
    blocks = []
    for name, _, n in SEGMENTS:
        assert len(parts[name]) == n, name
        blocks += parts[name]
    return np.stack(blocks)


def param_table(i):
    cols = [i[name].reshape(-1, P).T for name, _ in PARAMS]
    assert [c.shape[1] for c in cols] == [n for _, n in PARAMS]
    return np.concatenate(cols, 1)


def kernel(**inputs):
    import concourse.bacc as bacc
    from concourse.bass_utils import run_bass_kernel_spmd

    i = {k: np.asarray(v) for k, v in inputs.items()}
    arrays = {
        "in_stream": weight_stream(i), "in_params": param_table(i),
        "in_consts": constants(), "in_x": feature_major(i["x"][0]), "in_mem": feature_major(i["mem"][0]),
        "in_mem2": feature_major(i["mem_2"][0]), "in_rpb": i["na_rpb"][0], "in_gmlp_b": i["gmlp_b_s_2"][0],
        "in_gmlp_gain": i["gmlp_v_norm_2"], "in_gmlp_w": i["gmlp_w_s_2"][0].transpose(2, 0, 1).reshape(P, -1),
    }
    arrays = {k: np.ascontiguousarray(v) for k, v in arrays.items()}
    nc = bacc.Bacc("TRN2", target_bir_lowering=False, num_devices=1, dynamic_dma_scratch_size=1024)
    ap = {k: nc.dram_tensor(k, v.shape, F32, kind="ExternalInput").ap() for k, v in arrays.items()}
    out = nc.dram_tensor("out", (P, FP), F32, kind="ExternalOutput").ap()
    rpb = ap["in_rpb"]
    n_dr, n_dc = rpb.shape[1:]
    kh = T // NA_COLS

    def bias_window(h, row):
        at = h * n_dr * n_dc + (n_dr // 2 - row) * n_dc + n_dc // 2 - (NA_COLS - 1)
        return bass.AP(tensor=rpb.tensor, offset=at, ap=[[1, NA_COLS], [n_dc, kh], [1, NA_COLS]])

    a = Bag()
    a.stream, a.params, a.consts, a.mix_weights = (ap[f"in_{n}"] for n in ("stream", "params", "consts", "gmlp_w"))
    a.x_t, a.mem_t, a.mem2_t, a.bias_window, a.out = ap["in_x"], ap["in_mem"], ap["in_mem2"], bias_window, out
    a.bias_rows = ap["in_gmlp_b"].rearrange("(o g) c -> o (g c)", o=1).broadcast_to([P, GM_W])
    a.gain_rows = ap["in_gmlp_gain"].broadcast_to([P, GM_W])
    build(nc, a)
    got = run_bass_kernel_spmd(nc, [arrays], core_ids=[0]).results[0]["out"]
    return got.reshape(P, KT, T).transpose(2, 1, 0).reshape(1, T, D)
```
